# Optimizing a Trainium2 kernel written in Bass

```python
import jax, jax.numpy as jnp
from jax import lax
import numpy as np

D_MODEL = 1024
BATCH = 1
SEQ = 256
DEPTH = 2
DEC_BATCH = 1
DEC_SEQ = 32
PAST_LEN = 512

CHUNK = 64
MIX_WIDTH = D_MODEL
C_CONV = MIX_WIDTH // 2
CONV_WIDTH = 31
N_HEADS = 8
HEAD_DIM = (MIX_WIDTH - C_CONV) // N_HEADS
ATT_WIDTH = N_HEADS * HEAD_DIM
N_IDX_HEADS = 8
IDX_DIM = 64
MAX_TOPK = 256
Q_BLOCK = 128
D_FF = 2816
ROPE_THETA = 10000.0
EPS = 1e-6
ATT_SCALE = HEAD_DIM ** -0.5
IDX_SCALE = IDX_DIM ** -0.5
IDX_HEAD_SCALE = N_IDX_HEADS ** -0.5
IN_COLS = 2 * C_CONV + 3 * ATT_WIDTH + N_IDX_HEADS * IDX_DIM + IDX_DIM + N_IDX_HEADS

kernel_name = 'hymba_conformer_dsa_stream_step'

def rms_norm(x, g):
    xf = x.astype(jnp.float32)
    y = xf * lax.rsqrt(jnp.mean(xf * xf, axis=-1, keepdims=True) + EPS)
    return (y * g.astype(jnp.float32)).astype(x.dtype)

def layer_norm(x, g, b):
    xf = x.astype(jnp.float32)
    mu = jnp.mean(xf, axis=-1, keepdims=True)
    var = jnp.mean(jnp.square(xf - mu), axis=-1, keepdims=True)
    y = (xf - mu) * lax.rsqrt(var + EPS) * g.astype(jnp.float32) + b.astype(jnp.float32)
    return y.astype(x.dtype)

def rope_tables(pos, dim):
    inv = 1.0 / (ROPE_THETA ** (jnp.arange(0, dim, 2, dtype=jnp.float32) / dim))
    ang = pos.astype(jnp.float32)[:, None] * inv[None, :]
    return jnp.cos(ang), jnp.sin(ang)

def apply_rope(x, cos, sin):
    half = x.shape[-1] // 2
    shp = (cos.shape[0],) + (1,) * (x.ndim - 3) + (half,)
    c, s = cos.reshape(shp), sin.reshape(shp)
    x1 = x[..., :half].astype(jnp.float32)
    x2 = x[..., half:].astype(jnp.float32)
    return jnp.concatenate([x1 * c - x2 * s, x2 * c + x1 * s], axis=-1).astype(x.dtype)

def half_step_ffn(x, g_pre, g_post, w_up, w_down):
    h = rms_norm(x, g_pre) @ w_up
    gate, up = h[..., :D_FF], h[..., D_FF:]
    y = (jax.nn.silu(gate) * up) @ w_down
    return x + 0.5 * rms_norm(y, g_post)

def split_cols(proj):
    sizes = (C_CONV, C_CONV, ATT_WIDTH, ATT_WIDTH, ATT_WIDTH,
             N_IDX_HEADS * IDX_DIM, IDX_DIM, N_IDX_HEADS)
    out, start = [], 0
    for s in sizes:
        out.append(proj[..., start:start + s])
        start += s
    return out

def conformer_conv(a, g, hist, conv_w, conv_b, ln_g, ln_b):
    u = a * jax.nn.sigmoid(g)
    ext = jnp.concatenate([hist.astype(u.dtype), u], axis=1)
    y = lax.conv_general_dilated(
        ext, conv_w[:, None, :].astype(u.dtype), window_strides=(1,), padding='VALID',
        dimension_numbers=('NWC', 'WIO', 'NWC'), feature_group_count=C_CONV) + conv_b
    y = jax.nn.silu(layer_norm(y, ln_g, ln_b))
    return y, ext[:, ext.shape[1] - (CONV_WIDTH - 1):]

def dsa_block(q, qi, wi, q_pos, k, v, ki, k_pos, topk):
    logits = jnp.einsum('thd,sd->ths', qi, ki).astype(jnp.float32) * IDX_SCALE
    score = jnp.einsum('th,ths->ts', wi.astype(jnp.float32) * IDX_HEAD_SCALE, jax.nn.relu(logits))
    q_chunk = q_pos // CHUNK
    k_chunk = k_pos // CHUNK
    admissible = k_chunk[None, :] <= q_chunk[:, None]
    score = jnp.where(admissible, score, -jnp.inf)
    _, idx = lax.top_k(score, topk)
    valid = k_chunk[idx] <= q_chunk[:, None]
    k_sel = k[idx]
    v_sel = v[idx]
    att = jnp.einsum('thd,tkhd->thk', q, k_sel).astype(jnp.float32) * ATT_SCALE
    att = jnp.where(valid[:, None, :], att, -jnp.inf)
    p = jax.nn.softmax(att, axis=-1).astype(v.dtype)
    return jnp.einsum('thk,tkhd->thd', p, v_sel)

def sparse_attention(q, qi, wi, q_pos, k, v, ki):
    T = q.shape[1]
    S = k.shape[1]
    topk = min(MAX_TOPK, S // 4)
    qb = min(Q_BLOCK, T)
    nb = T // qb
    k_pos = jnp.arange(S)

    def per_seq(args):
        q_s, qi_s, wi_s, k_s, v_s, ki_s = args

        def per_block(blk):
            qb_, qib_, wib_, pb_ = blk
            return dsa_block(qb_, qib_, wib_, pb_, k_s, v_s, ki_s, k_pos, topk)

        blocks = (q_s.reshape(nb, qb, N_HEADS, HEAD_DIM),
                  qi_s.reshape(nb, qb, N_IDX_HEADS, IDX_DIM),
                  wi_s.reshape(nb, qb, N_IDX_HEADS),
                  q_pos.reshape(nb, qb))
        return lax.map(per_block, blocks).reshape(T, N_HEADS, HEAD_DIM)

    return lax.map(per_seq, (q, qi, wi, k, v, ki))

def hybrid_mixer(h, pos, past, w_in, conv_w, conv_b, ln_g, ln_b, w_out):
    B, T, _ = h.shape
    a, g, q, k, v, qi, ki, wi = split_cols(h @ w_in)
    q = q.reshape(B, T, N_HEADS, HEAD_DIM)
    k = k.reshape(B, T, N_HEADS, HEAD_DIM)
    v = v.reshape(B, T, N_HEADS, HEAD_DIM)
    qi = qi.reshape(B, T, N_IDX_HEADS, IDX_DIM)
    cos, sin = rope_tables(pos, HEAD_DIM)
    cos_i, sin_i = rope_tables(pos, IDX_DIM)
    q = apply_rope(q, cos, sin)
    k = apply_rope(k, cos, sin)
    qi = apply_rope(qi, cos_i, sin_i)
    ki = apply_rope(ki, cos_i, sin_i)
    if past is None:
        k_all, v_all, ki_all = k, v, ki
        conv_hist = jnp.zeros((B, CONV_WIDTH - 1, C_CONV), h.dtype)
    else:
        k_past, v_past, ki_past, conv_hist = past
        k_all = jnp.concatenate([k_past.astype(k.dtype), k], axis=1)
        v_all = jnp.concatenate([v_past.astype(v.dtype), v], axis=1)
        ki_all = jnp.concatenate([ki_past.astype(ki.dtype), ki], axis=1)
    conv_out, conv_state = conformer_conv(a, g, conv_hist, conv_w, conv_b, ln_g, ln_b)
    attn_out = sparse_attention(q, qi, wi, pos, k_all, v_all, ki_all)
    mixed = jnp.concatenate([conv_out, attn_out.reshape(B, T, ATT_WIDTH)], axis=-1) @ w_out
    return mixed, (k, v, ki, conv_state)

def encoder_layer(x, pos, past, lw):
    x = half_step_ffn(x, lw['ffn1_norm_pre'], lw['ffn1_norm_post'], lw['ffn1_w_up'], lw['ffn1_w_down'])
    h = rms_norm(x, lw['mix_norm_pre'])
    m, new_state = hybrid_mixer(h, pos, past, lw['w_in'], lw['conv_w'], lw['conv_b'],
                                lw['conv_ln_g'], lw['conv_ln_b'], lw['w_out'])
    x = x + rms_norm(m, lw['mix_norm_post'])
    x = half_step_ffn(x, lw['ffn2_norm_pre'], lw['ffn2_norm_post'], lw['ffn2_w_up'], lw['ffn2_w_down'])
    return x, new_state

def setup_inputs(seed: int = 0) -> dict:
    key = jax.random.key(seed)
    ks = jax.random.split(key, 24)
    f32 = jnp.float32

    def nrm(k, shape, scale):
        return jax.random.normal(k, shape, f32) * scale

    def gain(k, shape):
        return 1.0 + 0.02 * jax.random.normal(k, shape, f32)

    return {
        'x_prompt': nrm(ks[0], (BATCH, SEQ, D_MODEL), 1.0),
        'x_sample': nrm(ks[1], (DEC_BATCH, DEC_SEQ, D_MODEL), 1.0),
        'cache_k': nrm(ks[2], (DEPTH, DEC_BATCH, PAST_LEN, N_HEADS, HEAD_DIM), 1.0),
        'cache_v': nrm(ks[3], (DEPTH, DEC_BATCH, PAST_LEN, N_HEADS, HEAD_DIM), 1.0),
        'cache_kidx': nrm(ks[4], (DEPTH, DEC_BATCH, PAST_LEN, IDX_DIM), 1.0),
        'state_conv': nrm(ks[5], (DEPTH, DEC_BATCH, CONV_WIDTH - 1, C_CONV), 0.5),
        'ffn1_norm_pre': gain(ks[6], (DEPTH, D_MODEL)),
        'ffn1_norm_post': gain(ks[7], (DEPTH, D_MODEL)),
        'ffn1_w_up': nrm(ks[8], (DEPTH, D_MODEL, 2 * D_FF), D_MODEL ** -0.5),
        'ffn1_w_down': nrm(ks[9], (DEPTH, D_FF, D_MODEL), D_FF ** -0.5),
        'mix_norm_pre': gain(ks[10], (DEPTH, D_MODEL)),
        'mix_norm_post': gain(ks[11], (DEPTH, D_MODEL)),
        'w_in': nrm(ks[12], (DEPTH, D_MODEL, IN_COLS), D_MODEL ** -0.5),
        'conv_w': nrm(ks[13], (DEPTH, CONV_WIDTH, C_CONV), CONV_WIDTH ** -0.5),
        'conv_b': nrm(ks[14], (DEPTH, C_CONV), 0.02),
        'conv_ln_g': gain(ks[15], (DEPTH, C_CONV)),
        'conv_ln_b': nrm(ks[16], (DEPTH, C_CONV), 0.02),
        'w_out': nrm(ks[17], (DEPTH, MIX_WIDTH, D_MODEL), MIX_WIDTH ** -0.5),
        'ffn2_norm_pre': gain(ks[18], (DEPTH, D_MODEL)),
        'ffn2_norm_post': gain(ks[19], (DEPTH, D_MODEL)),
        'ffn2_w_up': nrm(ks[20], (DEPTH, D_MODEL, 2 * D_FF), D_MODEL ** -0.5),
        'ffn2_w_down': nrm(ks[21], (DEPTH, D_FF, D_MODEL), D_FF ** -0.5),
    }

def reference(x_prompt, x_sample, cache_k, cache_v, cache_kidx, state_conv,
              ffn1_norm_pre, ffn1_norm_post, ffn1_w_up, ffn1_w_down,
              mix_norm_pre, mix_norm_post, w_in, conv_w, conv_b, conv_ln_g, conv_ln_b, w_out,
              ffn2_norm_pre, ffn2_norm_post, ffn2_w_up, ffn2_w_down):
    past_len = cache_k.shape[2]
    pos_p = jnp.arange(x_prompt.shape[1])
    pos_s = past_len + jnp.arange(x_sample.shape[1])
    yp, ys = x_prompt, x_sample
    pk, pv, pki, pc = [], [], [], []
    sk, sv, ski, sc = [], [], [], []
    for l in range(DEPTH):
        lw = {
            'ffn1_norm_pre': ffn1_norm_pre[l], 'ffn1_norm_post': ffn1_norm_post[l],
            'ffn1_w_up': ffn1_w_up[l], 'ffn1_w_down': ffn1_w_down[l],
            'mix_norm_pre': mix_norm_pre[l], 'mix_norm_post': mix_norm_post[l],
            'w_in': w_in[l], 'conv_w': conv_w[l], 'conv_b': conv_b[l],
            'conv_ln_g': conv_ln_g[l], 'conv_ln_b': conv_ln_b[l], 'w_out': w_out[l],
            'ffn2_norm_pre': ffn2_norm_pre[l], 'ffn2_norm_post': ffn2_norm_post[l],
            'ffn2_w_up': ffn2_w_up[l], 'ffn2_w_down': ffn2_w_down[l],
        }
        yp, (k_p, v_p, ki_p, c_p) = encoder_layer(yp, pos_p, None, lw)
        ys, (k_s, v_s, ki_s, c_s) = encoder_layer(
            ys, pos_s, (cache_k[l], cache_v[l], cache_kidx[l], state_conv[l]), lw)
        pk.append(k_p); pv.append(v_p); pki.append(ki_p); pc.append(c_p)
        sk.append(k_s); sv.append(v_s); ski.append(ki_s); sc.append(c_s)
    return (yp, ys,
            jnp.stack(pk), jnp.stack(pv), jnp.stack(pki), jnp.stack(pc),
            jnp.stack(sk), jnp.stack(sv), jnp.stack(ski), jnp.stack(sc))


_drawn_inputs = setup_inputs


def setup_inputs(seed=0):
    import zlib

    import numpy as np

    out = dict(_drawn_inputs(seed))
    spreads = {}
    factors = {'ffn2_norm_pre': 3.009, 'ffn2_norm_post': 3.907}
    for name, (base, spread) in spreads.items():
        noise = np.random.default_rng([zlib.crc32(name.encode()), seed]).standard_normal(out[name].shape)
        drawn = base * np.exp(spread * noise) if base else spread * noise
        out[name] = __import__('jax').numpy.asarray(drawn.astype(out[name].dtype))
    for name, factor in factors.items():
        out[name] = (out[name] * factor).astype(out[name].dtype)
    return out
```

```python
from contextlib import ExitStack

import numpy as np

import concourse.bass as bass
from concourse import mybir

F32 = mybir.dt.float32
F32R = mybir.dt.float32r
ALU = mybir.AluOpType
ACT = mybir.ActivationFunctionType
AX_X = mybir.AxisListType.X

P = 128
D = 1024
SEQ = 256
DEC = 32
T = SEQ + DEC
PAST = 512
SKEYS = PAST + DEC
DEPTH = 2
DFF = 2816
KD = D // P
KF = DFF // P
CC = 512
CT = CC // P
TAPS = 31
HIST = TAPS - 1
HEADS = 8
HD = 64
CHUNK = 64
THETA = 10000.0
TOPK_P = min(256, SEQ // 4)
TOPK_S = min(256, SKEYS // 4)
EPS = 1e-6
STRIP = 256
NEG = -1.0e30
BARRED = -1.0e38
TAKEN = -3.0e38
TOK = [(0, 128), (128, 128), (256, 32)]

UP_STEPS = DFF // STRIP
QI_COL = 5 * CC
KI_COL = QI_COL + CC
WIDX = 2 * HD + HEADS
EXT = HIST + SEQ + HIST + DEC
CO = EXT - HIST
SAMPLE_AT = SEQ + HIST
U_UP, U_DOWN, U_IN, U_OUT = 4 * UP_STEPS, 24, 24, 8
U_LAYER = 2 * (U_UP + U_DOWN) + U_IN + U_OUT
U_TOTAL = DEPTH * U_LAYER
PARTS = (8, 8, 6)
QI, A, G, Q, K, V = 0, 4, 8, 12, 16, 20


def ffn_unit(f):
    return (f // 2) * U_LAYER + (f % 2) * (U_UP + U_DOWN + U_IN + U_OUT)


def mix_unit(m):
    return m * U_LAYER + U_UP + U_DOWN


def gain(n, l, c):
    return (n * DEPTH + l) * KD + c


def cvec(n, l, ct):
    return 6 * DEPTH * KD + (n * DEPTH + l) * CT + ct


def build(nc, ins, consts, outs):
    (y_prompt, y_sample, prompt_k, prompt_v, prompt_ki, prompt_conv,
     sample_k, sample_v, sample_ki, sample_conv) = outs
    with ExitStack() as ctx:
        BASE = (nc.sbuf_base + 31) // 32 * 32
        SIZE = nc.sbuf_usable_end - BASE
        ctx.enter_context(nc.sbuf_tensor("arena", [P, (SIZE - 64) // 4], F32))
        at = [0]

        def sb(name, shape, dt=F32):
            size = int(np.prod(shape[1:])) * 4
            t = nc.alloc_sbuf_tensor_at(name, list(shape), dt, offset=BASE + at[0])
            at[0] += (size + 31) // 32 * 32
            assert at[0] <= SIZE - 64, (name, at[0])
            return t

        def sem(name):
            return ctx.enter_context(nc.semaphore(name))

        raw = sb("raw", [P, 2, 8, STRIP])
        whi = sb("whi", [P, 4, 8, P], F32R)
        wlo = sb("wlo", [P, 4, 8, P], F32R)
        x = sb("x", [P, KD, T])
        hh = sb("hh", [P, KD, T], F32R)
        hl = sb("hl", [P, KD, T], F32R)
        y = sb("y", [P, KD * T])
        ht = sb("ht", [P, 2 * T])
        sq = sb("sq", [P, 2, T])
        ysq = sb("ysq", [P, 2 * T])
        acc = sb("acc", [P, T])
        root = sb("root", [P, T])
        rinv = sb("rinv", [P, T])
        shared_a = at[0]
        upd = sb("upd", [P, 2 * T])
        sil = sb("sil", [P, 2 * T])
        gt = sb("gt", [P, 2 * T])
        g_at = at[0]
        ghi = sb("ghi", [P, KF * T], F32R)
        glo = sb("glo", [P, KF * T], F32R)
        g_end = at[0]
        proj_at = at[0]
        proj = sb("proj", [P, 24 * T])
        ident = sb("ident", [P, P])
        ones = sb("ones", [P, P])
        swap = sb("swap", [P, P])
        cosT = sb("cosT", [P, T])
        sinT = sb("sinT", [P, T])
        par = sb("par", [P, 120])
        taps = sb("taps", [P, DEPTH * CT * TAPS])
        ext = sb("ext", [P, CT, EXT])
        kiT = sb("kiT", [P, T])
        wiT = sb("wiT", [HEADS, T])
        wrow = sb("wrow", [P, 3 * HEADS])
        score = sb("score", [P, 928])
        m8 = sb("m8", [P, 8])
        epsc = sb("epsc", [P, 2])
        stat = sb("stat", [P, 10 * 8])
        statein = sb("statein", [HIST, CC])
        at[0] = g_at
        wtail = sb("wtail", [P, KD, WIDX])
        wthi = sb("wthi", [P, KD, WIDX], F32R)
        wtlo = sb("wtlo", [P, KD, WIDX], F32R)
        rel_at = at[0]
        relP = sb("relP", [P, 2, 384])
        relS = sb("relS", [DEC, 2, SKEYS])
        kidx = sb("kidx", [P, 4, 2 * HD])
        kiTs = sb("kiTs", [P, SKEYS])
        ropa = sb("ropa", [P, T])
        ropb = sb("ropb", [P, T])
        kc_at = at[0]
        kc = sb("kc", [P, 4, CC])
        vc = sb("vc", [P, 4, CC])
        vrow = sb("vrow", [P, 3, CC])
        kirow = sb("kirow", [P, 3, HD])
        assert at[0] <= g_end, at[0] - g_end
        at[0] = g_at
        kTs = sb("kTs", [P, 4, SKEYS])
        at[0] = rel_at
        prob = sb("prob", [P, 2, SKEYS])
        maskS = sb("maskS", [P, SKEYS])
        at[0] = kc_at
        krow = sb("krow", [P, 3, CC])
        at[0] = shared_a
        probT = sb("probT", [P, 2, 640])
        at[0] = proj_at + A * T * 4
        yc = sb("yc", [P, CT, CO])
        crow = sb("crow", [HIST, 2, CC])
        assert at[0] <= proj_at + Q * T * 4
        at[0] = g_at
        xrow = sb("xrow", [P, 3, D])
        prow = sb("prow", [120, P])
        trow = sb("trow", [TAPS, DEPTH * CC])
        ps = ctx.enter_context(nc.psum_tensor("ps", [P, 8 * 512], F32))

        def bank(b, rows=slice(0, P), lo=0, n=T):
            return ps[rows, 512 * b + lo:512 * b + lo + n]

        const_in = sem("const_in")
        x_in = sem("x_in")
        par_in = sem("par_in")
        par_T = sem("par_T")
        par_ready = sem("par_ready")
        x_T = sem("x_T")
        loaded = [sem("loaded0"), sem("loaded1")]
        hi_ready = sem("hi_ready")
        lo_ready = sem("lo_ready")
        w_used = sem("w_used")
        x_ready = sem("x_ready")
        sq_ready = sem("sq_ready")
        sq_used = sem("sq_used")
        root_ready = sem("root_ready")
        ht_ready = sem("ht_ready")
        hh_ready = sem("hh_ready")
        hl_ready = sem("hl_ready")
        silu_ready = sem("silu_ready")
        gt_ready = sem("gt_ready")
        ghi_ready = sem("ghi_ready")
        glo_ready = sem("glo_ready")
        ysq_ready = sem("ysq_ready")
        acc_ready = sem("acc_ready")
        ss_done = sem("ss_done")
        proj_saved = sem("proj_saved")
        tail_in = sem("tail_in")
        tail_hi = sem("tail_hi")
        tail_lo = sem("tail_lo")
        tail_done = sem("tail_done")
        tail_saved = sem("tail_saved")
        kidx_in = sem("kidx_in")
        kc_in = sem("kc_in")
        vc_in = sem("vc_in")
        state_in = sem("state_in")
        rope_mm = sem("rope_mm")
        rope_done = sem("rope_done")
        wi_T = sem("wi_T")
        wrow_ready = sem("wrow_ready")
        kidx_T = sem("kidx_T")
        kiTs_ready = sem("kiTs_ready")
        lg_done = sem("lg_done")
        rel_ready = sem("rel_ready")
        rel_used = sem("rel_used")
        mask_ready = sem("mask_ready")
        sig_ready = sem("sig_ready")
        u_ready = sem("u_ready")
        st_T = sem("st_T")
        st_ready = sem("st_ready")
        crow_T = sem("crow_T")
        crow_ready = sem("crow_ready")
        conv_ready = sem("conv_ready")
        mu_done = sem("mu_done")
        dev_ready = sem("dev_ready")
        csq_ready = sem("csq_ready")
        csq_used = sem("csq_used")
        croot_ready = sem("croot_ready")
        cn_ready = sem("cn_ready")
        cmix_ready = sem("cmix_ready")
        vrow_T = sem("vrow_T")
        vrow_ready = sem("vrow_ready")
        kcT_done = sem("kcT_done")
        kTs_ready = sem("kTs_ready")
        krow_T = sem("krow_T")
        krow_ready = sem("krow_ready")
        s_done = sem("s_done")
        max_ready = sem("max_ready")
        exp_ready = sem("exp_ready")
        p_ready = sem("p_ready")
        pT_done = sem("pT_done")
        pT_ready = sem("pT_ready")
        pv_done = sem("pv_done")
        att_saved = sem("att_saved")
        rows_out = sem("rows_out")
        yT_done = sem("yT_done")
        yrow_ready = sem("yrow_ready")
        y_out = sem("y_out")
        dve_chain = sem("dve_chain")
        act_chain = sem("act_chain")
        ms_ready = sem("ms_ready")

        w_of = {0: ("ffn1_w_up", "ffn1_w_down"), 1: ("ffn2_w_up", "ffn2_w_down")}

        def strip_view(w, l, r0, rows, c0):
            return ins[w][l, r0:r0 + rows, :].rearrange("(k p) n -> p k n", p=P)[:, :, bass.ds(c0, STRIP)]

        block = ctx.enter_context(nc.Block())

        @block.sync
        def _(sp):
            def load(q, wait, src, n=8):
                if wait is not None:
                    sp.wait_ge(lo_ready, wait)
                sp.dma_start(raw[:, q, 0:n, :], src).then_inc(loaded[q], 16)

            def up_step(f, i, free=True):
                w = w_of[f % 2][0]
                u = ffn_unit(f)
                load(0, u + 4 * i - 2 if free else None, strip_view(w, f // 2, 0, D, i * STRIP))
                load(1, u + 4 * i if free else None, strip_view(w, f // 2, 0, D, i * STRIP + DFF))

            def down_step(f, i):
                w = w_of[f % 2][1]
                u = ffn_unit(f) + U_UP
                for r in range(6):
                    d, part = divmod(r, 3)
                    load(r % 2, u + 12 * i + 2 * r - 2,
                         strip_view(w, f // 2, part * 8 * P, PARTS[part] * P, (2 * i + d) * STRIP), PARTS[part])

            def in_step(m, i, c0):
                u = mix_unit(m)
                load(0, u + 4 * i - 2, strip_view("w_in", m, 0, D, c0))
                load(1, u + 4 * i, strip_view("w_in", m, 0, D, c0 + STRIP))

            for f in range(2 * DEPTH):
                if f == 0:
                    sp.dma_start(raw[:, 0], strip_view("ffn1_w_up", 0, 0, D, 0)).then_inc(loaded[0], 16)
                    sp.dma_start(raw[:, 1], strip_view("ffn1_w_up", 0, 0, D, DFF)).then_inc(loaded[1], 16)
                else:
                    up_step(f, 0)
                with sp.Fori(1, UP_STEPS) as i:
                    up_step(f, i)
                with sp.Fori(0, 2) as i:
                    down_step(f, i)
                if f % 2 == 0:
                    m = f // 2
                    in_step(m, 0, QI_COL)
                    with sp.Fori(1, 6) as i:
                        in_step(m, i, (i - 1) * 2 * STRIP)
                    u = mix_unit(m) + U_IN
                    for i in range(2):
                        for q in range(2):
                            load(q, u + 4 * i + 2 * q - 2, strip_view("w_out", m, 0, D, (2 * i + q) * STRIP))
            for tt, (t0, n) in enumerate(TOK):
                sp.wait_ge(yrow_ready, 2 * tt + 2)
                dst = y_prompt[0, t0:t0 + n, :] if tt < 2 else y_sample[0]
                sp.dma_start(dst, xrow[0:n, tt, :]).then_inc(y_out, 16)
            sp.wait_ge(y_out, 48)

        @block.scalar
        def _(act):
            n_chain = [0]

            def link(ins_):
                n_chain[0] += 1
                ins_.then_inc(act_chain, 1)
                act.wait_ge(act_chain, n_chain[0])

            def split_hi(unit, raw_slot, split_slot, half, raw_count, n=8, old=True):
                act.wait_ge(loaded[raw_slot], 16 * raw_count)
                if old:
                    act.wait_ge(w_used, unit - 3)
                act.activation(whi[:, split_slot, 0:n, :], raw[:, raw_slot, 0:n, half * P:(half + 1) * P],
                               ACT.Copy).then_inc(hi_ready, 1)

            def split_quad(u0, i, rel, down_raw=None, old=True):
                q, half = divmod(rel, 2)
                split_hi(u0 + 4 * i + rel, q, rel, half, u0 // 4 + i + 1, 8, old)

            def pre_norm(s, hq):
                for c in range(KD):
                    act.wait_ge(x_ready, 8 * s + c + 1)
                    if 8 * s + c - 1 > 0:
                        act.wait_ge(sq_used, 8 * s + c - 1)
                    act.activation(sq[:, c % 2, :], x[:, c, :], ACT.Square).then_inc(sq_ready, 1)
                act.wait_ge(sq_used, 8 * s + 8)
                act.activation(root[:], bank(6), ACT.Sqrt, bias=epsc[:, 0:1], scale=1.0 / D).then_inc(root_ready, 1)
                for c in range(KD):
                    act.wait_ge(ht_ready, 8 * s + c + 1)
                    act.activation(hh[:, c, :], ht[:, (c % 2) * T:(c % 2 + 1) * T], ACT.Copy).then_inc(hh_ready, 1)

            def post_root(s, half_step):
                k = 4.0 if half_step else 1.0
                act.wait_ge(ss_done, s + 1)
                act.activation(root[:], bank(6), ACT.Sqrt, bias=epsc[:, 1:2] if half_step else epsc[:, 0:1],
                               scale=k / D).then_inc(root_ready, 1)

            def save_y(s, c, b, slot, unit):
                act.wait_ge(w_used, unit + 1)
                act.activation(y[:, bass.ds(c * T, T)], bank(b), ACT.Copy)
                act.wait_ge(acc_ready, 10 * s + c + 1)
                act.activation(ysq[:, slot * T:(slot + 1) * T], bank(b), ACT.Square).then_inc(ysq_ready, 1)

            def ffn(f, s):
                u = ffn_unit(f)

                def up_step(i, first):
                    for j in range(2):
                        act.wait_ge(w_used, u + 4 * i + j + 1)
                        if not first:
                            act.wait_ge(gt_ready, KF * f + 2 * i + j - 1)
                        act.activation(sil[:, j * T:(j + 1) * T], bank(j), ACT.Silu).then_inc(silu_ready, 1)
                        split_quad(u + 4, i, j)
                    for j in range(2):
                        split_quad(u + 4, i, 2 + j)
                        act.wait_ge(gt_ready, KF * f + 2 * i + j + 1)
                        act.activation(ghi[:, bass.ds((2 * i + j) * T, T)], gt[:, j * T:(j + 1) * T],
                                       ACT.Copy).then_inc(ghi_ready, 1)

                up_step(0, True)
                with act.Fori(1, UP_STEPS) as i:
                    up_step(i, False)
                ud = u + U_UP

                def ahead(i, j, last):
                    jj = j + 4
                    if jj < 12:
                        r, half = divmod(jj, 2)
                        split_hi(ud + 12 * i + jj, r % 2, jj % 4, half, ud // 4 + 3 * i + r // 2 + 1, PARTS[r % 3])
                    elif not last:
                        r, half = divmod(jj - 12, 2)
                        split_hi(ud + 12 * i + jj, r % 2, jj % 4, half, ud // 4 + 3 * i + 3 + r // 2 + 1, 8)

                def down_step(i, last):
                    for d in range(2):
                        for j in range(6):
                            ahead(i, 6 * d + j, last)
                        for col in range(2):
                            save_y(s, 4 * i + 2 * d + col, 2 * d + col, col, ud + 12 * i + 6 * d + 4 + col)

                if f < 2 * DEPTH - 1:
                    with act.Fori(0, 2) as i:
                        down_step(i, False)
                else:
                    down_step(0, False)
                    down_step(1, True)
                post_root(s, True)

            def mixer(m, s):
                u = mix_unit(m)
                act.wait_ge(tail_in, 48 * (m + 1))
                act.activation(wthi[:], wtail[:], ACT.Copy).then_inc(tail_hi, 1)

                def in_step(i, first):
                    for j in range(4):
                        act.wait_ge(w_used, u + 4 * i + j + 1)
                        act.activation(proj[:, bass.ds((4 * i + j) * T, T)], bank(j), ACT.Copy).then_inc(proj_saved, 1)
                        split_quad(u + 4, i, j)

                in_step(0, True)
                act.wait_ge(tail_done, 2 * m + 1)
                act.activation(kiT[:], bank(4), ACT.Copy).then_inc(tail_saved, 1)
                act.wait_ge(tail_done, 2 * m + 2)
                act.activation(wiT[:], bank(5, slice(0, HEADS)), ACT.Copy).then_inc(tail_saved, 1)
                act.wait_ge(kidx_T, m + 1)
                act.activation(kiTs[:, 0:PAST], bank(5, n=PAST), ACT.Copy)
                act.wait_ge(rope_done, 13 * m + 5)
                act.activation(kiTs[:, PAST:SKEYS], kiT[:, SEQ:T], ACT.Copy).then_inc(kiTs_ready, 1)
                for h in range(HEADS):
                    act.wait_ge(lg_done, 8 * m + h + 1)
                    if h >= 2:
                        act.wait_ge(rel_used, 8 * m + h - 1)
                    act.activation(relP[:, h % 2, :], bank(6 + h % 2, n=384), ACT.Relu, scale=HD ** -0.5)
                    act.activation(relS[:, h % 2, :], bank(2 * (h % 2), slice(0, DEC), n=SKEYS), ACT.Relu,
                                   scale=HD ** -0.5).then_inc(rel_ready, 1)
                with act.Fori(1, 3) as i:
                    in_step(i, False)
                act.wait_ge(proj_saved, 24 * m + 12)
                act.activation(proj[:, G * T:Q * T], proj[:, G * T:Q * T], ACT.Sigmoid).then_inc(sig_ready, 1)
                with act.Fori(3, 6) as i:
                    in_step(i, False)
                act.wait_ge(st_T, m + 1)
                act.activation(ext[:, :, HIST + SEQ:HIST + SEQ + HIST],
                               bank(7, n=CT * HIST).rearrange("p (c t) -> p c t", c=CT), ACT.Copy).then_inc(st_ready, 1)
                for g in range(2):
                    act.wait_ge(crow_T, 2 * m + g + 1)
                    act.activation(crow[:, g, :], bank(2 + g, slice(0, HIST), n=CC), ACT.Copy).then_inc(crow_ready, 1)
                for tt, (t0, n) in enumerate(TOK):
                    act.wait_ge(vrow_T, 3 * m + tt + 1)
                    act.activation(vrow[0:n, tt, :], bank(4 + tt, slice(0, n), n=CC), ACT.Copy).then_inc(vrow_ready, 1)
                for hp in range(4):
                    act.wait_ge(kcT_done, 4 * m + hp + 1)
                    act.activation(kTs[:, hp, 0:PAST], bank(2 + hp % 2, n=PAST), ACT.Copy).then_inc(kTs_ready, 1)
                for hp in range(4):
                    act.wait_ge(rope_done, 13 * m + 5 + 4 + hp + 1)
                    act.activation(kTs[:, hp, PAST:SKEYS], proj[:, (K + hp) * T + SEQ:(K + hp + 1) * T],
                                   ACT.Copy).then_inc(kTs_ready, 1)
                for tt, (t0, n) in enumerate(TOK):
                    act.wait_ge(krow_T, 4 * m + tt + 1)
                    act.activation(krow[0:n, tt, :], bank(4 + tt, slice(0, n), n=CC), ACT.Copy).then_inc(krow_ready, 1)
                act.wait_ge(krow_T, 4 * m + 4)
                for tt, (t0, n) in enumerate(TOK):
                    last = act.activation(kirow[0:n, tt, :], bank(7, slice(0, n), HD * tt, HD), ACT.Copy)
                last.then_inc(krow_ready, 1)
                for ct in range(CT):
                    act.wait_ge(dev_ready, 4 * m + ct + 1)
                    if ct >= 2:
                        act.wait_ge(csq_used, 4 * m + ct - 1)
                    act.activation(y[:, (ct % 2) * CO:(ct % 2 + 1) * CO], yc[:, ct, :], ACT.Square).then_inc(csq_ready, 1)
                act.wait_ge(csq_used, 4 * m + 4)
                act.activation(ht[:, 0:CO], bank(7, n=CO), ACT.Sqrt, bias=epsc[:, 0:1],
                               scale=1.0 / CC).then_inc(croot_ready, 1)
                for ct in range(CT):
                    act.wait_ge(cn_ready, 4 * m + ct + 1)
                    for src, dst, n in ((0, 0, SEQ), (SAMPLE_AT, SEQ, DEC)):
                        last = act.activation(y[:, ct * T + dst:ct * T + dst + n], yc[:, ct, src:src + n], ACT.Silu,
                                              bias=par[:, cvec(2, m, ct):cvec(2, m, ct) + 1],
                                              scale=par[:, cvec(1, m, ct):cvec(1, m, ct) + 1])
                    last.then_inc(cmix_ready, 1)

                def softmax_exp(n):
                    act.wait_ge(max_ready, 10 * m + n + 1)
                    spans = [(0, SKEYS)] if n < 2 else [(0, P), (P, 384)]
                    for j, (a, b) in enumerate(spans):
                        last = act.activation(prob[:, n % 2, a:b], prob[:, n % 2, a:b], ACT.Exp,
                                              bias=stat[:, 8 * n + 2 + j:8 * n + 3 + j],
                                              accum_out=stat[:, 8 * n + 4 + j:8 * n + 5 + j])
                    last.then_inc(exp_ready, 1)

                def save_pT(n):
                    act.wait_ge(pT_done, 10 * m + n + 1)
                    if n >= 2:
                        act.wait_ge(pv_done, 10 * m + n - 1)
                    if n < 2:
                        act.activation(probT[:, n % 2, 0:512], bank(4, n=512), ACT.Copy)
                        act.activation(probT[0:DEC, n % 2, 512:640], bank(5, slice(0, DEC), n=P),
                                       ACT.Copy).then_inc(pT_ready, 1)
                    else:
                        act.activation(probT[:, n % 2, 0:384], bank(4 + n % 2, n=384), ACT.Copy).then_inc(pT_ready, 1)

                def save_att(n):
                    if n == 1:
                        act.wait_ge(pv_done, 10 * m + 2)
                        act.activation(y[:, 4 * T:8 * T].rearrange("p (c t) -> p c t", c=4)[:, :, SEQ:T],
                                       bank(7, n=P).rearrange("p (c t) -> p c t", c=4), ACT.Copy).then_inc(att_saved, 1)
                    elif n % 2:
                        hp = (n - 2) // 2
                        act.wait_ge(pv_done, 10 * m + n + 1)
                        act.activation(y[:, (4 + hp) * T:(4 + hp) * T + SEQ], bank(6 + hp % 2, n=SEQ),
                                       ACT.Copy).then_inc(att_saved, 1)

                softmax_exp(0)
                for n in range(10):
                    if n < 9:
                        softmax_exp(n + 1)
                    save_pT(n)
                    if n >= 1:
                        save_att(n - 1)
                save_att(9)
                for c in range(KD):
                    if c < 4:
                        act.wait_ge(cmix_ready, 4 * m + c + 1)
                    else:
                        act.wait_ge(att_saved, 5 * m + c - 4 + 2)
                    act.activation(hh[:, c, :], y[:, c * T:(c + 1) * T], ACT.Copy).then_inc(hh_ready, 1)
                uo = u + U_IN
                for i in range(2):
                    for j in range(4):
                        split_quad(uo + 4, i, j)
                        save_y(s, 4 * i + j, j, j % 2, uo + 4 * i + j)
                post_root(s, False)

            act.dma_start(xrow[:, 0:2, :], ins["x_prompt"][0].rearrange("(j p) d -> p j d", p=P)).then_inc(x_in, 16)
            act.dma_start(xrow[0:DEC, 2, :], ins["x_sample"][0]).then_inc(x_in, 16)
            for name, dst in (("ident", ident), ("swap", swap), ("cosT", cosT), ("sinT", sinT)):
                act.dma_start(dst[:], consts[name]).then_inc(const_in, 16)
            for n, name in enumerate(("ffn1_norm_pre", "ffn1_norm_post", "mix_norm_pre", "mix_norm_post",
                                      "ffn2_norm_pre", "ffn2_norm_post")):
                r = gain(n, 0, 0)
                act.dma_start(prow[r:r + DEPTH * KD, :], ins[name].rearrange("l (c p) -> (l c) p", p=P)).then_inc(par_in, 16)
            for n, name in enumerate(("conv_b", "conv_ln_g", "conv_ln_b")):
                r = cvec(n, 0, 0)
                act.dma_start(prow[r:r + DEPTH * CT, :], ins[name].rearrange("l (c p) -> (l c) p", p=P)).then_inc(par_in, 16)
            act.dma_start(trow[:].rearrange("k (l c) -> k l c", l=DEPTH),
                          ins["conv_w"].rearrange("l k c -> k l c")).then_inc(par_in, 16)
            act.wait_ge(par_T, 1)
            act.activation(par[:], bank(7, n=120), ACT.Copy)
            act.activation(taps[:], bank(5, n=DEPTH * CT * TAPS), ACT.Copy).then_inc(par_ready, 1)
            act.wait_ge(ms_ready, 1)
            for rel in range(4):
                split_quad(0, 0, rel, old=False)
            for l in range(DEPTH):
                pre_norm(3 * l, 4 * l)
                ffn(2 * l, 3 * l)
                pre_norm(3 * l + 1, 4 * l + 1)
                mixer(l, 3 * l + 1)
                pre_norm(3 * l + 2, 4 * l + 3)
                act.wait_ge(rows_out, 16 * 8 * (l + 1))
                ffn(2 * l + 1, 3 * l + 2)
            for n in range(6):
                tt, half = divmod(n, 2)
                act.wait_ge(yT_done, n + 1)
                k = TOK[tt][1]
                act.activation(xrow[0:k, tt, half * 512:(half + 1) * 512], bank(n, slice(0, k), n=512),
                               ACT.Copy).then_inc(yrow_ready, 1)

        @block.vector
        def _(dve):
            n_chain = [0]

            def link(ins_):
                n_chain[0] += 1
                ins_.then_inc(dve_chain, 1)
                dve.wait_ge(dve_chain, n_chain[0])

            def split_lo(unit, raw_slot, split_slot, half, n=8):
                dve.wait_ge(hi_ready, unit + 1)
                cols = slice(half * P, (half + 1) * P)
                dve.tensor_tensor(wlo[:, split_slot, 0:n, :], raw[:, raw_slot, 0:n, cols],
                                  whi[:, split_slot, 0:n, :].bitcast(F32), ALU.subtract).then_inc(lo_ready, 1)

            def split_quad(u0, i, rel):
                q, half = divmod(rel, 2)
                split_lo(u0 + 4 * i + rel, q, rel, half)

            def normalise(s, hq, g):
                dve.wait_ge(root_ready, 2 * s + 1)
                link(dve.reciprocal(rinv[:], root[:]))

                def low(c):
                    dve.wait_ge(hh_ready, 8 * hq + c + 1)
                    dve.tensor_tensor(hl[:, c, :], ht[:, (c % 2) * T:(c % 2 + 1) * T],
                                      hh[:, c, :].bitcast(F32), ALU.subtract).then_inc(hl_ready, 1)
                for c in range(KD):
                    if c >= 2:
                        dve.wait_ge(hl_ready, 8 * hq + c - 1)
                    dve.scalar_tensor_tensor(out=ht[:, (c % 2) * T:(c % 2 + 1) * T], in0=x[:, c, :],
                                             scalar=par[:, g + c:g + c + 1], in1=rinv[:],
                                             op0=ALU.mult, op1=ALU.mult).then_inc(ht_ready, 1)
                    if c >= 1:
                        low(c - 1)
                low(KD - 1)

            def clear_acc(s):
                dve.memset(acc[:], 0.0).then_inc(acc_ready, 2)

            def add_sq(s, c, slot):
                dve.wait_ge(ysq_ready, 8 * s + c + 1)
                dve.wait_ge(acc_ready, 10 * s + c + 2)
                dve.tensor_tensor(acc[:], acc[:], ysq[:, slot * T:(slot + 1) * T], ALU.add).then_inc(acc_ready, 1)

            def residual(s, g):
                dve.wait_ge(root_ready, 2 * s + 2)
                link(dve.reciprocal(rinv[:], root[:]))
                for c in range(KD):
                    k = slice((c % 2) * T, (c % 2 + 1) * T)
                    if c >= 2:
                        dve.wait_ge(x_ready, 8 * (s + 1) + c - 1)
                    link(dve.scalar_tensor_tensor(out=upd[:, k], in0=y[:, c * T:(c + 1) * T],
                                                  scalar=par[:, g + c:g + c + 1], in1=rinv[:],
                                                  op0=ALU.mult, op1=ALU.mult))
                    dve.tensor_tensor(x[:, c, :], x[:, c, :], upd[:, k], ALU.add).then_inc(x_ready, 1)

            def ffn(f, s, g):
                u = ffn_unit(f)

                def up_step(i, first):
                    split_quad(u + 4, i, 0)
                    split_quad(u + 4, i, 1)

                    def low(j):
                        dve.wait_ge(ghi_ready, KF * f + 2 * i + j + 1)
                        dve.tensor_tensor(glo[:, bass.ds((2 * i + j) * T, T)], gt[:, j * T:(j + 1) * T],
                                          ghi[:, bass.ds((2 * i + j) * T, T)].bitcast(F32),
                                          ALU.subtract).then_inc(glo_ready, 1)
                    for j in range(2):
                        dve.wait_ge(silu_ready, KF * f + 2 * i + j + 1)
                        dve.wait_ge(w_used, u + 4 * i + 2 + j + 1)
                        if not first:
                            dve.wait_ge(glo_ready, KF * f + 2 * i + j - 1)
                        dve.tensor_tensor(gt[:, j * T:(j + 1) * T], sil[:, j * T:(j + 1) * T], bank(2 + j),
                                          ALU.mult).then_inc(gt_ready, 1)
                        split_quad(u + 4, i, 2 + j)
                        low(j)

                up_step(0, True)
                with dve.Fori(1, UP_STEPS) as i:
                    up_step(i, False)
                ud = u + U_UP
                clear_acc(s)

                def down_step(i, last):
                    for d in range(2):
                        for j in range(6):
                            jj = 6 * d + j + 4
                            r, half = divmod(jj % 12, 2)
                            if jj < 12 or not last:
                                split_lo(ud + 12 * i + jj, r % 2, jj % 4, half, PARTS[r % 3] if jj < 12 else 8)
                        for col in range(2):
                            add_sq(s, 4 * i + 2 * d + col, col)

                if f < 2 * DEPTH - 1:
                    with dve.Fori(0, 2) as i:
                        down_step(i, False)
                else:
                    down_step(0, False)
                    down_step(1, True)
                residual(s, g)

            def rope(m, k, tile, b):
                dve.wait_ge(rope_mm, 13 * m + k + 1)
                if k:
                    dve.wait_ge(rope_done, 13 * m + k)
                link(dve.tensor_tensor(ropa[:], tile, cosT[:], ALU.mult))
                link(dve.tensor_tensor(ropb[:], bank(b), sinT[:], ALU.mult))
                dve.tensor_tensor(tile, ropa[:], ropb[:], ALU.add).then_inc(rope_done, 1)

            def top_k(rows, a, b, k):
                for _ in range(k // 8):
                    link(dve.max(m8[rows, :], score[rows, a:b]))
                    link(dve.match_replace(score[rows, a:b], m8[rows, :], score[rows, a:b], TAKEN))

            def mixer(m, s, g):
                for k in range(4):
                    rope(m, k, proj[:, (QI + k) * T:(QI + k + 1) * T], 6 + k % 2)
                rope(m, 4, kiT[:], 6)
                dve.wait_ge(wi_T, m + 1)
                link(dve.tensor_scalar(wrow[:, 0:16], bank(4, n=16), HEADS ** -0.5, None, ALU.mult))
                link(dve.tensor_scalar(wrow[0:DEC, 16:24], bank(4, slice(0, DEC), 16, 8), HEADS ** -0.5, None, ALU.mult))
                areas = [(slice(0, P), 0, P, 0), (slice(0, P), P, 384, 8), (slice(0, DEC), 384, 928, 16)]
                for h in range(HEADS):
                    dve.wait_ge(rel_ready, 8 * m + h + 1)
                    for rows, a, b, w0 in areas:
                        src = relP[:, h % 2, a:b] if a < 384 else relS[:, h % 2, :]
                        w = wrow[rows, w0 + h:w0 + h + 1]
                        if h == 0:
                            last = dve.tensor_scalar(score[rows, a:b], src, w, None, ALU.mult)
                        else:
                            last = dve.scalar_tensor_tensor(out=score[rows, a:b], in0=src, scalar=w,
                                                            in1=score[rows, a:b], op0=ALU.mult, op1=ALU.add)
                    last.then_inc(rel_used, 1)
                    dve.wait_ge(rel_used, 8 * m + h + 1)
                dve.memset(score[0:CHUNK, CHUNK:P], BARRED)
                link(dve.memset(score[0:CHUNK, P + 3 * CHUNK:P + 4 * CHUNK], BARRED))
                top_k(slice(0, DEC), 384, 928, TOPK_S)
                top_k(slice(0, P), 0, P, TOPK_P)
                top_k(slice(0, P), P, 384, TOPK_P)
                for j in range(4):
                    dve.tensor_scalar(maskS[32 * j:32 * j + 32, :], score[0:DEC, 384:928], TAKEN, NEG,
                                      ALU.not_equal, ALU.mult)
                link(dve.tensor_scalar(score[:, 0:384], score[:, 0:384], TAKEN, NEG, ALU.not_equal, ALU.mult))
                dve.wait_ge(u_ready, m + 1)
                dve.wait_ge(st_ready, m + 1)
                for k in range(TAPS):
                    for ct in range(CT):
                        w = taps[:, (m * CT + ct) * TAPS + k:(m * CT + ct) * TAPS + k + 1]
                        src = ext[:, ct, k:k + CO]
                        if k == 0:
                            ins_ = dve.tensor_scalar(yc[:, ct, :], src, w, par[:, cvec(0, m, ct):cvec(0, m, ct) + 1],
                                                     ALU.mult, ALU.add)
                        else:
                            dve.wait_ge(conv_ready, (m * TAPS + k - 1) * CT + ct + 1)
                            ins_ = dve.scalar_tensor_tensor(out=yc[:, ct, :], in0=src, scalar=w, in1=yc[:, ct, :],
                                                            op0=ALU.mult, op1=ALU.add)
                        ins_.then_inc(conv_ready, 1)
                for k in range(5, 13):
                    rope(m, k, proj[:, (Q + k - 5) * T:(Q + k - 4) * T], k % 2)
                dve.wait_ge(mu_done, m + 1)
                for ct in range(CT):
                    dve.scalar_tensor_tensor(out=yc[:, ct, :], in0=bank(7, n=CO), scalar=-1.0 / CC, in1=yc[:, ct, :],
                                             op0=ALU.mult, op1=ALU.add).then_inc(dev_ready, 1)
                dve.wait_ge(croot_ready, m + 1)
                dve.wait_ge(dev_ready, 4 * m + 4)
                link(dve.reciprocal(ht[:, 0:CO], ht[:, 0:CO]))
                for ct in range(CT):
                    dve.tensor_tensor(yc[:, ct, :], yc[:, ct, :], ht[:, 0:CO], ALU.mult).then_inc(cn_ready, 1)

                def softmax_max(n):
                    dve.wait_ge(s_done, 10 * m + n + 1)
                    if n >= 2:
                        dve.wait_ge(pT_done, 10 * m + n - 1)
                    spans = [(0, SKEYS)] if n < 2 else [(0, P), (P, 384)]
                    c = 8 * n
                    for j, (a, b) in enumerate(spans):
                        logits = ps[:, 1024 * (n % 2) + a:1024 * (n % 2) + b]
                        mask = maskS[:] if n < 2 else score[:, a:b]
                        link(dve.tensor_tensor_reduce(prob[:, n % 2, a:b], logits, mask, HD ** -0.5, -3.0e38,
                                                      ALU.add, ALU.max, stat[:, c + j:c + j + 1]))
                    k = len(spans)
                    dve.tensor_scalar(stat[:, c + 2:c + 2 + k], stat[:, c:c + k], -1.0, None,
                                      ALU.mult).then_inc(max_ready, 1)

                def softmax_norm(n):
                    dve.wait_ge(exp_ready, 10 * m + n + 1)
                    spans = [(0, SKEYS)] if n < 2 else [(0, P), (P, 384)]
                    k, c = len(spans), 8 * n
                    link(dve.reciprocal(stat[:, c + 6:c + 6 + k], stat[:, c + 4:c + 4 + k]))
                    for j, (a, b) in enumerate(spans):
                        last = dve.tensor_scalar(prob[:, n % 2, a:b], prob[:, n % 2, a:b],
                                                 stat[:, c + 6 + j:c + 7 + j], None, ALU.mult)
                    last.then_inc(p_ready, 1)

                softmax_max(0)
                for n in range(10):
                    if n < 9:
                        softmax_max(n + 1)
                    softmax_norm(n)
                for c in range(KD):
                    dve.wait_ge(hh_ready, 8 * (4 * m + 2) + c + 1)
                    dve.tensor_tensor(hl[:, c, :], y[:, c * T:(c + 1) * T], hh[:, c, :].bitcast(F32),
                                      ALU.subtract).then_inc(hl_ready, 1)
                clear_acc(s)
                for c in range(KD):
                    add_sq(s, c, c % 2)
                residual(s, g)

            dve.memset(ones[:], 1.0)
            dve.memset(epsc[:, 0:1], EPS)
            dve.memset(epsc[:, 1:2], 4.0 * EPS)
            dve.memset(ext[:, :, 0:HIST], 0.0).then_inc(ms_ready, 1)
            for c in range(KD):
                dve.wait_ge(x_T, c + 1)
                dve.tensor_copy(x[:, c, :], bank(c % 4)).then_inc(x_ready, 1)
            for rel in range(4):
                split_quad(0, 0, rel)
            dve.wait_ge(par_ready, 1)
            for l in range(DEPTH):
                normalise(3 * l, 4 * l, gain(0, l, 0))
                ffn(2 * l, 3 * l, gain(1, l, 0))
                normalise(3 * l + 1, 4 * l + 1, gain(2, l, 0))
                mixer(l, 3 * l + 1, gain(3, l, 0))
                normalise(3 * l + 2, 4 * l + 3, gain(4, l, 0))
                dve.wait_ge(lo_ready, ffn_unit(2 * l + 1) + 4)
                ffn(2 * l + 1, 3 * l + 2, gain(5, l, 0))

        @block.gpsimd
        def _(pool):
            def split_lo(unit, raw_slot, split_slot, half):
                pool.wait_ge(hi_ready, unit + 1)
                cols = slice(half * P, (half + 1) * P)
                pool.tensor_tensor(wlo[:, split_slot, :, :], raw[:, raw_slot, :, cols],
                                   whi[:, split_slot, :, :].bitcast(F32), ALU.subtract).then_inc(lo_ready, 1)

            def step(u0, i):
                for rel in range(4):
                    split_lo(u0 + 4 * i + rel, rel // 2, rel, rel % 2)

            for m in range(DEPTH):
                u = mix_unit(m)
                pool.wait_ge(x_ready, 8 * (3 * m + 1) + 8)
                w_in = ins["w_in"][m].rearrange("(k p) n -> p k n", p=P)
                for d, (c0, n) in ((0, (KI_COL, HD)), (HD, (KI_COL, HD)), (2 * HD, (KI_COL + HD, HEADS))):
                    with nc.allow_non_contiguous_dma(reason="8 head-weight columns"):
                        pool.dma_start(wtail[:, :, d:d + n], w_in[:, :, c0:c0 + n]).then_inc(tail_in, 16)
                kix = ins["cache_kidx"][m, 0].rearrange("(j p) d -> p j d", p=P)
                pool.dma_start(kidx[:, :, 0:HD], kix).then_inc(kidx_in, 16)
                pool.dma_start(kidx[:, :, HD:2 * HD], kix).then_inc(kidx_in, 16)
                pool.dma_start(kc[:], ins["cache_k"][m, 0].rearrange("(j p) h d -> p j (h d)", p=P)).then_inc(kc_in, 16)
                pool.dma_start(vc[:], ins["cache_v"][m, 0].rearrange("(j p) h d -> p j (h d)", p=P)).then_inc(vc_in, 16)
                pool.dma_start(statein[:], ins["state_conv"][m, 0]).then_inc(state_in, 16)
                pool.wait_ge(tail_hi, m + 1)
                pool.tensor_tensor(wtlo[:], wtail[:], wthi[:].bitcast(F32), ALU.subtract).then_inc(tail_lo, 1)
                pool.wait_ge(lo_ready, u + 4)
                step(u + 4, 0)
                with pool.Fori(1, 3) as i:
                    step(u + 4, i)
                pool.wait_ge(sig_ready, m + 1)
                if m:
                    pool.wait_ge(crow_T, 2 * m)
                pa = proj[:, A * T:G * T].rearrange("p (c t) -> p c t", c=CT)
                pg = proj[:, G * T:Q * T].rearrange("p (c t) -> p c t", c=CT)
                pool.tensor_tensor(ext[:, :, HIST:HIST + SEQ], pa[:, :, 0:SEQ], pg[:, :, 0:SEQ], ALU.mult)
                pool.tensor_tensor(ext[:, :, EXT - DEC:EXT], pa[:, :, SEQ:T], pg[:, :, SEQ:T],
                                   ALU.mult).then_inc(u_ready, 1)
                with pool.Fori(3, 6) as i:
                    step(u + 4, i)
                pool.wait_ge(crow_ready, 2 * m + 2)
                pool.dma_start(prompt_conv[m, 0], crow[:, 0, :]).then_inc(rows_out, 16)
                pool.dma_start(sample_conv[m, 0], crow[:, 1, :]).then_inc(rows_out, 16)
                for ready, need, buf, pr, sa in ((vrow_ready, 3 * m + 3, vrow, prompt_v, sample_v),
                                                 (krow_ready, 4 * m + 4, krow, prompt_k, sample_k)):
                    pool.wait_ge(ready, need)
                    pool.dma_start(pr[m, 0].rearrange("(j p) h d -> p j (h d)", p=P), buf[:, 0:2, :]).then_inc(rows_out, 16)
                    pool.dma_start(sa[m, 0].rearrange("p h d -> p (h d)"), buf[0:DEC, 2, :]).then_inc(rows_out, 16)
                pool.dma_start(prompt_ki[m, 0].rearrange("(j p) d -> p j d", p=P), kirow[:, 0:2, :]).then_inc(rows_out, 16)
                pool.dma_start(sample_ki[m, 0], kirow[0:DEC, 2, :]).then_inc(rows_out, 16)
                for i in range(2):
                    step(u + U_IN + 4, i)
            pool.wait_ge(rows_out, 16 * 8 * DEPTH)

        @block.tensor
        def _(pe):
            def triple(out, slot, k, hi, lo, start, stop):
                pe.matmul(out, wlo[:, slot, k, :], hi, start=start, stop=False)
                pe.matmul(out, whi[:, slot, k, :], lo, start=False, stop=False)
                return pe.matmul(out, whi[:, slot, k, :], hi, start=False, stop=stop)

            def squares(s):
                for c in range(KD):
                    pe.wait_ge(sq_ready, 8 * s + c + 1)
                    pe.matmul(bank(6), ones[:], sq[:, c % 2, :], start=(c == 0), stop=(c == KD - 1)).then_inc(sq_used, 1)

            def first_step(u0, hq):
                pe.wait_ge(lo_ready, u0 + 4)
                for k in range(KD):
                    pe.wait_ge(hl_ready, 8 * hq + k + 1)
                    for rel in range(4):
                        last = triple(bank(rel), rel, k, hh[:, k, :], hl[:, k, :], k == 0, k == KD - 1)
                        if k == KD - 1:
                            last.then_inc(w_used, 1)

            def up_step(f, i):
                u = ffn_unit(f)
                for rel in range(4):
                    pe.wait_ge(lo_ready, u + 4 * i + rel + 1)
                    pe.wait_ge(silu_ready if rel < 2 else gt_ready, KF * f + 2 * i + rel % 2 - 1)
                    for k in range(KD):
                        last = triple(bank(rel), rel, k, hh[:, k, :], hl[:, k, :], k == 0, k == KD - 1)
                    last.then_inc(w_used, 1)

            def down_step(f, s, i, first):
                ud = ffn_unit(f) + U_UP
                for d in range(2):
                    for part in range(3):
                        for col in range(2):
                            j = 6 * d + 2 * part + col
                            pe.wait_ge(lo_ready, ud + 12 * i + j + 1)
                            if part == 0:
                                if first:
                                    pe.wait_ge(silu_ready if d == 0 else gt_ready, KF * f + KF)
                                else:
                                    pe.wait_ge(ysq_ready, 8 * s + 4 * i + 2 * d + col - 3)
                            if first and d == 0 and col == 0:
                                pe.wait_ge(glo_ready, KF * f + 8 * part + PARTS[part])
                            for k in range(PARTS[part]):
                                kk = 8 * part + k
                                last = triple(bank(2 * d + col), j % 4, k, ghi[:, kk * T:(kk + 1) * T],
                                              glo[:, kk * T:(kk + 1) * T], kk == 0, kk == KF - 1)
                            last.then_inc(w_used, 1)

            def ffn(f, s, hq):
                first_step(ffn_unit(f), hq)
                with pe.Fori(1, UP_STEPS) as i:
                    up_step(f, i)
                down_step(f, s, 0, True)
                down_step(f, s, 1, False)
                pe.wait_ge(acc_ready, 10 * s + 10)
                pe.matmul(bank(6), ones[:], acc[:], start=True, stop=True).then_inc(ss_done, 1)

            def mixer(m, s, hq):
                u = mix_unit(m)
                first_step(u, hq)
                pe.wait_ge(tail_lo, m + 1)
                for b, c0, n in ((4, 0, P), (5, P, HEADS)):
                    for k in range(KD):
                        o = bank(b, slice(0, n))
                        pe.matmul(o, wtlo[:, k, c0:c0 + n], hh[:, k, :], start=(k == 0), stop=False)
                        pe.matmul(o, wthi[:, k, c0:c0 + n], hl[:, k, :], start=False, stop=False)
                        last = pe.matmul(o, wthi[:, k, c0:c0 + n], hh[:, k, :], start=False, stop=(k == KD - 1))
                    last.then_inc(tail_done, 1)
                for k in range(5):
                    if k < 4:
                        pe.wait_ge(proj_saved, 24 * m + k + 1)
                        src = proj[:, (QI + k) * T:(QI + k + 1) * T]
                    else:
                        pe.wait_ge(tail_saved, 2 * m + 1)
                        src = kiT[:]
                    if k >= 2:
                        pe.wait_ge(rope_done, 13 * m + k - 1)
                    pe.matmul(bank(6 + k % 2), swap[:], src, start=True, stop=True).then_inc(rope_mm, 1)
                pe.wait_ge(tail_saved, 2 * m + 2)
                for tt, (t0, n) in enumerate(TOK):
                    last = pe.transpose(bank(4, slice(0, n), 8 * tt, 8), wiT[:, t0:t0 + n], ident[0:HEADS, 0:HEADS])
                last.then_inc(wi_T, 1)
                pe.wait_ge(kidx_in, 32 * (m + 1))
                for j in range(4):
                    last = pe.transpose(bank(5, n=P, lo=P * j), kidx[:, j, :], ident[:])
                last.then_inc(kidx_T, 1)
                pe.wait_ge(rope_done, 13 * m + 5)
                pe.wait_ge(kiTs_ready, m + 1)
                for h in range(HEADS):
                    r = slice((h % 2) * HD, (h % 2 + 1) * HD)
                    q0 = (QI + h // 2) * T
                    if h >= 2:
                        pe.wait_ge(rel_ready, 8 * m + h - 1)
                    b, sbk = 6 + h % 2, 2 * (h % 2)
                    pe.matmul(bank(b, n=P), proj[r, q0:q0 + P], kiT[r, 0:P], start=True, stop=True)
                    pe.matmul(bank(b, lo=P, n=SEQ), proj[r, q0 + P:q0 + SEQ], kiT[r, 0:SEQ], start=True, stop=True)
                    pe.matmul(bank(sbk, slice(0, DEC), n=PAST), proj[r, q0 + SEQ:q0 + T], kiTs[r, 0:PAST],
                              start=True, stop=True)
                    pe.matmul(bank(sbk + 1, slice(0, DEC), n=DEC), proj[r, q0 + SEQ:q0 + T], kiTs[r, PAST:SKEYS],
                              start=True, stop=True).then_inc(lg_done, 1)
                pe.wait_ge(rel_ready, 8 * m + 8)
                with pe.Fori(1, 6) as i:
                    for rel in range(4):
                        pe.wait_ge(lo_ready, u + 4 * i + rel + 1)
                        pe.wait_ge(proj_saved, 24 * m + 4 * i + rel - 3)
                        for k in range(KD):
                            last = triple(bank(rel), rel, k, hh[:, k, :], hl[:, k, :], k == 0, k == KD - 1)
                        last.then_inc(w_used, 1)
                pe.wait_ge(state_in, 16 * (m + 1))
                for ct in range(CT):
                    last = pe.transpose(bank(7, lo=HIST * ct, n=HIST), statein[:, ct * P:(ct + 1) * P],
                                        ident[0:HIST, 0:HIST])
                last.then_inc(st_T, 1)
                pe.wait_ge(u_ready, m + 1)
                pe.wait_ge(st_ready, m + 1)
                pe.wait_ge(proj_saved, 24 * m + 24)
                for g, c0 in enumerate((SEQ, EXT - HIST)):
                    for ct in range(CT):
                        last = pe.transpose(bank(2 + g, slice(0, HIST), ct * P, P), ext[:, ct, c0:c0 + HIST], ident[:])
                    last.then_inc(crow_T, 1)
                for tt, (t0, n) in enumerate(TOK):
                    for c in range(4):
                        o = (V + c) * T + t0
                        last = pe.transpose(bank(4 + tt, slice(0, n), c * P, P), proj[:, o:o + n], ident[:])
                    last.then_inc(vrow_T, 1)
                pe.wait_ge(kc_in, 16 * (m + 1))
                for hp in range(4):
                    if hp < 2:
                        pe.wait_ge(crow_ready, 2 * m + hp + 1)
                    else:
                        pe.wait_ge(kTs_ready, 8 * m + hp - 1)
                    for j in range(4):
                        last = pe.transpose(bank(2 + hp % 2, lo=j * P, n=P), kc[:, j, hp * P:(hp + 1) * P], ident[:])
                    last.then_inc(kcT_done, 1)
                for k in range(5, 13):
                    if k >= 7:
                        pe.wait_ge(rope_done, 13 * m + k - 1)
                    pe.matmul(bank(k % 2), swap[:], proj[:, (Q + k - 5) * T:(Q + k - 4) * T], start=True,
                              stop=True).then_inc(rope_mm, 1)
                pe.wait_ge(rope_done, 13 * m + 13)
                pe.wait_ge(kTs_ready, 8 * m + 4)
                for tt, (t0, n) in enumerate(TOK):
                    pe.wait_ge(vrow_ready, 3 * m + tt + 1)
                    for c in range(4):
                        o = (K + c) * T + t0
                        last = pe.transpose(bank(4 + tt, slice(0, n), c * P, P), proj[:, o:o + n], ident[:])
                    last.then_inc(krow_T, 1)
                for tt, (t0, n) in enumerate(TOK):
                    last = pe.transpose(bank(7, slice(0, n), HD * tt, HD), kiT[0:HD, t0:t0 + n], ident[0:HD, 0:HD])
                last.then_inc(krow_T, 1)
                pe.wait_ge(krow_ready, 4 * m + 4)
                pe.wait_ge(conv_ready, (m + 1) * TAPS * CT)
                for ct in range(CT):
                    last = pe.matmul(bank(7, n=CO), ones[:], yc[:, ct, :], start=(ct == 0), stop=(ct == CT - 1))
                last.then_inc(mu_done, 1)
                for ct in range(CT):
                    pe.wait_ge(csq_ready, 4 * m + ct + 1)
                    if ct == 0:
                        pe.wait_ge(dev_ready, 4 * m + 4)
                    pe.matmul(bank(7, n=CO), ones[:], y[:, (ct % 2) * CO:(ct % 2 + 1) * CO], start=(ct == 0),
                              stop=(ct == CT - 1)).then_inc(csq_used, 1)

                def logits(n):
                    if n >= 2:
                        pe.wait_ge(max_ready, 10 * m + n - 1)
                    b = 2 * (n % 2)
                    if n < 2:
                        for j in range(4):
                            h = 4 * n + j
                            r = slice((h % 2) * HD, (h % 2 + 1) * HD)
                            o = slice(32 * j, 32 * j + 32)
                            q = proj[r, (Q + h // 2) * T + SEQ:(Q + h // 2 + 1) * T]
                            pe.matmul(bank(b, o, n=PAST), q, kTs[r, h // 2, 0:PAST], start=True, stop=True)
                            last = pe.matmul(bank(b + 1, o, n=DEC), q, kTs[r, h // 2, PAST:SKEYS], start=True, stop=True)
                    else:
                        h = n - 2
                        r = slice((h % 2) * HD, (h % 2 + 1) * HD)
                        q0, k0 = (Q + h // 2) * T, (K + h // 2) * T
                        pe.matmul(bank(b, n=P), proj[r, q0:q0 + P], proj[r, k0:k0 + P], start=True, stop=True)
                        last = pe.matmul(bank(b, lo=P, n=SEQ), proj[r, q0 + P:q0 + SEQ], proj[r, k0:k0 + SEQ],
                                         start=True, stop=True)
                    last.then_inc(s_done, 1)

                def turn(n):
                    pe.wait_ge(p_ready, 10 * m + n + 1)
                    if n >= 1:
                        pe.wait_ge(pT_ready, 10 * m + n)
                    if n < 2:
                        for j in range(4):
                            pe.transpose(bank(4, lo=j * P, n=P), prob[:, n % 2, j * P:(j + 1) * P], ident[:])
                        last = pe.transpose(bank(5, slice(0, DEC), n=P), prob[:, n % 2, PAST:SKEYS], ident[:])
                    else:
                        for j in range(3):
                            last = pe.transpose(bank(4 + n % 2, lo=j * P, n=P), prob[:, n % 2, j * P:(j + 1) * P], ident[:])
                    last.then_inc(pT_done, 1)

                def values(n):
                    pe.wait_ge(pT_ready, 10 * m + n + 1)
                    if n < 2:
                        pe.wait_ge(vc_in, 16 * (m + 1))
                        if n == 0:
                            pe.wait_ge(croot_ready, m + 1)
                        for j4 in range(4):
                            h = 4 * n + j4
                            r = slice((h % 2) * HD, (h % 2 + 1) * HD)
                            o = bank(7, r, 32 * (h // 2), DEC)
                            hc = slice(h * HD, (h + 1) * HD)
                            for j in range(4):
                                pe.matmul(o, vc[:, j, hc], probT[:, n % 2, j * P + 32 * j4:j * P + 32 * j4 + 32],
                                          start=(j == 0), stop=False)
                            last = pe.matmul(o, vrow[0:DEC, 2, hc], probT[0:DEC, n % 2, 512 + 32 * j4:544 + 32 * j4],
                                             start=False, stop=True)
                    else:
                        h = n - 2
                        hp = h // 2
                        if h % 2 == 0:
                            pe.wait_ge(att_saved, 5 * m + max(hp, 1))
                        r = slice((h % 2) * HD, (h % 2 + 1) * HD)
                        hc = slice(h * HD, (h + 1) * HD)
                        b = 6 + hp % 2
                        pe.matmul(bank(b, r, n=P), vrow[:, 0, hc], probT[:, n % 2, 0:P], start=True, stop=True)
                        pe.matmul(bank(b, r, P, P), vrow[:, 0, hc], probT[:, n % 2, P:2 * P], start=True, stop=False)
                        last = pe.matmul(bank(b, r, P, P), vrow[:, 1, hc], probT[:, n % 2, 2 * P:3 * P],
                                         start=False, stop=True)
                    last.then_inc(pv_done, 1)

                logits(0)
                logits(1)
                for n in range(10):
                    turn(n)
                    if n < 8:
                        logits(n + 2)
                    if n >= 1:
                        values(n - 1)
                values(9)
                uo = u + U_IN
                first_step(uo, 4 * m + 2)
                for rel in range(4):
                    pe.wait_ge(lo_ready, uo + 4 + rel + 1)
                    pe.wait_ge(ysq_ready, 8 * s + rel + 1)
                    for k in range(KD):
                        last = triple(bank(rel), rel, k, hh[:, k, :], hl[:, k, :], k == 0, k == KD - 1)
                    last.then_inc(w_used, 1)
                pe.wait_ge(acc_ready, 10 * s + 10)
                pe.matmul(bank(6), ones[:], acc[:], start=True, stop=True).then_inc(ss_done, 1)

            pe.wait_ge(const_in, 16 * 4)
            pe.wait_ge(par_in, 16 * 10)
            pe.transpose(bank(7, n=120), prow[:], ident[0:120, 0:120])
            for j in range(DEPTH * CT):
                last = pe.transpose(bank(5, lo=TAPS * j, n=TAPS), trow[:, j * P:(j + 1) * P], ident[0:TAPS, 0:TAPS])
            last.then_inc(par_T, 1)
            pe.wait_ge(x_in, 32)
            for c in range(KD):
                if c >= 4:
                    pe.wait_ge(x_ready, c - 3)
                for tt, (t0, n) in enumerate(TOK):
                    last = pe.transpose(bank(c % 4, lo=t0, n=n), xrow[0:n, tt, c * P:(c + 1) * P], ident[0:n, 0:n])
                last.then_inc(x_T, 1)
            pe.wait_ge(ms_ready, 1)
            pe.wait_ge(par_ready, 1)
            for l in range(DEPTH):
                squares(3 * l)
                ffn(2 * l, 3 * l, 4 * l)
                squares(3 * l + 1)
                mixer(l, 3 * l + 1, 4 * l + 1)
                squares(3 * l + 2)
                ffn(2 * l + 1, 3 * l + 2, 4 * l + 3)
            pe.wait_ge(x_ready, 8 * 6 + 8)
            for n in range(6):
                tt, half = divmod(n, 2)
                t0, k = TOK[tt]
                for c in range(4):
                    last = pe.transpose(bank(n, slice(0, k), c * P, P), x[:, 4 * half + c, t0:t0 + k], ident[:])
                last.then_inc(yT_done, 1)


_INS = ["x_prompt", "x_sample", "cache_k", "cache_v", "cache_kidx", "state_conv", "ffn1_norm_pre",
        "ffn1_norm_post", "ffn1_w_up", "ffn1_w_down", "mix_norm_pre", "mix_norm_post", "w_in", "conv_w", "conv_b",
        "conv_ln_g", "conv_ln_b", "w_out", "ffn2_norm_pre", "ffn2_norm_post", "ffn2_w_up", "ffn2_w_down"]
_OUTS = [(1, SEQ, D), (1, DEC, D), (DEPTH, 1, SEQ, HEADS, HD), (DEPTH, 1, SEQ, HEADS, HD), (DEPTH, 1, SEQ, HD),
         (DEPTH, 1, HIST, CC), (DEPTH, 1, DEC, HEADS, HD), (DEPTH, 1, DEC, HEADS, HD), (DEPTH, 1, DEC, HD),
         (DEPTH, 1, HIST, CC)]


def shape_constants():
    f = np.float32
    pos = np.concatenate([np.arange(SEQ), PAST + np.arange(DEC)]).astype(f)
    inv = (f(1.0) / (f(THETA) ** (np.arange(0, HD, 2).astype(f) / f(HD)))).astype(f)
    angle = (pos[:, None] * inv[None, :]).astype(f)
    half = np.arange(P) % (HD // 2)
    swap = np.zeros((P, P), f)
    for j in range(P):
        if j % HD < HD // 2:
            swap[j + HD // 2, j] = -1.0
        else:
            swap[j - HD // 2, j] = 1.0
    return {"ident": np.eye(P, dtype=f), "swap": swap,
            "cosT": np.ascontiguousarray(np.cos(angle).astype(f)[:, half].T),
            "sinT": np.ascontiguousarray(np.sin(angle).astype(f)[:, half].T)}


def kernel(**inputs):
    import concourse.bacc as _bacc
    from concourse.bass_utils import run_bass_kernel_spmd as _run

    nc = _bacc.Bacc("TRN2", target_bir_lowering=False, num_devices=1)
    arrays, ins, consts = {}, {}, {}
    for name in _INS:
        a = np.ascontiguousarray(inputs[name])
        arrays[f"in_{name}"] = a
        ins[name] = nc.dram_tensor(f"in_{name}", a.shape, mybir.dt.from_np(a.dtype), kind="ExternalInput").ap()
    for name, a in shape_constants().items():
        arrays[f"const_{name}"] = a
        consts[name] = nc.dram_tensor(f"const_{name}", a.shape, F32, kind="ExternalInput").ap()
    outs = [nc.dram_tensor(f"out_{i}", shape, F32, kind="ExternalOutput").ap() for i, shape in enumerate(_OUTS)]
    build(nc, ins, consts, outs)
    r = _run(nc, [arrays], core_ids=[0])
    return tuple(r.results[0][f"out_{i}"] for i in range(len(_OUTS)))
```

```python
from contextlib import ExitStack

import numpy as np

import concourse.bass as bass
from concourse import mybir

F32 = mybir.dt.float32
F32R = mybir.dt.float32r
ALU = mybir.AluOpType
ACT = mybir.ActivationFunctionType
AX_X = mybir.AxisListType.X

P = 128
D = 1024
SEQ = 256
DEC = 32
T = SEQ + DEC
PAST = 512
SKEYS = PAST + DEC
DEPTH = 2
DFF = 2816
KD = D // P
KF = DFF // P
CC = 512
CT = CC // P
TAPS = 31
HIST = TAPS - 1
HEADS = 8
HD = 64
CHUNK = 64
THETA = 10000.0
TOPK_P = min(256, SEQ // 4)
TOPK_S = min(256, SKEYS // 4)
EPS = 1e-6
STRIP = 256
NEG = -1.0e30
BARRED = -1.0e38
TAKEN = -3.0e38
TOK = [(0, 128), (128, 128), (256, 32)]

UP_STEPS = DFF // STRIP
QI_COL = 5 * CC
KI_COL = QI_COL + CC
WIDX = 2 * HD + HEADS
EXT = HIST + SEQ + HIST + DEC
CO = EXT - HIST
SAMPLE_AT = SEQ + HIST
U_UP, U_DOWN, U_IN, U_OUT = 4 * UP_STEPS, 24, 24, 8
U_LAYER = 2 * (U_UP + U_DOWN) + U_IN + U_OUT
CV = CT - 1
CONV_FIRST = 12
CONV_EARLY = 30
CONV_ITEM = 10
MERGED = 5
PARTS = (8, 8, 6)
QI, A, G, Q, K, V = 0, 4, 8, 12, 16, 20


def ffn_unit(f):
    return (f // 2) * U_LAYER + (f % 2) * (U_UP + U_DOWN + U_IN + U_OUT)


def mix_unit(m):
    return m * U_LAYER + U_UP + U_DOWN


def gain(n, l, c):
    return (n * DEPTH + l) * KD + c


def cvec(n, l, ct):
    return 6 * DEPTH * KD + (n * DEPTH + l) * CT + ct


def build(nc, ins, consts, outs):
    (y_prompt, y_sample, prompt_k, prompt_v, prompt_ki, prompt_conv,
     sample_k, sample_v, sample_ki, sample_conv) = outs
    with ExitStack() as ctx:
        BASE = (nc.sbuf_base + 31) // 32 * 32
        SIZE = nc.sbuf_usable_end - BASE
        ctx.enter_context(nc.sbuf_tensor("arena", [P, (SIZE - 64) // 4], F32))
        at = [0]

        def sb(name, shape, dt=F32):
            size = int(np.prod(shape[1:])) * 4
            t = nc.alloc_sbuf_tensor_at(name, list(shape), dt, offset=BASE + at[0])
            at[0] += (size + 31) // 32 * 32
            assert at[0] <= SIZE - 64, (name, at[0])
            return t

        def sem(name):
            return ctx.enter_context(nc.semaphore(name))

        raw = sb("raw", [P, 2, 8, STRIP])
        whi = sb("whi", [P, 4, 8, P], F32R)
        wlo = sb("wlo", [P, 4, 8, P], F32R)
        x = sb("x", [P, KD, T])
        hh = sb("hh", [P, KD, T], F32R)
        hl = sb("hl", [P, KD, T], F32R)
        y = sb("y", [P, KD * T])
        cinv = sb("cinv", [P, CO])
        accx = sb("accx", [P, T])
        sq = sb("sq", [P, 2, T])
        ysq = sb("ysq", [P, 2 * T])
        acc = sb("acc", [P, T])
        root = sb("root", [P, T])
        rinv = sb("rinv", [P, T])
        shared_a = at[0]
        upd = sb("upd", [P, 2 * T])
        tail_at = at[0]
        sil = sb("sil", [P, 2 * T])
        gt = sb("gt", [P, 2 * T])
        g_at = at[0]
        ghi = sb("ghi", [P, KF * T], F32R)
        glo = sb("glo", [P, KF * T], F32R)
        g_end = at[0]
        proj_at = at[0]
        proj = sb("proj", [P, 24 * T])
        ident = sb("ident", [P, P])
        ones = sb("ones", [P, P])
        swap = sb("swap", [P, P])
        cosT = sb("cosT", [P, T])
        sinT = sb("sinT", [P, T])
        par = sb("par", [P, 120])
        taps = sb("taps", [P, DEPTH * CT * TAPS])
        ext = sb("ext", [P, CT, EXT])
        kiT = sb("kiT", [P, T])
        wiT = sb("wiT", [HEADS, T])
        wrow = sb("wrow", [P, 3 * HEADS])
        rtok = sb("rtok", [P, 3])
        wS = sb("wS", [P, 2])
        wdiag = sb("wdiag", [P, 2, DEC])
        stack = sb("stack", [P, DEC])
        score = sb("score", [P, 928])
        m8 = sb("m8", [P, 8])
        epsc = sb("epsc", [P, 2])
        stat = sb("stat", [P, 10 * 8])
        statein = sb("statein", [HIST, CC])
        cosR = sb("cosR", [P, T])
        sinR = sb("sinR", [P, T])
        at[0] = g_at
        wthi = sb("wthi", [P, KD, WIDX], F32R)
        wtlo = sb("wtlo", [P, KD, WIDX], F32R)
        rel_at = at[0]
        relP = sb("relP", [P, 2, 384])
        relS = sb("relS", [P, 2, SKEYS])
        kidx_at = at[0]
        kidx = sb("kidx", [P, 4, 2 * HD])
        kiTs = sb("kiTs", [P, SKEYS])
        ropa = sb("ropa", [P, T])
        ropb = sb("ropb", [P, T])
        kc_at = at[0]
        kc = sb("kc", [P, 4, CC])
        vc = sb("vc", [P, 4, CC])
        vrow = sb("vrow", [P, 3, CC])
        kirow = sb("kirow", [P, 3, HD])
        assert at[0] <= g_end, at[0] - g_end
        at[0] = g_at
        kTs = sb("kTs", [P, 4, SKEYS])
        at[0] = rel_at
        prob = sb("prob", [P, 2, SKEYS])
        maskS = sb("maskS", [P, SKEYS])
        at[0] = kidx_at
        prod = sb("prod", [P, 3, CO])
        assert at[0] <= kc_at
        at[0] = kc_at
        krow = sb("krow", [P, 3, CC])
        at[0] = tail_at
        wtail = sb("wtail", [P, KD, WIDX])
        assert at[0] <= g_at
        at[0] = shared_a
        probT = sb("probT", [P, 2, 640])
        at[0] = proj_at + A * T * 4
        yc = sb("yc", [P, CT, CO])
        crow = sb("crow", [HIST, 2, CC])
        assert at[0] <= proj_at + Q * T * 4
        at[0] = g_at
        xrow = sb("xrow", [P, 3, D])
        prow = sb("prow", [120, P])
        trow = sb("trow", [TAPS, DEPTH * CC])
        ps = ctx.enter_context(nc.psum_tensor("ps", [P, 8 * 512], F32))

        def bank(b, rows=slice(0, P), lo=0, n=T):
            return ps[rows, 512 * b + lo:512 * b + lo + n]

        const_in = sem("const_in")
        x_in = sem("x_in")
        par_in = sem("par_in")
        par_T = sem("par_T")
        par_ready = sem("par_ready")
        x_T = sem("x_T")
        loaded = [sem("loaded0"), sem("loaded1")]
        hi_ready = sem("hi_ready")
        lo_ready = sem("lo_ready")
        w_used = sem("w_used")
        x_ready = sem("x_ready")
        sq_ready = sem("sq_ready")
        accx_ready = sem("accx_ready")
        sx_done = sem("sx_done")
        root_ready = sem("root_ready")
        r_ready = sem("r_ready")
        hh_ready = sem("hh_ready")
        hl_ready = sem("hl_ready")
        gr_ready = sem("gr_ready")
        silu_ready = sem("silu_ready")
        up_ready = sem("up_ready")
        gt_ready = sem("gt_ready")
        ghi_ready = sem("ghi_ready")
        glo_ready = sem("glo_ready")
        ysq_ready = sem("ysq_ready")
        y_saved = sem("y_saved")
        acc_ready = sem("acc_ready")
        ss_done = sem("ss_done")
        proj_saved = sem("proj_saved")
        tail_in = sem("tail_in")
        tail_hi = sem("tail_hi")
        tail_lo = sem("tail_lo")
        tail_done = sem("tail_done")
        tail_saved = sem("tail_saved")
        kidx_in = sem("kidx_in")
        kc_in = sem("kc_in")
        vc_in = sem("vc_in")
        state_in = sem("state_in")
        rope_mm = sem("rope_mm")
        rope_done = sem("rope_done")
        wi_T = sem("wi_T")
        wrow_ready = sem("wrow_ready")
        relS_ready = sem("relS_ready")
        scoreS_done = sem("scoreS_done")
        kidx_T = sem("kidx_T")
        kiTs_ready = sem("kiTs_ready")
        lgS_done = sem("lgS_done")
        scoreS_saved = sem("scoreS_saved")
        lg_done = sem("lg_done")
        rel_ready = sem("rel_ready")
        rel_used = sem("rel_used")
        mask_ready = sem("mask_ready")
        glu_r = sem("glu_r")
        sig_ready = sem("sig_ready")
        u_ready = sem("u_ready")
        st_T = sem("st_T")
        st_ready = sem("st_ready")
        crow_T = sem("crow_T")
        crow_ready = sem("crow_ready")
        conv_ready = sem("conv_ready")
        prod_ready = sem("prod_ready")
        pconv_ready = sem("pconv_ready")
        mu_done = sem("mu_done")
        dev_ready = sem("dev_ready")
        csq_ready = sem("csq_ready")
        csq_used = sem("csq_used")
        croot_ready = sem("croot_ready")
        cn_ready = sem("cn_ready")
        cmix_ready = sem("cmix_ready")
        vrow_T = sem("vrow_T")
        vrow_ready = sem("vrow_ready")
        kcT_done = sem("kcT_done")
        kTs_ready = sem("kTs_ready")
        krow_T = sem("krow_T")
        krow_ready = sem("krow_ready")
        s_done = sem("s_done")
        max_ready = sem("max_ready")
        exp_ready = sem("exp_ready")
        p_ready = sem("p_ready")
        pT_done = sem("pT_done")
        pT_ready = sem("pT_ready")
        pv_done = sem("pv_done")
        att_saved = sem("att_saved")
        rows_out = sem("rows_out")
        yT_done = sem("yT_done")
        yrow_ready = sem("yrow_ready")
        y_out = sem("y_out")
        dve_chain = sem("dve_chain")
        act_chain = sem("act_chain")
        ms_ready = sem("ms_ready")

        w_of = {0: ("ffn1_w_up", "ffn1_w_down"), 1: ("ffn2_w_up", "ffn2_w_down")}

        def strip_view(w, l, r0, rows, c0):
            return ins[w][l, r0:r0 + rows, :].rearrange("(k p) n -> p k n", p=P)[:, :, bass.ds(c0, STRIP)]

        block = ctx.enter_context(nc.Block())

        @block.sync
        def _(sp):
            def load(q, wait, src, n=8):
                if wait is not None:
                    sp.wait_ge(lo_ready, wait)
                sp.dma_start(raw[:, q, 0:n, :], src).then_inc(loaded[q], 16)

            def up_step(f, i, free=True):
                w = w_of[f % 2][0]
                u = ffn_unit(f)
                load(0, u + 4 * i - 2 if free else None, strip_view(w, f // 2, 0, D, i * STRIP))
                load(1, u + 4 * i if free else None, strip_view(w, f // 2, 0, D, i * STRIP + DFF))

            def down_step(f, i):
                w = w_of[f % 2][1]
                u = ffn_unit(f) + U_UP
                for r in range(6):
                    d, part = divmod(r, 3)
                    load(r % 2, u + 12 * i + 2 * r - 2,
                         strip_view(w, f // 2, part * 8 * P, PARTS[part] * P, (2 * i + d) * STRIP), PARTS[part])

            def in_step(m, i, c0):
                u = mix_unit(m)
                load(0, u + 4 * i - 2, strip_view("w_in", m, 0, D, c0))
                load(1, u + 4 * i, strip_view("w_in", m, 0, D, c0 + STRIP))

            for f in range(2 * DEPTH):
                if f == 0:
                    sp.dma_start(raw[:, 0], strip_view("ffn1_w_up", 0, 0, D, 0)).then_inc(loaded[0], 16)
                    sp.dma_start(raw[:, 1], strip_view("ffn1_w_up", 0, 0, D, DFF)).then_inc(loaded[1], 16)
                else:
                    up_step(f, 0)
                with sp.Fori(1, UP_STEPS) as i:
                    up_step(f, i)
                with sp.Fori(0, 2) as i:
                    down_step(f, i)
                if f % 2 == 0:
                    m = f // 2
                    in_step(m, 0, QI_COL)
                    with sp.Fori(1, 6) as i:
                        in_step(m, i, (i - 1) * 2 * STRIP)
                    u = mix_unit(m) + U_IN
                    for i in range(2):
                        for q in range(2):
                            load(q, u + 4 * i + 2 * q - 2, strip_view("w_out", m, 0, D, (2 * i + q) * STRIP))
            for tt, (t0, n) in enumerate(TOK):
                sp.wait_ge(yrow_ready, 2 * tt + 2)
                dst = y_prompt[0, t0:t0 + n, :] if tt < 2 else y_sample[0]
                sp.dma_start(dst, xrow[0:n, tt, :]).then_inc(y_out, 16)
            sp.wait_ge(y_out, 48)

        @block.scalar
        def _(act):
            n_chain = [0]

            def link(ins_):
                n_chain[0] += 1
                ins_.then_inc(act_chain, 1)
                act.wait_ge(act_chain, n_chain[0])

            def split_hi(unit, raw_slot, split_slot, half, raw_count, n=8, old=True):
                act.wait_ge(loaded[raw_slot], 16 * raw_count)
                if old:
                    act.wait_ge(w_used, unit - 3)
                act.activation(whi[:, split_slot, 0:n, :], raw[:, raw_slot, 0:n, half * P:(half + 1) * P],
                               ACT.Copy).then_inc(hi_ready, 1)

            def split_quad(u0, i, rel, down_raw=None, old=True):
                q, half = divmod(rel, 2)
                split_hi(u0 + 4 * i + rel, q, rel, half, u0 // 4 + i + 1, 8, old)

            def split_x(s, hq, g):
                for c in range(KD):
                    act.wait_ge(x_ready, 8 * s + c + 1)
                    act.activation(hh[:, c, :], x[:, c, :], ACT.Copy, scale=par[:, g + c:g + c + 1]).then_inc(hh_ready, 1)
                    if c >= 2:
                        act.wait_ge(accx_ready, 10 * s + c + 1)
                    act.activation(sq[:, c % 2, :], x[:, c, :], ACT.Square).then_inc(sq_ready, 1)

            def pre_root(s):
                act.wait_ge(sx_done, s + 1)
                act.activation(root[:], bank(6), ACT.Sqrt, bias=epsc[:, 0:1], scale=1.0 / D).then_inc(root_ready, 1)

            def post_root(s, half_step):
                k = 4.0 if half_step else 1.0
                act.wait_ge(ss_done, s + 1)
                act.activation(root[:], bank(6), ACT.Sqrt, bias=epsc[:, 1:2] if half_step else epsc[:, 0:1],
                               scale=k / D).then_inc(root_ready, 1)

            def save_y(s, c, b, slot, unit):
                act.wait_ge(w_used, unit + 1)
                act.wait_ge(acc_ready, 9 * s + c + 1)
                act.activation(ysq[:, slot * T:(slot + 1) * T], bank(b), ACT.Square).then_inc(ysq_ready, 1)
                act.activation(y[:, bass.ds(c * T, T)], bank(b), ACT.Copy).then_inc(y_saved, 1)

            def sqrt_table():
                link(act.activation(stat[:, 79:80], epsc[:, 0:1], ACT.Sqrt))

            def ffn(f, s):
                u = ffn_unit(f)

                def up_step(i, first):
                    if first:
                        split_quad(u + 4, i, 0)
                        split_quad(u + 4, i, 1)
                        pre_root(s)
                    for j in range(2):
                        act.wait_ge(gr_ready, KF * f + 2 * i + j + 1)
                        act.activation(sil[:, j * T:(j + 1) * T], sil[:, j * T:(j + 1) * T],
                                       ACT.Silu).then_inc(silu_ready, 1)
                        if not first:
                            split_quad(u + 4, i, j)
                    for j in range(2):
                        split_quad(u + 4, i, 2 + j)
                        act.wait_ge(gt_ready, KF * f + 2 * i + j + 1)
                        act.activation(ghi[:, bass.ds((2 * i + j) * T, T)], gt[:, j * T:(j + 1) * T],
                                       ACT.Copy).then_inc(ghi_ready, 1)

                up_step(0, True)
                with act.Fori(1, UP_STEPS) as i:
                    up_step(i, False)
                sqrt_table()
                ud = u + U_UP

                def ahead(i, j, last):
                    jj = j + 4
                    if jj < 12:
                        r, half = divmod(jj, 2)
                        split_hi(ud + 12 * i + jj, r % 2, jj % 4, half, ud // 4 + 3 * i + r // 2 + 1, PARTS[r % 3])
                    elif not last:
                        r, half = divmod(jj - 12, 2)
                        split_hi(ud + 12 * i + jj, r % 2, jj % 4, half, ud // 4 + 3 * i + 3 + r // 2 + 1, 8)

                def down_step(i, last):
                    for d in range(2):
                        for j in range(6):
                            if j >= 4:
                                save_y(s, 4 * i + 2 * d + j - 4, 2 * d + j - 4, j - 4, ud + 12 * i + 6 * d + j)
                            ahead(i, 6 * d + j, last)

                if f < 2 * DEPTH - 1:
                    with act.Fori(0, 2) as i:
                        down_step(i, False)
                else:
                    down_step(0, False)
                    down_step(1, True)
                post_root(s, True)

            def mixer(m, s):
                u = mix_unit(m)
                act.wait_ge(tail_in, 48 * (m + 1))
                act.activation(wthi[:], wtail[:], ACT.Copy).then_inc(tail_hi, 1)

                def in_step(i, first):
                    for j in range(4):
                        act.wait_ge(w_used, u + 4 * i + j + 1)
                        act.activation(proj[:, bass.ds((4 * i + j) * T, T)], bank(j), ACT.Copy).then_inc(proj_saved, 1)
                        split_quad(u + 4, i, j)
                        if first and j == 1:
                            pre_root(s)

                in_step(0, True)
                act.wait_ge(tail_done, 2 * m + 1)
                act.activation(kiT[:], bank(4), ACT.Copy).then_inc(tail_saved, 1)
                act.wait_ge(tail_done, 2 * m + 2)
                act.activation(wiT[:], bank(5, slice(0, HEADS)), ACT.Copy).then_inc(tail_saved, 1)
                act.wait_ge(kidx_T, m + 1)
                act.activation(kiTs[:, 0:PAST], bank(5, n=PAST), ACT.Copy).then_inc(kiTs_ready, 1)
                for hp in range(4):
                    act.wait_ge(kcT_done, 4 * m + hp + 1)
                    act.activation(kTs[:, hp, 0:PAST], bank(hp, n=PAST), ACT.Copy).then_inc(kTs_ready, 1)
                act.wait_ge(rope_done, 13 * m + 5)
                act.activation(kiTs[:, PAST:SKEYS], kiT[:, SEQ:T], ACT.Copy).then_inc(kiTs_ready, 1)
                for g in range(2):
                    act.wait_ge(lgS_done, 2 * m + g + 1)
                    act.activation(relS[:, g, :], bank(2 * g, n=SKEYS), ACT.Relu, scale=HD ** -0.5).then_inc(relS_ready, 1)
                for h in range(HEADS):
                    act.wait_ge(lg_done, 8 * m + h + 1)
                    if h >= 2:
                        act.wait_ge(rel_used, 8 * m + h - 1)
                    act.activation(relP[:, h % 2, :], bank(6 + h % 2, n=384), ACT.Relu,
                                   scale=HD ** -0.5).then_inc(rel_ready, 1)
                with act.Fori(1, 4) as i:
                    in_step(i, False)
                act.wait_ge(st_T, m + 1)
                act.activation(ext[:, :, HIST + SEQ:HIST + SEQ + HIST],
                               bank(5, n=CT * HIST).rearrange("p (c t) -> p c t", c=CT), ACT.Copy).then_inc(st_ready, 1)
                act.wait_ge(glu_r, m + 1)
                act.activation(proj[:, G * T:Q * T], proj[:, G * T:Q * T], ACT.Sigmoid).then_inc(sig_ready, 1)

                def products(first, last_):
                    for k in range(first, min(last_, TAPS)):
                        c = (m * CT + CV) * TAPS + k
                        if k == 0:
                            act.wait_ge(u_ready, m + 1)
                            ins_ = act.activation(yc[:, CV, :], ext[:, CV, 0:CO], ACT.Identity, scale=taps[:, c:c + 1],
                                                  bias=par[:, cvec(0, m, CV):cvec(0, m, CV) + 1])
                        else:
                            if k > 3:
                                act.wait_ge(pconv_ready, m * (TAPS - 1) + k - 3)
                            ins_ = act.activation(prod[:, k % 3, :], ext[:, CV, k:k + CO], ACT.Copy,
                                                  scale=taps[:, c:c + 1])
                        ins_.then_inc(prod_ready, 1)

                in_step(4, False)
                products(0, 4)
                in_step(5, False)
                for tt, (t0, n) in enumerate(TOK):
                    act.wait_ge(vrow_T, 3 * m + tt + 1)
                    act.activation(vrow[0:n, tt, :], bank(tt, slice(0, n), n=CC), ACT.Copy,
                                   scale=rtok[0:n, tt:tt + 1]).then_inc(vrow_ready, 1)
                for hp in range(4):
                    act.wait_ge(rope_done, 13 * m + 5 + 4 + hp + 1)
                    act.activation(kTs[:, hp, PAST:SKEYS], proj[:, (K + hp) * T + SEQ:(K + hp + 1) * T],
                                   ACT.Copy).then_inc(kTs_ready, 1)

                def softmax_exp(n):
                    act.wait_ge(max_ready, 10 * m + n + 1)
                    spans = [(0, SKEYS)] if n < 2 else [(0, P), (P, 384)]
                    for j, (a, b) in enumerate(spans):
                        last = act.activation(prob[:, n % 2, a:b], prob[:, n % 2, a:b], ACT.Exp,
                                              bias=stat[:, 8 * n + 2 + j:8 * n + 3 + j],
                                              accum_out=stat[:, 8 * n + 4 + j:8 * n + 5 + j])
                    last.then_inc(exp_ready, 1)

                def save_pT(n):
                    act.wait_ge(pT_done, 10 * m + n + 1)
                    if n >= 2:
                        act.wait_ge(pv_done, 10 * m + n - 1)
                    if n < 2:
                        act.activation(probT[:, n % 2, 0:512], bank(4, n=512), ACT.Copy)
                        act.activation(probT[0:DEC, n % 2, 512:640], bank(5, slice(0, DEC), n=P),
                                       ACT.Copy).then_inc(pT_ready, 1)
                    else:
                        act.activation(probT[:, n % 2, 0:384], bank(4 + n % 2, n=384), ACT.Copy).then_inc(pT_ready, 1)

                def save_att(n):
                    if n == 1:
                        act.wait_ge(pv_done, 10 * m + 2)
                        act.activation(y[:, 4 * T:8 * T].rearrange("p (c t) -> p c t", c=4)[:, :, SEQ:T],
                                       bank(7, n=P).rearrange("p (c t) -> p c t", c=4), ACT.Copy).then_inc(att_saved, 1)
                    elif n % 2:
                        hp = (n - 2) // 2
                        act.wait_ge(pv_done, 10 * m + n + 1)
                        link(act.activation(y[:, (4 + hp) * T:(4 + hp) * T + SEQ], bank(6 + hp % 2, n=SEQ), ACT.Copy))
                        act.activation(hh[:, 4 + hp, :], y[:, (4 + hp) * T:(5 + hp) * T], ACT.Copy).then_inc(hh_ready, 1)

                products(4, 7)
                softmax_exp(0)
                for n in range(10):
                    if n < 9:
                        softmax_exp(n + 1)
                    save_pT(n)
                    products(7 + 4 * n, 11 + 4 * n)
                    if n >= 1:
                        save_att(n - 1)
                    if n == 7:
                        for ct in range(CT):
                            act.wait_ge(dev_ready, 4 * m + ct + 1)
                            if ct >= 2:
                                act.wait_ge(csq_used, 4 * m + ct - 1)
                            act.activation(y[:, (ct % 2) * CO:(ct % 2 + 1) * CO], yc[:, ct, :],
                                           ACT.Square).then_inc(csq_ready, 1)
                    if n == 8:
                        act.wait_ge(csq_used, 4 * m + 4)
                        act.activation(cinv[:], bank(3, n=CO), ACT.Sqrt, bias=epsc[:, 0:1],
                                       scale=1.0 / CC).then_inc(croot_ready, 1)
                save_att(9)
                for ct in range(CT):
                    act.wait_ge(cn_ready, 4 * m + ct + 1)
                    for src, dst, n in ((0, 0, SEQ), (SAMPLE_AT, SEQ, DEC)):
                        last = act.activation(y[:, ct * T + dst:ct * T + dst + n], yc[:, ct, src:src + n], ACT.Silu,
                                              bias=par[:, cvec(2, m, ct):cvec(2, m, ct) + 1],
                                              scale=par[:, cvec(1, m, ct):cvec(1, m, ct) + 1])
                    link(last)
                    act.activation(hh[:, ct, :], y[:, ct * T:(ct + 1) * T], ACT.Copy).then_inc(hh_ready, 1)
                sqrt_table()
                for g in range(2):
                    act.wait_ge(crow_T, 2 * m + g + 1)
                    act.activation(crow[:, g, :], bank(2 * g + 1, slice(0, HIST), n=CC), ACT.Copy).then_inc(crow_ready, 1)
                for tt, b in enumerate((0, 2, 1)):
                    n = TOK[tt][1]
                    act.wait_ge(krow_T, 4 * m + tt + 1)
                    act.activation(krow[0:n, tt, :], bank(b, slice(0, n), n=CC), ACT.Copy).then_inc(krow_ready, 1)
                act.wait_ge(krow_T, 4 * m + 4)
                for tt, (t0, n) in enumerate(TOK):
                    last = act.activation(kirow[0:n, tt, :], bank(3, slice(0, n), HD * tt, HD), ACT.Copy)
                last.then_inc(krow_ready, 1)
                uo = u + U_IN
                for i in range(2):
                    for j in range(4):
                        if i == 0:
                            split_quad(uo + 4, i, j)
                        save_y(s, 4 * i + j, j if i else 4 + j, j % 2, uo + 4 * i + j)
                        if i:
                            split_quad(uo + 4, i, j)
                post_root(s, False)

            act.dma_start(xrow[:, 0:2, :], ins["x_prompt"][0].rearrange("(j p) d -> p j d", p=P)).then_inc(x_in, 16)
            act.dma_start(xrow[0:DEC, 2, :], ins["x_sample"][0]).then_inc(x_in, 16)
            for name, dst in (("ident", ident), ("swap", swap), ("cosT", cosT), ("sinT", sinT), ("stack", stack)):
                act.dma_start(dst[:], consts[name]).then_inc(const_in, 16)
            for n, name in enumerate(("ffn1_norm_pre", "ffn1_norm_post", "mix_norm_pre", "mix_norm_post",
                                      "ffn2_norm_pre", "ffn2_norm_post")):
                r = gain(n, 0, 0)
                act.dma_start(prow[r:r + DEPTH * KD, :], ins[name].rearrange("l (c p) -> (l c) p", p=P)).then_inc(par_in, 16)
            for n, name in enumerate(("conv_b", "conv_ln_g", "conv_ln_b")):
                r = cvec(n, 0, 0)
                act.dma_start(prow[r:r + DEPTH * CT, :], ins[name].rearrange("l (c p) -> (l c) p", p=P)).then_inc(par_in, 16)
            act.dma_start(trow[:].rearrange("k (l c) -> k l c", l=DEPTH),
                          ins["conv_w"].rearrange("l k c -> k l c")).then_inc(par_in, 16)
            act.wait_ge(par_T, 1)
            act.activation(par[:], bank(7, n=120), ACT.Copy)
            act.activation(taps[:], bank(5, n=DEPTH * CT * TAPS), ACT.Copy).then_inc(par_ready, 1)
            act.wait_ge(ms_ready, 1)
            for rel in range(4):
                split_quad(0, 0, rel, old=False)
            for l in range(DEPTH):
                split_x(3 * l, 4 * l, gain(0, l, 0))
                ffn(2 * l, 3 * l)
                split_x(3 * l + 1, 4 * l + 1, gain(2, l, 0))
                mixer(l, 3 * l + 1)
                split_x(3 * l + 2, 4 * l + 3, gain(4, l, 0))
                act.wait_ge(rows_out, 16 * 8 * (l + 1))
                ffn(2 * l + 1, 3 * l + 2)
            for n in range(6):
                tt, half = divmod(n, 2)
                act.wait_ge(yT_done, n + 1)
                k = TOK[tt][1]
                act.activation(xrow[0:k, tt, half * 512:(half + 1) * 512], bank(n, slice(0, k), n=512),
                               ACT.Copy).then_inc(yrow_ready, 1)

        @block.vector
        def _(dve):
            n_chain = [0]

            def link(ins_):
                n_chain[0] += 1
                ins_.then_inc(dve_chain, 1)
                dve.wait_ge(dve_chain, n_chain[0])

            def split_lo(unit, raw_slot, split_slot, half, n=8):
                dve.wait_ge(hi_ready, unit + 1)
                cols = slice(half * P, (half + 1) * P)
                dve.tensor_tensor(wlo[:, split_slot, 0:n, :], raw[:, raw_slot, 0:n, cols],
                                  whi[:, split_slot, 0:n, :].bitcast(F32), ALU.subtract).then_inc(lo_ready, 1)

            def split_quad(u0, i, rel):
                q, half = divmod(rel, 2)
                split_lo(u0 + 4 * i + rel, q, rel, half)

            def low_x(hq, g, c):
                dve.wait_ge(hh_ready, 8 * hq + c + 1)
                dve.scalar_tensor_tensor(out=hl[:, c, :], in0=x[:, c, :], scalar=par[:, g + c:g + c + 1],
                                         in1=hh[:, c, :].bitcast(F32), op0=ALU.mult, op1=ALU.subtract).then_inc(hl_ready, 1)

            def rms_x(s):
                dve.wait_ge(root_ready, 2 * s + 1)
                dve.reciprocal(rinv[:], root[:]).then_inc(r_ready, 1)
                dve.wait_ge(r_ready, s + 1)

            def clear_acc(s):
                dve.memset(acc[:], 0.0).then_inc(acc_ready, 2)

            def add_sq(s, c, slot):
                dve.wait_ge(ysq_ready, 8 * s + c + 1)
                dve.wait_ge(acc_ready, 9 * s + c + 2)
                dve.tensor_tensor(acc[:], acc[:], ysq[:, slot * T:(slot + 1) * T], ALU.add).then_inc(acc_ready, 1)

            def residual(s, g, hq_next, g_next):
                dve.wait_ge(root_ready, 2 * s + 2)
                link(dve.reciprocal(rinv[:], root[:]))
                dve.wait_ge(y_saved, 8 * s + 8)
                for c in range(KD):
                    k = slice((c % 2) * T, (c % 2 + 1) * T)
                    link(dve.scalar_tensor_tensor(out=upd[:, k], in0=y[:, c * T:(c + 1) * T],
                                                  scalar=par[:, g + c:g + c + 1], in1=rinv[:],
                                                  op0=ALU.mult, op1=ALU.mult))
                    dve.tensor_tensor(x[:, c, :], x[:, c, :], upd[:, k], ALU.add).then_inc(x_ready, 1)
                    if hq_next is not None and c >= 1:
                        low_x(hq_next, g_next, c - 1)
                if hq_next is not None:
                    low_x(hq_next, g_next, KD - 1)

            def ffn(f, s, g, hq_next, g_next):
                u = ffn_unit(f)

                def up_step(i, first):
                    if first:
                        split_quad(u + 4, i, 0)
                        split_quad(u + 4, i, 1)
                        rms_x(s)
                    b0 = (4, 5, 7, 3) if first else (0, 1, 2, 3)
                    for j in range(2):
                        dve.wait_ge(w_used, u + 4 * i + j + 1)
                        dve.tensor_tensor(sil[:, j * T:(j + 1) * T], bank(b0[j]), rinv[:], ALU.mult).then_inc(gr_ready, 1)
                        if not first:
                            split_quad(u + 4, i, j)

                    def low(j):
                        dve.wait_ge(ghi_ready, KF * f + 2 * i + j + 1)
                        dve.tensor_tensor(glo[:, bass.ds((2 * i + j) * T, T)], gt[:, j * T:(j + 1) * T],
                                          ghi[:, bass.ds((2 * i + j) * T, T)].bitcast(F32),
                                          ALU.subtract).then_inc(glo_ready, 1)
                    for j in range(2):
                        dve.wait_ge(w_used, u + 4 * i + 2 + j + 1)
                        if not first:
                            dve.wait_ge(glo_ready, KF * f + 2 * i + j - 1)
                        dve.tensor_tensor(gt[:, j * T:(j + 1) * T], bank(b0[2 + j]), rinv[:],
                                          ALU.mult).then_inc(up_ready, 1)
                        dve.wait_ge(up_ready, KF * f + 2 * i + j + 1)
                        dve.wait_ge(silu_ready, KF * f + 2 * i + j + 1)
                        dve.tensor_tensor(gt[:, j * T:(j + 1) * T], gt[:, j * T:(j + 1) * T],
                                          sil[:, j * T:(j + 1) * T], ALU.mult).then_inc(gt_ready, 1)
                        split_quad(u + 4, i, 2 + j)
                        low(j)

                up_step(0, True)
                with dve.Fori(1, UP_STEPS) as i:
                    up_step(i, False)
                ud = u + U_UP
                clear_acc(s)

                def down_step(i, last):
                    for d in range(2):
                        for j in range(6):
                            c = 4 * i + 2 * d + j - 4
                            if j >= 4 and c < KD - 1:
                                add_sq(s, c, j - 4)
                            jj = 6 * d + j + 4
                            r, half = divmod(jj % 12, 2)
                            if jj < 12 or not last:
                                split_lo(ud + 12 * i + jj, r % 2, jj % 4, half, PARTS[r % 3] if jj < 12 else 8)

                down_step(0, False)
                down_step(1, f == 2 * DEPTH - 1)
                residual(s, g, hq_next, g_next)

            def rope(m, k, tile, b):
                dve.wait_ge(rope_mm, 13 * m + k + 1)
                if k:
                    dve.wait_ge(rope_done, 13 * m + k)
                link(dve.tensor_tensor(ropa[:], tile, cosR[:], ALU.mult))
                link(dve.tensor_tensor(ropb[:], bank(b), sinR[:], ALU.mult))
                dve.tensor_tensor(tile, ropa[:], ropb[:], ALU.add).then_inc(rope_done, 1)

            def top_k(rows, a, b, k):
                for _ in range(k // 8):
                    link(dve.max(m8[rows, :], score[rows, a:b]))
                    link(dve.match_replace(score[rows, a:b], m8[rows, :], score[rows, a:b], TAKEN))

            def mixer(m, s, g, hq_next, g_next):
                dve.wait_ge(tail_hi, m + 1)
                dve.tensor_tensor(wtlo[:], wtail[:], wthi[:].bitcast(F32), ALU.subtract).then_inc(tail_lo, 1)
                rms_x(s)
                dve.tensor_tensor(cosR[:], cosT[:], rinv[:], ALU.mult)
                link(dve.tensor_tensor(sinR[:], sinT[:], rinv[:], ALU.mult))
                for k in range(4):
                    rope(m, k, proj[:, (QI + k) * T:(QI + k + 1) * T], 6 + k % 2)
                rope(m, 4, kiT[:], 6)
                dve.wait_ge(wi_T, m + 1)
                dve.tensor_copy(rtok[:, 0:2], bank(4, lo=24, n=2))
                link(dve.tensor_copy(rtok[0:DEC, 2:3], bank(4, slice(0, DEC), 26, 1)))
                for tt, (t0, n) in enumerate(TOK):
                    last = dve.tensor_scalar(wrow[0:n, 8 * tt:8 * tt + 8], bank(4, slice(0, n), 8 * tt, 8),
                                             rtok[0:n, tt:tt + 1], HEADS ** -0.5, ALU.mult, ALU.mult)
                link(last)
                for h in range(HEADS):
                    last = dve.tensor_copy(wS[32 * (h % 4):32 * (h % 4) + 32, h // 4:h // 4 + 1],
                                           wrow[0:DEC, 16 + h:17 + h])
                link(last)
                dve.tensor_scalar(wdiag[:, 0, :], stack[:], wS[:, 0:1], None, ALU.mult)
                dve.tensor_scalar(wdiag[:, 1, :], stack[:], wS[:, 1:2], None, ALU.mult).then_inc(wrow_ready, 1)
                for h in range(HEADS):
                    dve.wait_ge(rel_ready, 8 * m + h + 1)
                    for a, b, w0 in ((0, P, 0), (P, 384, 8)):
                        src = relP[:, h % 2, a:b]
                        w = wrow[:, w0 + h:w0 + h + 1]
                        if h == 0:
                            last = dve.tensor_scalar(score[:, a:b], src, w, None, ALU.mult)
                        else:
                            last = dve.scalar_tensor_tensor(out=score[:, a:b], in0=src, scalar=w,
                                                            in1=score[:, a:b], op0=ALU.mult, op1=ALU.add)
                    last.then_inc(rel_used, 1)
                    dve.wait_ge(rel_used, 8 * m + h + 1)
                dve.memset(score[0:CHUNK, CHUNK:P], BARRED)
                dve.memset(score[0:CHUNK, P + 3 * CHUNK:P + 4 * CHUNK], BARRED)
                dve.wait_ge(scoreS_done, m + 1)
                dve.tensor_copy(score[0:DEC, 384:928], bank(4, slice(0, DEC), n=SKEYS)).then_inc(scoreS_saved, 1)
                dve.wait_ge(scoreS_saved, m + 1)
                top_k(slice(0, DEC), 384, 928, TOPK_S)
                top_k(slice(0, P), 0, P, TOPK_P)
                top_k(slice(0, P), P, 384, TOPK_P)
                rb = rinv[:].rearrange("p (o t) -> p o t", o=1).to_broadcast([P, CT, T])
                pa = proj[:, A * T:G * T].rearrange("p (c t) -> p c t", c=CT)
                pg = proj[:, G * T:Q * T].rearrange("p (c t) -> p c t", c=CT)
                dve.wait_ge(proj_saved, 24 * m + 12)
                dve.tensor_tensor(pg, pg, rb, ALU.mult).then_inc(glu_r, 1)
                dve.tensor_tensor(pa, pa, rb, ALU.mult)
                for j in range(4):
                    dve.tensor_scalar(maskS[32 * j:32 * j + 32, :], score[0:DEC, 384:928], TAKEN, NEG,
                                      ALU.not_equal, ALU.mult)
                link(dve.tensor_scalar(score[:, 0:384], score[:, 0:384], TAKEN, NEG, ALU.not_equal, ALU.mult))
                dve.wait_ge(sig_ready, m + 1)
                if m:
                    dve.wait_ge(crow_T, 2 * m)
                dve.tensor_tensor(ext[:, :, HIST:HIST + SEQ], pa[:, :, 0:SEQ], pg[:, :, 0:SEQ], ALU.mult)
                dve.tensor_tensor(ext[:, :, EXT - DEC:EXT], pa[:, :, SEQ:T], pg[:, :, SEQ:T],
                                  ALU.mult).then_inc(u_ready, 1)
                dve.wait_ge(u_ready, m + 1)
                dve.wait_ge(st_ready, m + 1)

                def conv(first, last_):
                    for k, ct in (divmod(j, CV) for j in range(first, min(last_, TAPS * CV))):
                        w = taps[:, (m * CT + ct) * TAPS + k:(m * CT + ct) * TAPS + k + 1]
                        src = ext[:, ct, k:k + CO]
                        if k == 0:
                            ins_ = dve.tensor_scalar(yc[:, ct, :], src, w, par[:, cvec(0, m, ct):cvec(0, m, ct) + 1],
                                                     ALU.mult, ALU.add)
                        else:
                            dve.wait_ge(conv_ready, (m * TAPS + k - 1) * CV + ct + 1)
                            ins_ = dve.scalar_tensor_tensor(out=yc[:, ct, :], in0=src, scalar=w, in1=yc[:, ct, :],
                                                            op0=ALU.mult, op1=ALU.add)
                        ins_.then_inc(conv_ready, 1)

                conv(0, CONV_FIRST)
                for k in range(5, 9):
                    rope(m, k, proj[:, (Q + k - 5) * T:(Q + k - 4) * T], 4 + (k - 5))
                conv(CONV_FIRST, CONV_EARLY)
                for k in range(9, 13):
                    rope(m, k, proj[:, (Q + k - 5) * T:(Q + k - 4) * T], 4 + (k - 9))

                def softmax_max(n):
                    dve.wait_ge(s_done, 10 * m + n + 1)
                    if n >= 2:
                        dve.wait_ge(pT_done, 10 * m + n - 1)
                    spans = [(0, SKEYS)] if n < 2 else [(0, P), (P, 384)]
                    c = 8 * n
                    for j, (a, b) in enumerate(spans):
                        logits = ps[:, 1024 * (n % 2) + a:1024 * (n % 2) + b]
                        mask = maskS[:] if n < 2 else score[:, a:b]
                        link(dve.tensor_tensor_reduce(prob[:, n % 2, a:b], logits, mask, HD ** -0.5, -3.0e38,
                                                      ALU.add, ALU.max, stat[:, c + j:c + j + 1]))
                    k = len(spans)
                    dve.tensor_scalar(stat[:, c + 2:c + 2 + k], stat[:, c:c + k], -1.0, None,
                                      ALU.mult).then_inc(max_ready, 1)

                def softmax_norm(n):
                    dve.wait_ge(exp_ready, 10 * m + n + 1)
                    spans = [(0, SKEYS)] if n < 2 else [(0, P), (P, 384)]
                    k, c = len(spans), 8 * n
                    link(dve.reciprocal(stat[:, c + 6:c + 6 + k], stat[:, c + 4:c + 4 + k]))
                    for j, (a, b) in enumerate(spans):
                        last = dve.tensor_scalar(prob[:, n % 2, a:b], prob[:, n % 2, a:b],
                                                 stat[:, c + 6 + j:c + 7 + j], None, ALU.mult)
                    last.then_inc(p_ready, 1)

                def low_mix(k, c):
                    dve.wait_ge(hh_ready, 8 * (4 * m + 2) + k + 1)
                    dve.tensor_tensor(hl[:, c, :], y[:, c * T:(c + 1) * T], hh[:, c, :].bitcast(F32),
                                      ALU.subtract).then_inc(hl_ready, 1)

                softmax_max(0)
                for n in range(10):
                    if n < 9:
                        softmax_max(n + 1)
                    softmax_norm(n)
                    conv(CONV_EARLY + n * CONV_ITEM, CONV_EARLY + (n + 1) * CONV_ITEM)
                    if n == 6:
                        dve.wait_ge(mu_done, m + 1)
                        for ct in range(CT):
                            dve.scalar_tensor_tensor(out=yc[:, ct, :], in0=bank(1, n=CO), scalar=-1.0 / CC,
                                                     in1=yc[:, ct, :], op0=ALU.mult, op1=ALU.add).then_inc(dev_ready, 1)
                    if n in (5, 7, 9):
                        low_mix((n - 5) // 2, 4 + (n - 5) // 2)
                dve.wait_ge(croot_ready, m + 1)
                link(dve.reciprocal(cinv[:], cinv[:]))
                for ct in range(CT):
                    dve.tensor_tensor(yc[:, ct, :], yc[:, ct, :], cinv[:], ALU.mult).then_inc(cn_ready, 1)
                low_mix(3, 7)
                for ct in range(CT):
                    low_mix(4 + ct, ct)
                clear_acc(s)
                for c in range(KD - 1):
                    add_sq(s, c, c % 2)
                residual(s, g, hq_next, g_next)

            dve.memset(ones[:], 1.0)
            dve.memset(epsc[:, 0:1], EPS)
            dve.memset(epsc[:, 1:2], 4.0 * EPS)
            dve.memset(ext[:, :, 0:HIST], 0.0).then_inc(ms_ready, 1)
            dve.wait_ge(par_ready, 1)
            for c in range(KD):
                dve.wait_ge(x_T, c + 1)
                dve.tensor_copy(x[:, c, :], bank(c % 4)).then_inc(x_ready, 1)
                if c:
                    low_x(0, gain(0, 0, 0), c - 1)
            for rel in range(4):
                split_quad(0, 0, rel)
            low_x(0, gain(0, 0, 0), KD - 1)
            for l in range(DEPTH):
                ffn(2 * l, 3 * l, gain(1, l, 0), 4 * l + 1, gain(2, l, 0))
                mixer(l, 3 * l + 1, gain(3, l, 0), 4 * l + 3, gain(4, l, 0))
                dve.wait_ge(lo_ready, ffn_unit(2 * l + 1) + 4)
                ffn(2 * l + 1, 3 * l + 2, gain(5, l, 0), *((4 * l + 4, gain(0, l + 1, 0)) if l < DEPTH - 1 else (None, None)))

        @block.gpsimd
        def _(pool):
            def split_lo(unit, raw_slot, split_slot, half):
                pool.wait_ge(hi_ready, unit + 1)
                cols = slice(half * P, (half + 1) * P)
                pool.tensor_tensor(wlo[:, split_slot, :, :], raw[:, raw_slot, :, cols],
                                   whi[:, split_slot, :, :].bitcast(F32), ALU.subtract).then_inc(lo_ready, 1)

            def step(u0, i):
                for rel in range(4):
                    split_lo(u0 + 4 * i + rel, rel // 2, rel, rel % 2)

            def sum_x(s):
                pool.wait_ge(sq_ready, 8 * s + 1)
                pool.memset(accx[:], 0.0).then_inc(accx_ready, 2)
                for c in range(KD):
                    pool.wait_ge(sq_ready, 8 * s + c + 1)
                    pool.wait_ge(accx_ready, 10 * s + c + 2)
                    pool.tensor_tensor(accx[:], accx[:], sq[:, c % 2, :], ALU.add).then_inc(accx_ready, 1)

            sum_x(0)
            for m in range(DEPTH):
                u = mix_unit(m)
                pool.wait_ge(glo_ready, KF * (2 * m + 1))
                w_in = ins["w_in"][m].rearrange("(k p) n -> p k n", p=P)
                for d, (c0, n) in ((0, (KI_COL, HD)), (HD, (KI_COL, HD)), (2 * HD, (KI_COL + HD, HEADS))):
                    with nc.allow_non_contiguous_dma(reason="8 head-weight columns"):
                        pool.dma_start(wtail[:, :, d:d + n], w_in[:, :, c0:c0 + n]).then_inc(tail_in, 16)
                sum_x(3 * m + 1)
                pool.wait_ge(x_ready, 8 * (3 * m + 1) + 8)
                kix = ins["cache_kidx"][m, 0].rearrange("(j p) d -> p j d", p=P)
                pool.dma_start(kidx[:, :, 0:HD], kix).then_inc(kidx_in, 16)
                pool.dma_start(kidx[:, :, HD:2 * HD], kix).then_inc(kidx_in, 16)
                pool.dma_start(kc[:], ins["cache_k"][m, 0].rearrange("(j p) h d -> p j (h d)", p=P)).then_inc(kc_in, 16)
                pool.dma_start(vc[:], ins["cache_v"][m, 0].rearrange("(j p) h d -> p j (h d)", p=P)).then_inc(vc_in, 16)
                pool.dma_start(statein[:], ins["state_conv"][m, 0]).then_inc(state_in, 16)
                pool.wait_ge(lo_ready, u + 4)
                step(u + 4, 0)
                with pool.Fori(1, 6) as i:
                    step(u + 4, i)
                for k in range(1, TAPS):
                    pool.wait_ge(prod_ready, m * TAPS + k + 1)
                    if k > 1:
                        pool.wait_ge(pconv_ready, m * (TAPS - 1) + k - 1)
                    pool.tensor_tensor(yc[:, CV, :], yc[:, CV, :], prod[:, k % 3, :], ALU.add).then_inc(pconv_ready, 1)
                step(u + U_IN + 4, 0)
                pool.wait_ge(crow_ready, 2 * m + 2)
                pool.dma_start(prompt_conv[m, 0], crow[:, 0, :]).then_inc(rows_out, 16)
                pool.dma_start(sample_conv[m, 0], crow[:, 1, :]).then_inc(rows_out, 16)
                for ready, need, buf, pr, sa in ((vrow_ready, 3 * m + 3, vrow, prompt_v, sample_v),
                                                 (krow_ready, 4 * m + 4, krow, prompt_k, sample_k)):
                    pool.wait_ge(ready, need)
                    pool.dma_start(pr[m, 0].rearrange("(j p) h d -> p j (h d)", p=P), buf[:, 0:2, :]).then_inc(rows_out, 16)
                    pool.dma_start(sa[m, 0].rearrange("p h d -> p (h d)"), buf[0:DEC, 2, :]).then_inc(rows_out, 16)
                pool.dma_start(prompt_ki[m, 0].rearrange("(j p) d -> p j d", p=P), kirow[:, 0:2, :]).then_inc(rows_out, 16)
                pool.dma_start(sample_ki[m, 0], kirow[0:DEC, 2, :]).then_inc(rows_out, 16)
                step(u + U_IN + 4, 1)
                sum_x(3 * m + 2)
                if m < DEPTH - 1:
                    sum_x(3 * m + 3)
            pool.wait_ge(rows_out, 16 * 8 * DEPTH)

        @block.tensor
        def _(pe):
            def triple(out, slot, k, hi, lo, start, stop):
                pe.matmul(out, wlo[:, slot, k, :], hi, start=start, stop=False)
                pe.matmul(out, whi[:, slot, k, :], lo, start=False, stop=False)
                return pe.matmul(out, whi[:, slot, k, :], hi, start=False, stop=stop)

            def sum_squares(s):
                pe.wait_ge(accx_ready, 10 * s + 10)
                pe.matmul(bank(6), ones[:], accx[:], start=True, stop=True).then_inc(sx_done, 1)

            def sum_y(s):
                pe.wait_ge(acc_ready, 9 * s + 9)
                pe.matmul(bank(6), ones[:], acc[:], start=True, stop=False)
                pe.wait_ge(ysq_ready, 8 * s + 8)
                pe.matmul(bank(6), ones[:], ysq[:, T:2 * T], start=False, stop=True).then_inc(ss_done, 1)

            def first_step(u0, hq, banks, order=range(KD), s=None, between=None):
                pe.wait_ge(lo_ready, u0 + 4)
                for n, k in enumerate(order[:MERGED]):
                    pe.wait_ge(hl_ready, 8 * hq + n + 1)
                    for rel in range(4):
                        triple(bank(banks[rel]), rel, k, hh[:, k, :], hl[:, k, :], n == 0, False)
                if between is not None:
                    between()
                for rel in range(4):
                    for n, k in enumerate(order[MERGED:], MERGED):
                        if rel == 0:
                            pe.wait_ge(hl_ready, 8 * hq + n + 1)
                        last = triple(bank(banks[rel]), rel, k, hh[:, k, :], hl[:, k, :], False, n == KD - 1)
                    last.then_inc(w_used, 1)
                    if rel == 1 and s is not None:
                        sum_squares(s)

            def up_step(f, i):
                u = ffn_unit(f)
                for rel in range(4):
                    pe.wait_ge(lo_ready, u + 4 * i + rel + 1)
                    pe.wait_ge(gr_ready if rel < 2 else up_ready, KF * f + 2 * i + rel % 2 - 1)
                    for k in range(KD):
                        last = triple(bank(rel), rel, k, hh[:, k, :], hl[:, k, :], k == 0, k == KD - 1)
                    last.then_inc(w_used, 1)

            def down_step(f, s, i, first):
                ud = ffn_unit(f) + U_UP
                for d in range(2):
                    for part in range(3):
                        for col in range(2):
                            j = 6 * d + 2 * part + col
                            pe.wait_ge(lo_ready, ud + 12 * i + j + 1)
                            if part == 0:
                                if first:
                                    pe.wait_ge(gr_ready if d == 0 else up_ready, KF * f + KF)
                                else:
                                    pe.wait_ge(y_saved, 8 * s + 4 * i + 2 * d + col - 3)
                            if first and d == 0 and col == 0:
                                pe.wait_ge(glo_ready, KF * f + 8 * part + PARTS[part])
                            for k in range(PARTS[part]):
                                kk = 8 * part + k
                                last = triple(bank(2 * d + col), j % 4, k, ghi[:, kk * T:(kk + 1) * T],
                                              glo[:, kk * T:(kk + 1) * T], kk == 0, kk == KF - 1)
                            last.then_inc(w_used, 1)

            def ffn(f, s, hq):
                first_step(ffn_unit(f), hq, (4, 5, 7, 3), s=s)
                with pe.Fori(1, UP_STEPS) as i:
                    up_step(f, i)
                down_step(f, s, 0, True)
                down_step(f, s, 1, False)
                sum_y(s)

            def mixer(m, s, hq):
                u = mix_unit(m)
                first_step(u, hq, (0, 1, 2, 3), s=s)
                pe.wait_ge(tail_lo, m + 1)
                for b, c0, n in ((4, 0, P), (5, P, HEADS)):
                    for k in range(KD):
                        o = bank(b, slice(0, n))
                        pe.matmul(o, wtlo[:, k, c0:c0 + n], hh[:, k, :], start=(k == 0), stop=False)
                        pe.matmul(o, wthi[:, k, c0:c0 + n], hl[:, k, :], start=False, stop=False)
                        last = pe.matmul(o, wthi[:, k, c0:c0 + n], hh[:, k, :], start=False, stop=(k == KD - 1))
                    last.then_inc(tail_done, 1)
                pe.wait_ge(root_ready, 2 * s + 1)
                for k in range(5):
                    if k < 4:
                        pe.wait_ge(proj_saved, 24 * m + k + 1)
                        src = proj[:, (QI + k) * T:(QI + k + 1) * T]
                    else:
                        pe.wait_ge(tail_saved, 2 * m + 1)
                        src = kiT[:]
                    if k >= 2:
                        pe.wait_ge(rope_done, 13 * m + k - 1)
                    pe.matmul(bank(6 + k % 2), swap[:], src, start=True, stop=True).then_inc(rope_mm, 1)
                pe.wait_ge(tail_saved, 2 * m + 2)
                pe.wait_ge(r_ready, s + 1)
                for tt, (t0, n) in enumerate(TOK):
                    pe.transpose(bank(4, slice(0, n), 8 * tt, 8), wiT[:, t0:t0 + n], ident[0:HEADS, 0:HEADS])
                    last = pe.matmul(bank(4, slice(0, n), 24 + tt, 1), rinv[0:1, t0:t0 + n], ones[0:1, 0:1],
                                     start=True, stop=True)
                last.then_inc(wi_T, 1)
                pe.wait_ge(kidx_in, 32 * (m + 1))
                for j in range(4):
                    last = pe.transpose(bank(5, n=P, lo=P * j), kidx[:, j, :], ident[:])
                last.then_inc(kidx_T, 1)
                pe.wait_ge(kc_in, 16 * (m + 1))
                for hp in range(4):
                    for j in range(4):
                        last = pe.transpose(bank(hp, lo=j * P, n=P), kc[:, j, hp * P:(hp + 1) * P], ident[:])
                    last.then_inc(kcT_done, 1)
                pe.wait_ge(rope_done, 13 * m + 5)
                pe.wait_ge(kiTs_ready, 2 * m + 2)
                for g in range(2):
                    for j in range(4):
                        h = 4 * g + j
                        r = slice((h % 2) * HD, (h % 2 + 1) * HD)
                        o = slice(32 * j, 32 * j + 32)
                        q = proj[r, (QI + h // 2) * T + SEQ:(QI + h // 2 + 1) * T]
                        pe.matmul(bank(2 * g, o, n=PAST), q, kiTs[r, 0:PAST], start=True, stop=True)
                        last = pe.matmul(bank(2 * g + 1, o, n=DEC), q, kiTs[r, PAST:SKEYS], start=True, stop=True)
                    last.then_inc(lgS_done, 1)
                for h in range(HEADS):
                    r = slice((h % 2) * HD, (h % 2 + 1) * HD)
                    q0 = (QI + h // 2) * T
                    if h >= 2:
                        pe.wait_ge(rel_ready, 8 * m + h - 1)
                    b = 6 + h % 2
                    pe.matmul(bank(b, n=P), proj[r, q0:q0 + P], kiT[r, 0:P], start=True, stop=True)
                    pe.matmul(bank(b, lo=P, n=SEQ), proj[r, q0 + P:q0 + SEQ], kiT[r, 0:SEQ], start=True,
                              stop=True).then_inc(lg_done, 1)
                pe.wait_ge(wrow_ready, m + 1)
                pe.wait_ge(relS_ready, 2 * m + 2)
                for g in range(2):
                    pe.matmul(bank(4, slice(0, DEC), n=PAST), wdiag[:, g, :], relS[:, g, 0:PAST], start=(g == 0), stop=(g == 1))
                for g in range(2):
                    last = pe.matmul(bank(5, slice(0, DEC), n=DEC), wdiag[:, g, :], relS[:, g, PAST:SKEYS],
                                     start=(g == 0), stop=(g == 1))
                last.then_inc(scoreS_done, 1)

                def in_step(i):
                    for rel in range(4):
                        pe.wait_ge(lo_ready, u + 4 * i + rel + 1)
                        pe.wait_ge(proj_saved, 24 * m + 4 * i + rel - 3)
                        for k in range(KD):
                            last = triple(bank(rel), rel, k, hh[:, k, :], hl[:, k, :], k == 0, k == KD - 1)
                        last.then_inc(w_used, 1)

                def partners(k0):
                    for k in range(k0, k0 + 4):
                        pe.matmul(bank(4 + k - k0), swap[:], proj[:, (Q + k - 5) * T:(Q + k - 4) * T], start=True,
                                  stop=True).then_inc(rope_mm, 1)

                with pe.Fori(1, 4) as i:
                    in_step(i)
                pe.wait_ge(state_in, 16 * (m + 1))
                pe.wait_ge(scoreS_saved, m + 1)
                for ct in range(CT):
                    last = pe.transpose(bank(5, lo=HIST * ct, n=HIST), statein[:, ct * P:(ct + 1) * P],
                                        ident[0:HIST, 0:HIST])
                last.then_inc(st_T, 1)
                in_step(4)
                pe.wait_ge(proj_saved, 24 * m + 16)
                pe.wait_ge(st_ready, m + 1)
                pe.wait_ge(rel_ready, 8 * m + 8)
                partners(5)
                in_step(5)
                pe.wait_ge(proj_saved, 24 * m + 20)
                pe.wait_ge(rope_done, 13 * m + 9)
                partners(9)
                pe.wait_ge(proj_saved, 24 * m + 24)
                for tt, (t0, n) in enumerate(TOK):
                    for c in range(4):
                        o = (V + c) * T + t0
                        last = pe.transpose(bank(tt, slice(0, n), c * P, P), proj[:, o:o + n], ident[:])
                    last.then_inc(vrow_T, 1)

                def conv_mean():
                    pe.wait_ge(conv_ready, (m + 1) * TAPS * CV)
                    pe.wait_ge(pconv_ready, (m + 1) * (TAPS - 1))
                    for ct in range(CT):
                        last = pe.matmul(bank(1, n=CO), ones[:], yc[:, ct, :], start=(ct == 0), stop=(ct == CT - 1))
                    last.then_inc(mu_done, 1)

                def conv_var():
                    for ct in range(CT):
                        pe.wait_ge(csq_ready, 4 * m + ct + 1)
                        pe.matmul(bank(3, n=CO), ones[:], y[:, (ct % 2) * CO:(ct % 2 + 1) * CO], start=(ct == 0),
                                  stop=(ct == CT - 1)).then_inc(csq_used, 1)

                def logits(n):
                    if n >= 2:
                        pe.wait_ge(max_ready, 10 * m + n - 1)
                    b = 2 * (n % 2)
                    if n < 2:
                        for j in range(4):
                            h = 4 * n + j
                            r = slice((h % 2) * HD, (h % 2 + 1) * HD)
                            o = slice(32 * j, 32 * j + 32)
                            q = proj[r, (Q + h // 2) * T + SEQ:(Q + h // 2 + 1) * T]
                            pe.matmul(bank(b, o, n=PAST), q, kTs[r, h // 2, 0:PAST], start=True, stop=True)
                            last = pe.matmul(bank(b + 1, o, n=DEC), q, kTs[r, h // 2, PAST:SKEYS], start=True, stop=True)
                    else:
                        h = n - 2
                        r = slice((h % 2) * HD, (h % 2 + 1) * HD)
                        q0, k0 = (Q + h // 2) * T, (K + h // 2) * T
                        pe.matmul(bank(b, n=P), proj[r, q0:q0 + P], proj[r, k0:k0 + P], start=True, stop=True)
                        last = pe.matmul(bank(b, lo=P, n=SEQ), proj[r, q0 + P:q0 + SEQ], proj[r, k0:k0 + SEQ],
                                         start=True, stop=True)
                    last.then_inc(s_done, 1)

                def turn(n):
                    pe.wait_ge(p_ready, 10 * m + n + 1)
                    if n >= 1:
                        pe.wait_ge(pT_ready, 10 * m + n)
                    if n < 2:
                        for j in range(4):
                            pe.transpose(bank(4, lo=j * P, n=P), prob[:, n % 2, j * P:(j + 1) * P], ident[:])
                        last = pe.transpose(bank(5, slice(0, DEC), n=P), prob[:, n % 2, PAST:SKEYS], ident[:])
                    else:
                        for j in range(3):
                            last = pe.transpose(bank(4 + n % 2, lo=j * P, n=P), prob[:, n % 2, j * P:(j + 1) * P], ident[:])
                    last.then_inc(pT_done, 1)

                def values(n):
                    pe.wait_ge(pT_ready, 10 * m + n + 1)
                    if n < 2:
                        pe.wait_ge(vc_in, 16 * (m + 1))
                        pe.wait_ge(vrow_ready, 3 * m + 3)
                        for j4 in range(4):
                            h = 4 * n + j4
                            r = slice((h % 2) * HD, (h % 2 + 1) * HD)
                            o = bank(7, r, 32 * (h // 2), DEC)
                            hc = slice(h * HD, (h + 1) * HD)
                            for j in range(4):
                                pe.matmul(o, vc[:, j, hc], probT[:, n % 2, j * P + 32 * j4:j * P + 32 * j4 + 32],
                                          start=(j == 0), stop=False)
                            last = pe.matmul(o, vrow[0:DEC, 2, hc], probT[0:DEC, n % 2, 512 + 32 * j4:544 + 32 * j4],
                                             start=False, stop=True)
                    else:
                        h = n - 2
                        hp = h // 2
                        if h % 2 == 0:
                            pe.wait_ge(att_saved, m + 1)
                            if hp >= 2:
                                pe.wait_ge(hh_ready, 8 * (4 * m + 2) + hp - 1)
                        r = slice((h % 2) * HD, (h % 2 + 1) * HD)
                        hc = slice(h * HD, (h + 1) * HD)
                        b = 6 + hp % 2
                        pe.matmul(bank(b, r, n=P), vrow[:, 0, hc], probT[:, n % 2, 0:P], start=True, stop=True)
                        pe.matmul(bank(b, r, P, P), vrow[:, 0, hc], probT[:, n % 2, P:2 * P], start=True, stop=False)
                        last = pe.matmul(bank(b, r, P, P), vrow[:, 1, hc], probT[:, n % 2, 2 * P:3 * P],
                                         start=False, stop=True)
                    last.then_inc(pv_done, 1)

                pe.wait_ge(rope_done, 13 * m + 13)
                pe.wait_ge(kTs_ready, 8 * m + 8)
                logits(0)
                logits(1)
                for n in range(10):
                    turn(n)
                    if n < 8:
                        logits(n + 2)
                    if n >= 1:
                        values(n - 1)
                    if n == 6:
                        conv_mean()
                    if n == 8:
                        conv_var()
                values(9)
                pe.wait_ge(croot_ready, m + 1)
                for g, c0 in enumerate((SEQ, EXT - HIST)):
                    for ct in range(CT):
                        last = pe.transpose(bank(2 * g + 1, slice(0, HIST), ct * P, P), ext[:, ct, c0:c0 + HIST], ident[:])
                    last.then_inc(crow_T, 1)

                def key_rows(tt, b):
                    t0, n = TOK[tt]
                    for c in range(4):
                        o = (K + c) * T + t0
                        last = pe.transpose(bank(b, slice(0, n), c * P, P), proj[:, o:o + n], ident[:])
                    last.then_inc(krow_T, 1)

                def last_rows():
                    pe.wait_ge(crow_ready, 2 * m + 2)
                    key_rows(2, 1)
                    for tt, (t0, n) in enumerate(TOK):
                        last = pe.transpose(bank(3, slice(0, n), HD * tt, HD), kiT[0:HD, t0:t0 + n], ident[0:HD, 0:HD])
                    last.then_inc(krow_T, 1)

                key_rows(0, 0)
                key_rows(1, 2)
                uo = u + U_IN
                pe.wait_ge(hh_ready, 8 * (4 * m + 2) + 4)
                first_step(uo, 4 * m + 2, (4, 5, 6, 7), (4, 5, 6, 7, 0, 1, 2, 3), between=last_rows)
                pe.wait_ge(krow_ready, 4 * m + 4)
                for rel in range(4):
                    pe.wait_ge(lo_ready, uo + 4 + rel + 1)
                    for k in range(KD):
                        last = triple(bank(rel), rel, k, hh[:, k, :], hl[:, k, :], k == 0, k == KD - 1)
                    last.then_inc(w_used, 1)
                sum_y(s)

            pe.wait_ge(const_in, 16 * 5)
            pe.wait_ge(par_in, 16 * 10)
            pe.transpose(bank(7, n=120), prow[:], ident[0:120, 0:120])
            for j in range(DEPTH * CT):
                last = pe.transpose(bank(5, lo=TAPS * j, n=TAPS), trow[:, j * P:(j + 1) * P], ident[0:TAPS, 0:TAPS])
            last.then_inc(par_T, 1)
            pe.wait_ge(x_in, 32)
            for c in range(KD):
                if c >= 4:
                    pe.wait_ge(x_ready, c - 3)
                for tt, (t0, n) in enumerate(TOK):
                    last = pe.transpose(bank(c % 4, lo=t0, n=n), xrow[0:n, tt, c * P:(c + 1) * P], ident[0:n, 0:n])
                last.then_inc(x_T, 1)
            pe.wait_ge(ms_ready, 1)
            pe.wait_ge(par_ready, 1)
            for l in range(DEPTH):
                ffn(2 * l, 3 * l, 4 * l)
                mixer(l, 3 * l + 1, 4 * l + 1)
                ffn(2 * l + 1, 3 * l + 2, 4 * l + 3)
            pe.wait_ge(x_ready, 8 * 6 + 8)
            for n in range(6):
                tt, half = divmod(n, 2)
                t0, k = TOK[tt]
                for c in range(4):
                    last = pe.transpose(bank(n, slice(0, k), c * P, P), x[:, 4 * half + c, t0:t0 + k], ident[:])
                last.then_inc(yT_done, 1)


_INS = ["x_prompt", "x_sample", "cache_k", "cache_v", "cache_kidx", "state_conv", "ffn1_norm_pre",
        "ffn1_norm_post", "ffn1_w_up", "ffn1_w_down", "mix_norm_pre", "mix_norm_post", "w_in", "conv_w", "conv_b",
        "conv_ln_g", "conv_ln_b", "w_out", "ffn2_norm_pre", "ffn2_norm_post", "ffn2_w_up", "ffn2_w_down"]
_OUTS = [(1, SEQ, D), (1, DEC, D), (DEPTH, 1, SEQ, HEADS, HD), (DEPTH, 1, SEQ, HEADS, HD), (DEPTH, 1, SEQ, HD),
         (DEPTH, 1, HIST, CC), (DEPTH, 1, DEC, HEADS, HD), (DEPTH, 1, DEC, HEADS, HD), (DEPTH, 1, DEC, HD),
         (DEPTH, 1, HIST, CC)]


def shape_constants():
    f = np.float32
    pos = np.concatenate([np.arange(SEQ), PAST + np.arange(DEC)]).astype(f)
    inv = (f(1.0) / (f(THETA) ** (np.arange(0, HD, 2).astype(f) / f(HD)))).astype(f)
    angle = (pos[:, None] * inv[None, :]).astype(f)
    half = np.arange(P) % (HD // 2)
    swap = np.zeros((P, P), f)
    for j in range(P):
        if j % HD < HD // 2:
            swap[j + HD // 2, j] = -1.0
        else:
            swap[j - HD // 2, j] = 1.0
    return {"ident": np.eye(P, dtype=f), "swap": swap, "stack": np.tile(np.eye(DEC, dtype=f), (4, 1)),
            "cosT": np.ascontiguousarray(np.cos(angle).astype(f)[:, half].T),
            "sinT": np.ascontiguousarray(np.sin(angle).astype(f)[:, half].T)}


def kernel(**inputs):
    import concourse.bacc as _bacc
    from concourse.bass_utils import run_bass_kernel_spmd as _run

    nc = _bacc.Bacc("TRN2", target_bir_lowering=False, num_devices=1)
    arrays, ins, consts = {}, {}, {}
    for name in _INS:
        a = np.ascontiguousarray(inputs[name])
        arrays[f"in_{name}"] = a
        ins[name] = nc.dram_tensor(f"in_{name}", a.shape, mybir.dt.from_np(a.dtype), kind="ExternalInput").ap()
    for name, a in shape_constants().items():
        arrays[f"const_{name}"] = a
        consts[name] = nc.dram_tensor(f"const_{name}", a.shape, F32, kind="ExternalInput").ap()
    outs = [nc.dram_tensor(f"out_{i}", shape, F32, kind="ExternalOutput").ap() for i, shape in enumerate(_OUTS)]
    build(nc, ins, consts, outs)
    r = _run(nc, [arrays], core_ids=[0])
    return tuple(r.results[0][f"out_{i}"] for i in range(len(_OUTS)))
```

```python
from contextlib import ExitStack

import numpy as np

import concourse.bass as bass
from concourse import mybir

F32 = mybir.dt.float32
F32R = mybir.dt.float32r
ALU = mybir.AluOpType
ACT = mybir.ActivationFunctionType

P = 128
D = 1024
SEQ = 256
DEC = 32
T = SEQ + DEC
PAST = 512
SKEYS = PAST + DEC
DEPTH = 2
DFF = 2816
KD = D // P
KF = DFF // P
CC = 512
CT = CC // P
TAPS = 31
HIST = TAPS - 1
HEADS = 8
HD = 64
CHUNK = 64
THETA = 10000.0
TOPK_P = min(256, SEQ // 4)
TOPK_S = min(256, SKEYS // 4)
EPS = 1e-6
STRIP = 256
NEG = -1.0e30
BARRED = -1.0e38
TAKEN = -3.0e38
assert TOPK_P % 8 == 0 and TOPK_S % 8 == 0
TOK = [(0, 128), (128, 128), (256, 32)]

UP_STEPS = DFF // STRIP
QI_COL = 5 * CC
KI_COL = QI_COL + CC
WIDX = 2 * HD + HEADS
EXT = HIST + SEQ + HIST + DEC
CO = EXT - HIST
SAMPLE_AT = SEQ + HIST
U_UP, U_DOWN, U_IN, U_OUT = 4 * UP_STEPS, 24, 24, 8
U_LAYER = 2 * (U_UP + U_DOWN) + U_IN + U_OUT
TAPS_CT2 = 21
DVE_STEPS = [(ct, k) for k in range(TAPS) for ct in range(3) if ct < 2 or k < TAPS_CT2]
POOL_STEPS = [(3, k) for k in range(TAPS)] + [(2, k) for k in range(TAPS_CT2, TAPS)]
POOL_SUMS = len(POOL_STEPS) - 2
CONV_FIRST = 8
CONV_EARLY = 22
CONV_LATE = 28
CONV_ITEM = 8
PROD_ITEM = 6
SPAN0 = (0, P, T - P)
KEEP_BUSY = 6
MERGED = 5
PARTS = (8, 8, 6)
QI, A, G, Q, K, V = 0, 4, 8, 12, 16, 20


def ffn_unit(f):
    return (f // 2) * U_LAYER + (f % 2) * (U_UP + U_DOWN + U_IN + U_OUT)


def mix_unit(m):
    return m * U_LAYER + U_UP + U_DOWN


def gain(n, l, c):
    return (n * DEPTH + l) * KD + c


def cvec(n, l, ct):
    return 6 * DEPTH * KD + (n * DEPTH + l) * CT + ct


def build(nc, ins, consts, outs):
    (y_prompt, y_sample, prompt_k, prompt_v, prompt_ki, prompt_conv,
     sample_k, sample_v, sample_ki, sample_conv) = outs
    with ExitStack() as ctx:
        BASE = (nc.sbuf_base + 31) // 32 * 32
        SIZE = nc.sbuf_usable_end - BASE
        ctx.enter_context(nc.sbuf_tensor("arena", [P, (SIZE - 64) // 4], F32))
        at = [0]

        def sb(name, shape, dt=F32):
            size = int(np.prod(shape[1:])) * 4
            t = nc.alloc_sbuf_tensor_at(name, list(shape), dt, offset=BASE + at[0])
            at[0] += (size + 31) // 32 * 32
            assert at[0] <= SIZE - 64, (name, at[0])
            return t

        def sem(name):
            return ctx.enter_context(nc.semaphore(name))

        raw = sb("raw", [P, 2, 8, STRIP])
        whi = sb("whi", [P, 4, 8, P], F32R)
        wlo = sb("wlo", [P, 4, 8, P], F32R)
        x = sb("x", [P, KD, T])
        hh = sb("hh", [P, KD, T], F32R)
        hl = sb("hl", [P, KD, T], F32R)
        y = sb("y", [P, KD * T])
        cinv = sb("cinv", [P, CO])
        accx = sb("accx", [P, T])
        sq = sb("sq", [P, 2, T])
        ysq = sb("ysq", [P, 2 * T])
        acc = sb("acc", [P, T])
        root = sb("root", [P, T])
        rinv = sb("rinv", [P, T])
        shared_a = at[0]
        upd = sb("upd", [P, 2 * T])
        tail_at = at[0]
        sil = sb("sil", [P, 2 * T])
        gt = sb("gt", [P, 2 * T])
        g_at = at[0]
        ghi = sb("ghi", [P, KF * T], F32R)
        glo = sb("glo", [P, KF * T], F32R)
        g_end = at[0]
        proj_at = at[0]
        proj = sb("proj", [P, 24 * T])
        ident = sb("ident", [P, P])
        ones = sb("ones", [P, P])
        swap = sb("swap", [P, P])
        cosT = sb("cosT", [P, T])
        sinT = sb("sinT", [P, T])
        par = sb("par", [P, 120])
        taps = sb("taps", [P, DEPTH * CT * TAPS])
        ext = sb("ext", [P, CT, EXT])
        kiT = sb("kiT", [P, T])
        wiT = sb("wiT", [HEADS, T])
        wrow = sb("wrow", [P, 3 * HEADS])
        rcol = sb("rcol", [P, 3])
        rtok = sb("rtok", [P, 3])
        wS = sb("wS", [P, 2])
        wdiag = sb("wdiag", [P, 2, DEC])
        stack = sb("stack", [P, DEC])
        score = sb("score", [P, 928])
        m8 = sb("m8", [P, 16])
        epsc = sb("epsc", [P, 2])
        stat = sb("stat", [P, 10 * 8])
        statein = sb("statein", [HIST, CC])
        cosR = sb("cosR", [P, T])
        sinR = sb("sinR", [P, T])
        at[0] = g_at
        wthi = sb("wthi", [P, KD, WIDX], F32R)
        wtlo = sb("wtlo", [P, KD, WIDX], F32R)
        rel_at = at[0]
        relP = sb("relP", [P, 2, 384])
        relS = sb("relS", [P, 2, SKEYS])
        kidx_at = at[0]
        kidx = sb("kidx", [P, 4, 2 * HD])
        kiTs = sb("kiTs", [P, SKEYS])
        ropa = sb("ropa", [P, 3, T])
        ropb = sb("ropb", [P, 3, T])
        kc_at = at[0]
        kc = sb("kc", [P, 4, CC])
        vc = sb("vc", [P, 4, CC])
        vrow = sb("vrow", [P, 3, CC])
        kirow = sb("kirow", [P, 3, HD])
        assert at[0] <= g_end, at[0] - g_end
        at[0] = g_at
        kTs = sb("kTs", [P, 4, SKEYS])
        at[0] = rel_at
        prob = sb("prob", [P, 2, SKEYS])
        maskS = sb("maskS", [P, SKEYS])
        at[0] = kidx_at
        prod = sb("prod", [P, 3, CO])
        assert at[0] <= kc_at
        at[0] = kc_at
        krow = sb("krow", [P, 3, CC])
        at[0] = tail_at
        wtail = sb("wtail", [P, KD, WIDX])
        assert at[0] <= g_at
        at[0] = shared_a
        probT = sb("probT", [P, 2, 640])
        yc2 = sb("yc2", [P, CO])
        assert at[0] <= g_at
        at[0] = proj_at + A * T * 4
        yc = sb("yc", [P, CT, CO])
        crow = sb("crow", [HIST, 2, CC])
        assert at[0] <= proj_at + Q * T * 4
        at[0] = g_at
        xrow = sb("xrow", [P, 3, D])
        prow = sb("prow", [120, P])
        trow = sb("trow", [TAPS, DEPTH * CC])
        ps = ctx.enter_context(nc.psum_tensor("ps", [P, 8 * 512], F32))

        def bank(b, rows=slice(0, P), lo=0, n=T):
            return ps[rows, 512 * b + lo:512 * b + lo + n]

        const_in = sem("const_in")
        ident_in = sem("ident_in")
        taps_in = sem("taps_in")
        taps_T = sem("taps_T")
        x_in = sem("x_in")
        par_in = sem("par_in")
        par_T = sem("par_T")
        par_ready = sem("par_ready")
        x_T = sem("x_T")
        loaded = [sem("loaded0"), sem("loaded1")]
        hi_ready = sem("hi_ready")
        lo_ready = sem("lo_ready")
        w_used = sem("w_used")
        x_ready = sem("x_ready")
        sq_ready = sem("sq_ready")
        accx_ready = sem("accx_ready")
        sx_done = sem("sx_done")
        root_ready = sem("root_ready")
        r_ready = sem("r_ready")
        hh_ready = sem("hh_ready")
        hl_ready = sem("hl_ready")
        gr_ready = sem("gr_ready")
        silu_ready = sem("silu_ready")
        up_ready = sem("up_ready")
        gt_ready = sem("gt_ready")
        ghi_ready = sem("ghi_ready")
        glo_ready = sem("glo_ready")
        ysq_ready = sem("ysq_ready")
        y_saved = sem("y_saved")
        acc_ready = sem("acc_ready")
        rcol_ready = sem("rcol_ready")
        rb_done = sem("rb_done")
        ss_done = sem("ss_done")
        proj_saved = sem("proj_saved")
        tail_in = sem("tail_in")
        tail_hi = sem("tail_hi")
        tail_lo = sem("tail_lo")
        tail_done = sem("tail_done")
        tail_saved = sem("tail_saved")
        kidx_in = sem("kidx_in")
        kc_in = sem("kc_in")
        vc_in = sem("vc_in")
        state_in = sem("state_in")
        rope_mm = sem("rope_mm")
        rope_prod = sem("rope_prod")
        rope_done = sem("rope_done")
        wi_T = sem("wi_T")
        wrow_ready = sem("wrow_ready")
        relS_ready = sem("relS_ready")
        scoreS_done = sem("scoreS_done")
        kidx_T = sem("kidx_T")
        kiTs_ready = sem("kiTs_ready")
        lgS_done = sem("lgS_done")
        scoreS_saved = sem("scoreS_saved")
        lg_done = sem("lg_done")
        rel_ready = sem("rel_ready")
        rel_used = sem("rel_used")
        glu_r = sem("glu_r")
        sig_ready = sem("sig_ready")
        u_ready = sem("u_ready")
        st_T = sem("st_T")
        st_ready = sem("st_ready")
        crow_T = sem("crow_T")
        crow_ready = sem("crow_ready")
        conv_ready = sem("conv_ready")
        prod_ready = sem("prod_ready")
        pconv_ready = sem("pconv_ready")
        yc_ready = sem("yc_ready")
        mu_done = sem("mu_done")
        dev_ready = sem("dev_ready")
        csq_ready = sem("csq_ready")
        csq_used = sem("csq_used")
        croot_ready = sem("croot_ready")
        cn_ready = sem("cn_ready")
        vrow_T = sem("vrow_T")
        vrow_ready = sem("vrow_ready")
        kcT_done = sem("kcT_done")
        kTs_ready = sem("kTs_ready")
        krow_T = sem("krow_T")
        krow_ready = sem("krow_ready")
        s_done = sem("s_done")
        max_ready = sem("max_ready")
        exp_ready = sem("exp_ready")
        p_ready = sem("p_ready")
        pT_done = sem("pT_done")
        pT_ready = sem("pT_ready")
        pv_done = sem("pv_done")
        att_saved = sem("att_saved")
        rows_out = sem("rows_out")
        yT_done = sem("yT_done")
        yrow_ready = sem("yrow_ready")
        y_out = sem("y_out")
        dve_chain = sem("dve_chain")
        act_chain = sem("act_chain")
        ms_ready = sem("ms_ready")

        w_of = {0: ("ffn1_w_up", "ffn1_w_down"), 1: ("ffn2_w_up", "ffn2_w_down")}

        def strip_view(w, l, r0, rows, c0):
            return ins[w][l, r0:r0 + rows, :].rearrange("(k p) n -> p k n", p=P)[:, :, bass.ds(c0, STRIP)]

        block = ctx.enter_context(nc.Block())

        @block.sync
        def _(sp):
            def load(q, wait, src, n=8):
                sp.wait_ge(lo_ready, wait)
                sp.dma_start(raw[:, q, 0:n, :], src).then_inc(loaded[q], 16)

            def up_step(f, i):
                w = w_of[f % 2][0]
                u = ffn_unit(f)
                load(0, u + 4 * i - 2, strip_view(w, f // 2, 0, D, i * STRIP))
                load(1, u + 4 * i, strip_view(w, f // 2, 0, D, i * STRIP + DFF))

            def down_step(f, i):
                w = w_of[f % 2][1]
                u = ffn_unit(f) + U_UP
                for r in range(6):
                    d, part = divmod(r, 3)
                    load(r % 2, u + 12 * i + 2 * r - 2,
                         strip_view(w, f // 2, part * 8 * P, PARTS[part] * P, (2 * i + d) * STRIP), PARTS[part])

            def in_step(m, i, c0):
                u = mix_unit(m)
                load(0, u + 4 * i - 2, strip_view("w_in", m, 0, D, c0))
                load(1, u + 4 * i, strip_view("w_in", m, 0, D, c0 + STRIP))

            for f in range(2 * DEPTH):
                if f == 0:
                    sp.dma_start(xrow[:, 0:2, :], ins["x_prompt"][0].rearrange("(j p) d -> p j d", p=P)).then_inc(x_in, 16)
                    sp.dma_start(xrow[0:DEC, 2, :], ins["x_sample"][0]).then_inc(x_in, 16)
                    sp.wait_ge(ident_in, 16)
                    sp.dma_start(raw[:, 0], strip_view("ffn1_w_up", 0, 0, D, 0)).then_inc(loaded[0], 16)
                    sp.dma_start(raw[:, 1], strip_view("ffn1_w_up", 0, 0, D, DFF)).then_inc(loaded[1], 16)
                else:
                    up_step(f, 0)
                with sp.Fori(1, UP_STEPS) as i:
                    up_step(f, i)
                with sp.Fori(0, 2) as i:
                    down_step(f, i)
                if f % 2 == 0:
                    m = f // 2
                    in_step(m, 0, QI_COL)
                    in_step(m, 1, 0)
                    sp.wait_ge(x_ready, 8 * (3 * m + 1) + 1)
                    kix = ins["cache_kidx"][m, 0].rearrange("(j p) d -> p j d", p=P)
                    sp.dma_start(kidx[:, :, 0:HD], kix).then_inc(kidx_in, 16)
                    sp.dma_start(kidx[:, :, HD:2 * HD], kix).then_inc(kidx_in, 16)
                    sp.dma_start(kc[:], ins["cache_k"][m, 0].rearrange("(j p) h d -> p j (h d)", p=P)).then_inc(kc_in, 16)
                    sp.dma_start(statein[:], ins["state_conv"][m, 0]).then_inc(state_in, 16)
                    sp.dma_start(vc[:], ins["cache_v"][m, 0].rearrange("(j p) h d -> p j (h d)", p=P)).then_inc(vc_in, 16)
                    with sp.Fori(2, 6) as i:
                        in_step(m, i, (i - 1) * 2 * STRIP)
                    u = mix_unit(m) + U_IN
                    for i in range(2):
                        for q in range(2):
                            load(q, u + 4 * i + 2 * q - 2, strip_view("w_out", m, 0, D, (2 * i + q) * STRIP))
                    sp.wait_ge(vrow_ready, 3 * m + 3)
                    sp.wait_ge(crow_ready, 2 * m + 2)
                    sp.wait_ge(krow_ready, 4 * m + 4)
                    sp.dma_start(prompt_conv[m, 0], crow[:, 0, :]).then_inc(rows_out, 16)
                    sp.dma_start(sample_conv[m, 0], crow[:, 1, :]).then_inc(rows_out, 16)
                    for buf, pr, sa in ((vrow, prompt_v, sample_v), (krow, prompt_k, sample_k)):
                        sp.dma_start(pr[m, 0].rearrange("(j p) h d -> p j (h d)", p=P), buf[:, 0:2, :]).then_inc(rows_out, 16)
                        sp.dma_start(sa[m, 0].rearrange("p h d -> p (h d)"), buf[0:DEC, 2, :]).then_inc(rows_out, 16)
                    sp.dma_start(prompt_ki[m, 0].rearrange("(j p) d -> p j d", p=P), kirow[:, 0:2, :]).then_inc(rows_out, 16)
                    sp.dma_start(sample_ki[m, 0], kirow[0:DEC, 2, :]).then_inc(rows_out, 16)
            for half in range(2):
                cols = slice(half * 512, (half + 1) * 512)
                for tt, (t0, n) in enumerate(TOK):
                    sp.wait_ge(yrow_ready, 3 * half + tt + 1)
                    dst = y_prompt[0, t0:t0 + n, cols] if tt < 2 else y_sample[0, :, cols]
                    sp.dma_start(dst, xrow[0:n, tt, cols]).then_inc(y_out, 16)
            sp.wait_ge(y_out, 16 * 6)
            sp.wait_ge(rows_out, 16 * 8 * DEPTH)

        @block.scalar
        def _(act):
            n_chain = [0]

            def link(ins_):
                n_chain[0] += 1
                ins_.then_inc(act_chain, 1)
                act.wait_ge(act_chain, n_chain[0])

            def split_hi(unit, raw_slot, split_slot, half, raw_count, n=8, old=True):
                act.wait_ge(loaded[raw_slot], 16 * raw_count)
                if old:
                    act.wait_ge(w_used, unit - 3)
                act.activation(whi[:, split_slot, 0:n, :], raw[:, raw_slot, 0:n, half * P:(half + 1) * P],
                               ACT.Copy).then_inc(hi_ready, 1)

            def split_quad(u0, i, rel, down_raw=None, old=True):
                q, half = divmod(rel, 2)
                split_hi(u0 + 4 * i + rel, q, rel, half, u0 // 4 + i + 1, 8, old)

            def split_x(s, hq, g):
                for c in range(KD):
                    act.wait_ge(x_ready, 8 * s + c + 1)
                    act.activation(hh[:, c, :], x[:, c, :], ACT.Copy, scale=par[:, g + c:g + c + 1]).then_inc(hh_ready, 1)
                    if c >= 2:
                        act.wait_ge(accx_ready, 10 * s + c + 1)
                    act.activation(sq[:, c % 2, :], x[:, c, :], ACT.Square).then_inc(sq_ready, 1)

            def pre_root(s):
                act.wait_ge(sx_done, s + 1)
                act.activation(root[:], bank(6), ACT.Sqrt, bias=epsc[:, 0:1], scale=1.0 / D).then_inc(root_ready, 1)

            def post_root(s, half_step):
                k = 4.0 if half_step else 1.0
                act.wait_ge(ss_done, s + 1)
                act.activation(rcol[:], ps[:].rearrange("p (b n) -> p b n", b=8)[:, 5:8, 0], ACT.Sqrt,
                               bias=epsc[:, 1:2] if half_step else epsc[:, 0:1], scale=k / D).then_inc(root_ready, 1)

            def save_y(s, c, b, slot, unit):
                act.wait_ge(w_used, unit + 1)
                act.wait_ge(acc_ready, 9 * s + c + 1)
                act.activation(ysq[:, slot * T:(slot + 1) * T], bank(b), ACT.Square).then_inc(ysq_ready, 1)
                act.activation(y[:, bass.ds(c * T, T)], bank(b), ACT.Copy).then_inc(y_saved, 1)

            def sqrt_table():
                link(act.activation(stat[:, 79:80], epsc[:, 0:1], ACT.Sqrt))

            def ffn(f, s):
                u = ffn_unit(f)

                def up_step(i, first):
                    if first:
                        split_quad(u + 4, i, 0)
                        split_quad(u + 4, i, 1)
                        pre_root(s)
                    for j in range(2):
                        act.wait_ge(gr_ready, KF * f + 2 * i + j + 1)
                        act.activation(sil[:, j * T:(j + 1) * T], sil[:, j * T:(j + 1) * T],
                                       ACT.Silu).then_inc(silu_ready, 1)
                        if not first:
                            split_quad(u + 4, i, j)
                    for j in range(2):
                        split_quad(u + 4, i, 2 + j)
                        act.wait_ge(gt_ready, KF * f + 2 * i + j + 1)
                        act.activation(ghi[:, bass.ds((2 * i + j) * T, T)], gt[:, j * T:(j + 1) * T],
                                       ACT.Copy).then_inc(ghi_ready, 1)

                up_step(0, True)
                with act.Fori(1, UP_STEPS) as i:
                    up_step(i, False)
                sqrt_table()
                ud = u + U_UP

                def ahead(i, j, last):
                    jj = j + 4
                    if jj < 12:
                        r, half = divmod(jj, 2)
                        split_hi(ud + 12 * i + jj, r % 2, jj % 4, half, ud // 4 + 3 * i + r // 2 + 1, PARTS[r % 3])
                    elif not last:
                        r, half = divmod(jj - 12, 2)
                        split_hi(ud + 12 * i + jj, r % 2, jj % 4, half, ud // 4 + 3 * i + 3 + r // 2 + 1, 8)

                def down_step(i, last):
                    for d in range(2):
                        for j in range(6):
                            if j >= 4:
                                save_y(s, 4 * i + 2 * d + j - 4, 2 * d + j - 4, j - 4, ud + 12 * i + 6 * d + j)
                            ahead(i, 6 * d + j, last)

                down_step(0, False)
                down_step(1, f == 2 * DEPTH - 1)
                post_root(s, True)

            def mixer(m, s):
                u = mix_unit(m)
                act.wait_ge(tail_in, 48 * (m + 1))
                act.activation(wthi[:], wtail[:], ACT.Copy).then_inc(tail_hi, 1)

                def in_step(i, first):
                    for j in range(4):
                        act.wait_ge(w_used, u + 4 * i + j + 1)
                        act.activation(proj[:, bass.ds((4 * i + j) * T, T)], bank(j), ACT.Copy).then_inc(proj_saved, 1)
                        split_quad(u + 4, i, j)
                        if first and j == 1:
                            pre_root(s)

                in_step(0, True)
                act.wait_ge(tail_done, 2 * m + 1)
                act.activation(kiT[:], bank(4), ACT.Copy).then_inc(tail_saved, 1)
                act.wait_ge(tail_done, 2 * m + 2)
                act.activation(wiT[:], bank(5, slice(0, HEADS)), ACT.Copy).then_inc(tail_saved, 1)
                in_step(1, False)
                act.wait_ge(kidx_T, m + 1)
                act.activation(kiTs[:, 0:PAST], bank(5, n=PAST), ACT.Copy).then_inc(kiTs_ready, 1)
                act.wait_ge(rope_done, 13 * m + 5)
                act.activation(kiTs[:, PAST:SKEYS], kiT[:, SEQ:T], ACT.Copy).then_inc(kiTs_ready, 1)
                for hp in range(4):
                    act.wait_ge(kcT_done, 4 * m + hp + 1)
                    act.activation(kTs[:, hp, 0:PAST], bank(hp, n=PAST), ACT.Copy).then_inc(kTs_ready, 1)
                for h in range(HEADS):
                    if h == 4:
                        for g in range(2):
                            act.wait_ge(lgS_done, 2 * m + g + 1)
                            act.activation(relS[:, g, :], bank(2 * g, n=SKEYS), ACT.Relu,
                                           scale=HD ** -0.5).then_inc(relS_ready, 1)
                    act.wait_ge(lg_done, 8 * m + h + 1)
                    if h >= 2:
                        act.wait_ge(rel_used, 8 * m + h - 1)
                    act.activation(relP[:, h % 2, :], bank(6 + h % 2, n=384), ACT.Relu,
                                   scale=HD ** -0.5).then_inc(rel_ready, 1)
                with act.Fori(2, 4) as i:
                    in_step(i, False)
                act.wait_ge(st_T, m + 1)
                act.activation(ext[:, :, HIST + SEQ:HIST + SEQ + HIST],
                               bank(5, n=CT * HIST).rearrange("p (c t) -> p c t", c=CT), ACT.Copy).then_inc(st_ready, 1)
                act.wait_ge(glu_r, m + 1)
                act.activation(proj[:, G * T:Q * T], proj[:, G * T:Q * T], ACT.Sigmoid).then_inc(sig_ready, 1)

                def products(first, last_):
                    for j in range(first, min(last_, len(POOL_STEPS))):
                        ct, k = POOL_STEPS[j]
                        c = (m * CT + ct) * TAPS + k
                        if j == 0:
                            act.wait_ge(u_ready, m + 1)
                            ins_ = act.activation(yc[:, ct, :], ext[:, ct, 0:CO], ACT.Identity, scale=taps[:, c:c + 1],
                                                  bias=par[:, cvec(0, m, ct):cvec(0, m, ct) + 1])
                        elif j == TAPS:
                            ins_ = act.activation(yc2[:], ext[:, ct, k:k + CO], ACT.Copy, scale=taps[:, c:c + 1])
                        else:
                            n = j if j < TAPS else j - 1
                            if n > 3:
                                act.wait_ge(pconv_ready, m * POOL_SUMS + n - 3)
                            ins_ = act.activation(prod[:, n % 3, :], ext[:, ct, k:k + CO], ACT.Copy,
                                                  scale=taps[:, c:c + 1])
                        ins_.then_inc(prod_ready, 1)

                in_step(4, False)
                products(0, 4)
                in_step(5, False)
                for tt, (t0, n) in enumerate(TOK):
                    act.wait_ge(vrow_T, 3 * m + tt + 1)
                    act.activation(vrow[0:n, tt, :], bank(tt, slice(0, n), n=CC), ACT.Copy,
                                   scale=rtok[0:n, tt:tt + 1]).then_inc(vrow_ready, 1)
                for hp in range(4):
                    act.wait_ge(rope_done, 13 * m + 5 + 4 + hp + 1)
                    act.activation(kTs[:, hp, PAST:SKEYS], proj[:, (K + hp) * T + SEQ:(K + hp + 1) * T],
                                   ACT.Copy).then_inc(kTs_ready, 1)

                def softmax_exp(n):
                    act.wait_ge(max_ready, 10 * m + n + 1)
                    spans = [(0, SKEYS)] if n < 2 else [(0, P), (P, 384)]
                    for j, (a, b) in enumerate(spans):
                        last = act.activation(prob[:, n % 2, a:b], prob[:, n % 2, a:b], ACT.Exp,
                                              bias=stat[:, 8 * n + 2 + j:8 * n + 3 + j],
                                              accum_out=stat[:, 8 * n + 4 + j:8 * n + 5 + j])
                    last.then_inc(exp_ready, 1)

                def save_pT(n):
                    act.wait_ge(pT_done, 10 * m + n + 1)
                    if n >= 2:
                        act.wait_ge(pv_done, 10 * m + n - 1)
                    if n < 2:
                        act.activation(probT[:, n % 2, 0:512], bank(4, n=512), ACT.Copy)
                        act.activation(probT[0:DEC, n % 2, 512:640], bank(5, slice(0, DEC), n=P),
                                       ACT.Copy).then_inc(pT_ready, 1)
                    else:
                        act.activation(probT[:, n % 2, 0:384], bank(4 + n % 2, n=384), ACT.Copy).then_inc(pT_ready, 1)

                def save_att(n):
                    if n == 1:
                        act.wait_ge(pv_done, 10 * m + 2)
                        act.activation(y[:, 4 * T:8 * T].rearrange("p (c t) -> p c t", c=4)[:, :, SEQ:T],
                                       bank(7, n=P).rearrange("p (c t) -> p c t", c=4), ACT.Copy).then_inc(att_saved, 1)
                    elif n % 2:
                        hp = (n - 2) // 2
                        act.wait_ge(pv_done, 10 * m + n + 1)
                        link(act.activation(y[:, (4 + hp) * T:(4 + hp) * T + SEQ], bank(6 + hp % 2, n=SEQ), ACT.Copy))
                        act.activation(hh[:, 4 + hp, :], y[:, (4 + hp) * T:(5 + hp) * T], ACT.Copy).then_inc(hh_ready, 1)

                products(4, 7)
                softmax_exp(0)
                for n in range(10):
                    if n < 9:
                        softmax_exp(n + 1)
                    save_pT(n)
                    products(7 + PROD_ITEM * n, 7 + PROD_ITEM * (n + 1))
                    if n >= 1:
                        save_att(n - 1)
                    if n == 7:
                        for ct in range(CT):
                            act.wait_ge(dev_ready, 4 * m + ct + 1)
                            if ct >= 2:
                                act.wait_ge(csq_used, 4 * m + ct - 1)
                            act.activation(y[:, (ct % 2) * CO:(ct % 2 + 1) * CO], yc[:, ct, :],
                                           ACT.Square).then_inc(csq_ready, 1)
                    if n == 8:
                        act.wait_ge(csq_used, 4 * m + 4)
                        act.activation(cinv[:], bank(3, n=CO), ACT.Sqrt, bias=epsc[:, 0:1],
                                       scale=1.0 / CC).then_inc(croot_ready, 1)
                save_att(9)
                for ct in range(CT):
                    act.wait_ge(cn_ready, 4 * m + ct + 1)
                    for src, dst, n in ((0, 0, SEQ), (SAMPLE_AT, SEQ, DEC)):
                        last = act.activation(y[:, ct * T + dst:ct * T + dst + n], yc[:, ct, src:src + n], ACT.Silu,
                                              bias=par[:, cvec(2, m, ct):cvec(2, m, ct) + 1],
                                              scale=par[:, cvec(1, m, ct):cvec(1, m, ct) + 1])
                    link(last)
                    act.activation(hh[:, ct, :], y[:, ct * T:(ct + 1) * T], ACT.Copy).then_inc(hh_ready, 1)
                sqrt_table()
                for g in range(2):
                    act.wait_ge(crow_T, 2 * m + g + 1)
                    act.activation(crow[:, g, :], bank(2 * g + 1, slice(0, HIST), n=CC), ACT.Copy).then_inc(crow_ready, 1)
                for tt, b in enumerate((0, 2, 1)):
                    n = TOK[tt][1]
                    act.wait_ge(krow_T, 4 * m + tt + 1)
                    act.activation(krow[0:n, tt, :], bank(b, slice(0, n), n=CC), ACT.Copy).then_inc(krow_ready, 1)
                act.wait_ge(krow_T, 4 * m + 4)
                for tt, (t0, n) in enumerate(TOK):
                    last = act.activation(kirow[0:n, tt, :], bank(3, slice(0, n), HD * tt, HD), ACT.Copy)
                last.then_inc(krow_ready, 1)
                uo = u + U_IN
                for i in range(2):
                    for j in range(4):
                        if i == 0:
                            split_quad(uo + 4, i, j)
                        save_y(s, 4 * i + j, j if i else 4 + j, j % 2, uo + 4 * i + j)
                        if i:
                            split_quad(uo + 4, i, j)
                post_root(s, False)

            act.dma_start(ident[:], consts["ident"]).then_inc(ident_in, 16)
            for n, name in enumerate(("ffn1_norm_pre", "ffn1_norm_post", "mix_norm_pre", "mix_norm_post",
                                      "ffn2_norm_pre", "ffn2_norm_post")):
                r = gain(n, 0, 0)
                act.dma_start(prow[r:r + DEPTH * KD, :], ins[name].rearrange("l (c p) -> (l c) p", p=P)).then_inc(par_in, 16)
            for n, name in enumerate(("conv_b", "conv_ln_g", "conv_ln_b")):
                r = cvec(n, 0, 0)
                act.dma_start(prow[r:r + DEPTH * CT, :], ins[name].rearrange("l (c p) -> (l c) p", p=P)).then_inc(par_in, 16)
            act.wait_ge(par_T, 1)
            act.activation(par[:], bank(6, n=120), ACT.Copy).then_inc(par_ready, 1)
            act.wait_ge(par_ready, 1)
            for c in range(KD):
                act.wait_ge(x_ready, c + 1)
                act.activation(hh[:, c, :], x[:, c, :], ACT.Copy, scale=par[:, c:c + 1]).then_inc(hh_ready, 1)
            act.wait_ge(ms_ready, 1)
            for rel in range(4):
                split_quad(0, 0, rel, old=False)
            for c in range(KD):
                if c >= 2:
                    act.wait_ge(accx_ready, c + 1)
                act.activation(sq[:, c % 2, :], x[:, c, :], ACT.Square).then_inc(sq_ready, 1)
            act.wait_ge(taps_T, 1)
            act.activation(taps[:], bank(1, n=DEPTH * CT * TAPS), ACT.Copy).then_inc(par_ready, 1)
            for l in range(DEPTH):
                if l:
                    split_x(3 * l, 4 * l, gain(0, l, 0))
                ffn(2 * l, 3 * l)
                split_x(3 * l + 1, 4 * l + 1, gain(2, l, 0))
                mixer(l, 3 * l + 1)
                split_x(3 * l + 2, 4 * l + 3, gain(4, l, 0))
                act.wait_ge(rows_out, 16 * 8 * (l + 1))
                ffn(2 * l + 1, 3 * l + 2)
            for n in range(6):
                half, tt = divmod(n, 3)
                act.wait_ge(yT_done, n + 1)
                k = TOK[tt][1]
                act.activation(xrow[0:k, tt, half * 512:(half + 1) * 512], bank(n, slice(0, k), n=512),
                               ACT.Copy).then_inc(yrow_ready, 1)

        @block.vector
        def _(dve):
            n_chain = [0]

            def link(ins_):
                n_chain[0] += 1
                ins_.then_inc(dve_chain, 1)
                dve.wait_ge(dve_chain, n_chain[0])

            def split_lo(unit, raw_slot, split_slot, half, n=8):
                dve.wait_ge(hi_ready, unit + 1)
                cols = slice(half * P, (half + 1) * P)
                dve.tensor_tensor(wlo[:, split_slot, 0:n, :], raw[:, raw_slot, 0:n, cols],
                                  whi[:, split_slot, 0:n, :].bitcast(F32), ALU.subtract).then_inc(lo_ready, 1)

            def split_quad(u0, i, rel):
                q, half = divmod(rel, 2)
                split_lo(u0 + 4 * i + rel, q, rel, half)

            def low_x(hq, g, c):
                dve.wait_ge(hh_ready, 8 * hq + c + 1)
                dve.scalar_tensor_tensor(out=hl[:, c, :], in0=x[:, c, :], scalar=par[:, g + c:g + c + 1],
                                         in1=hh[:, c, :].bitcast(F32), op0=ALU.mult, op1=ALU.subtract).then_inc(hl_ready, 1)

            def rms_x(s):
                dve.wait_ge(root_ready, 2 * s + 1)
                dve.reciprocal(rinv[:], root[:]).then_inc(r_ready, 1)
                dve.wait_ge(r_ready, s + 1)

            def clear_acc(s):
                dve.memset(acc[:], 0.0).then_inc(acc_ready, 2)

            def add_sq(s, c, slot):
                dve.wait_ge(ysq_ready, 8 * s + c + 1)
                dve.wait_ge(acc_ready, 9 * s + c + 2)
                dve.tensor_tensor(acc[:], acc[:], ysq[:, slot * T:(slot + 1) * T], ALU.add).then_inc(acc_ready, 1)

            def residual(s, g, hq_next, g_next):
                dve.wait_ge(root_ready, 2 * s + 2)
                dve.reciprocal(rcol[:], rcol[:]).then_inc(rcol_ready, 1)
                dve.wait_ge(y_saved, 8 * s + 8)
                dve.wait_ge(rb_done, s + 1)
                chain = {}

                def gained(c):
                    if c >= 2:
                        dve.wait_ge(x_ready, 8 * (s + 1) + c - 1)
                    dve.scalar_tensor_tensor(out=upd[:, (c % 2) * T:(c % 2 + 1) * T], in0=y[:, c * T:(c + 1) * T],
                                             scalar=par[:, g + c:g + c + 1], in1=bank(6, lo=8),
                                             op0=ALU.mult, op1=ALU.mult).then_inc(dve_chain, 1)
                    n_chain[0] += 1
                    chain[c] = n_chain[0]

                def add(c):
                    dve.wait_ge(dve_chain, chain[c])
                    dve.tensor_tensor(x[:, c, :], x[:, c, :], upd[:, (c % 2) * T:(c % 2 + 1) * T],
                                      ALU.add).then_inc(x_ready, 1)

                gained(0)
                if hq_next is not None:
                    add(0)
                    gained(1)
                    low_x(hq_next, g_next, 0)
                    add(1)
                    for c in range(2, KD):
                        gained(c)
                        add(c)
                        low_x(hq_next, g_next, c - 1)
                    low_x(hq_next, g_next, KD - 1)
                else:
                    for c in range(KD):
                        if c < KD - 1:
                            gained(c + 1)
                        add(c)

            def ffn(f, s, g, hq_next, g_next):
                u = ffn_unit(f)

                def up_step(i, first):
                    if first:
                        split_quad(u + 4, i, 0)
                        split_quad(u + 4, i, 1)
                        rms_x(s)
                    b0 = (4, 5, 7, 3) if first else (0, 1, 2, 3)
                    for j in range(2):
                        dve.wait_ge(w_used, u + 4 * i + j + 1)
                        dve.tensor_tensor(sil[:, j * T:(j + 1) * T], bank(b0[j]), rinv[:], ALU.mult).then_inc(gr_ready, 1)
                        if not first:
                            split_quad(u + 4, i, j)

                    def low(j):
                        dve.wait_ge(ghi_ready, KF * f + 2 * i + j + 1)
                        dve.tensor_tensor(glo[:, bass.ds((2 * i + j) * T, T)], gt[:, j * T:(j + 1) * T],
                                          ghi[:, bass.ds((2 * i + j) * T, T)].bitcast(F32),
                                          ALU.subtract).then_inc(glo_ready, 1)
                    for j in range(2):
                        dve.wait_ge(w_used, u + 4 * i + 2 + j + 1)
                        if not first:
                            dve.wait_ge(glo_ready, KF * f + 2 * i + j - 1)
                        dve.tensor_tensor(gt[:, j * T:(j + 1) * T], bank(b0[2 + j]), rinv[:],
                                          ALU.mult).then_inc(up_ready, 1)
                        dve.wait_ge(up_ready, KF * f + 2 * i + j + 1)
                        dve.wait_ge(silu_ready, KF * f + 2 * i + j + 1)
                        dve.tensor_tensor(gt[:, j * T:(j + 1) * T], gt[:, j * T:(j + 1) * T],
                                          sil[:, j * T:(j + 1) * T], ALU.mult).then_inc(gt_ready, 1)
                        split_quad(u + 4, i, 2 + j)
                        low(j)

                up_step(0, True)
                with dve.Fori(1, UP_STEPS) as i:
                    up_step(i, False)
                ud = u + U_UP
                clear_acc(s)

                def down_step(i, last):
                    for d in range(2):
                        for j in range(6):
                            c = 4 * i + 2 * d + j - 4
                            if j >= 4 and c < KD - 1:
                                add_sq(s, c, j - 4)
                            jj = 6 * d + j + 4
                            r, half = divmod(jj % 12, 2)
                            if jj < 12 or i == 0 or not (last or jj == 15):
                                split_lo(ud + 12 * i + jj, r % 2, jj % 4, half, PARTS[r % 3] if jj < 12 else 8)

                down_step(0, False)
                down_step(1, f == 2 * DEPTH - 1)
                residual(s, g, hq_next, g_next)

            def ropes(m, k0, tiles, banks):
                def products(k):
                    dve.wait_ge(rope_mm, 13 * m + k0 + k + 1)
                    if k0 + k >= 3:
                        dve.wait_ge(rope_done, 13 * m + k0 + k - 2)
                    dve.tensor_tensor(ropa[:, (k0 + k) % 3, :], tiles[k], cosR[:], ALU.mult).then_inc(rope_prod, 1)
                    dve.tensor_tensor(ropb[:, (k0 + k) % 3, :], bank(banks[k]), sinR[:], ALU.mult).then_inc(rope_prod, 1)

                def total(k):
                    dve.wait_ge(rope_prod, 2 * (13 * m + k0 + k + 1))
                    dve.tensor_tensor(tiles[k], ropa[:, (k0 + k) % 3, :], ropb[:, (k0 + k) % 3, :],
                                      ALU.add).then_inc(rope_done, 1)
                for k in range(len(tiles)):
                    products(k)
                    if k:
                        total(k - 1)
                total(len(tiles) - 1)

            def top_k(lists):
                steps = []
                for n, parts in enumerate(lists):
                    steps.append([(n, rows, a, b) for rows, a, b, k in parts for _ in range(k // 8)])
                mine = [0] * len(lists)
                for r in range(max(len(st) for st in steps)):
                    for pick in range(2):
                        for n, rows, a, b in (st[r] for st in steps if r < len(st)):
                            if mine[n]:
                                dve.wait_ge(dve_chain, mine[n])
                            if pick == 0:
                                ins_ = dve.max(m8[rows, 8 * n:8 * n + 8], score[rows, a:b])
                            else:
                                ins_ = dve.match_replace(score[rows, a:b], m8[rows, 8 * n:8 * n + 8],
                                                         score[rows, a:b], TAKEN)
                            ins_.then_inc(dve_chain, 1)
                            n_chain[0] += 1
                            mine[n] = n_chain[0]
                dve.wait_ge(dve_chain, n_chain[0])

            def mixer(m, s, g, hq_next, g_next):
                dve.wait_ge(tail_hi, m + 1)
                dve.tensor_tensor(wtlo[:], wtail[:], wthi[:].bitcast(F32), ALU.subtract).then_inc(tail_lo, 1)
                rms_x(s)
                dve.wait_ge(const_in, 16 * 4)
                dve.tensor_tensor(cosR[:], cosT[:], rinv[:], ALU.mult)
                link(dve.tensor_tensor(sinR[:], sinT[:], rinv[:], ALU.mult))
                ropes(m, 0, [proj[:, (QI + k) * T:(QI + k + 1) * T] for k in range(4)] + [kiT[:]], (6, 7, 6, 7, 6))
                dve.wait_ge(wi_T, m + 1)
                dve.tensor_copy(rtok[:, 0:2], bank(4, lo=24, n=2))
                link(dve.tensor_copy(rtok[0:DEC, 2:3], bank(4, slice(0, DEC), 26, 1)))
                for tt, (t0, n) in enumerate(TOK):
                    last = dve.tensor_scalar(wrow[0:n, 8 * tt:8 * tt + 8], bank(4, slice(0, n), 8 * tt, 8),
                                             rtok[0:n, tt:tt + 1], HEADS ** -0.5, ALU.mult, ALU.mult)
                link(last)
                for h in range(HEADS):
                    last = dve.tensor_copy(wS[32 * (h % 4):32 * (h % 4) + 32, h // 4:h // 4 + 1],
                                           wrow[0:DEC, 16 + h:17 + h])
                link(last)
                dve.tensor_scalar(wdiag[:, 0, :], stack[:], wS[:, 0:1], None, ALU.mult)
                dve.tensor_scalar(wdiag[:, 1, :], stack[:], wS[:, 1:2], None, ALU.mult).then_inc(wrow_ready, 1)
                for h in range(HEADS):
                    dve.wait_ge(rel_ready, 8 * m + h + 1)
                    for a, b, w0 in ((0, P, 0), (P, 384, 8)):
                        src = relP[:, h % 2, a:b]
                        w = wrow[:, w0 + h:w0 + h + 1]
                        if h == 0:
                            last = dve.tensor_scalar(score[:, a:b], src, w, None, ALU.mult)
                        else:
                            last = dve.scalar_tensor_tensor(out=score[:, a:b], in0=src, scalar=w,
                                                            in1=score[:, a:b], op0=ALU.mult, op1=ALU.add)
                    last.then_inc(rel_used, 1)
                    dve.wait_ge(rel_used, 8 * m + h + 1)
                dve.memset(score[0:CHUNK, CHUNK:P], BARRED)
                dve.memset(score[0:CHUNK, P + 3 * CHUNK:P + 4 * CHUNK], BARRED)
                dve.wait_ge(scoreS_done, m + 1)
                dve.tensor_copy(score[0:DEC, 384:928], bank(4, slice(0, DEC), n=SKEYS)).then_inc(scoreS_saved, 1)
                dve.wait_ge(scoreS_saved, m + 1)
                top_k([[(slice(0, DEC), 384, 928, TOPK_S)],
                       [(slice(0, P), 0, P, TOPK_P), (slice(0, P), P, 384, TOPK_P)]])
                rb = rinv[:].rearrange("p (o t) -> p o t", o=1).to_broadcast([P, CT, T])
                pa = proj[:, A * T:G * T].rearrange("p (c t) -> p c t", c=CT)
                pg = proj[:, G * T:Q * T].rearrange("p (c t) -> p c t", c=CT)
                dve.wait_ge(proj_saved, 24 * m + 12)
                dve.tensor_tensor(pg, pg, rb, ALU.mult).then_inc(glu_r, 1)
                dve.tensor_tensor(pa, pa, rb, ALU.mult)
                for j in range(4):
                    dve.tensor_scalar(maskS[32 * j:32 * j + 32, :], score[0:DEC, 384:928], TAKEN, NEG,
                                      ALU.not_equal, ALU.mult)
                link(dve.tensor_scalar(score[:, 0:384], score[:, 0:384], TAKEN, NEG, ALU.not_equal, ALU.mult))
                dve.wait_ge(sig_ready, m + 1)
                if m:
                    dve.wait_ge(crow_T, 2 * m)
                dve.tensor_tensor(ext[:, :, HIST:HIST + SEQ], pa[:, :, 0:SEQ], pg[:, :, 0:SEQ], ALU.mult)
                dve.tensor_tensor(ext[:, :, EXT - DEC:EXT], pa[:, :, SEQ:T], pg[:, :, SEQ:T],
                                  ALU.mult).then_inc(u_ready, 1)
                dve.wait_ge(u_ready, m + 1)
                dve.wait_ge(st_ready, m + 1)

                def conv(first, last_):
                    for j in range(first, min(last_, len(DVE_STEPS))):
                        ct, k = DVE_STEPS[j]
                        w = taps[:, (m * CT + ct) * TAPS + k:(m * CT + ct) * TAPS + k + 1]
                        src = ext[:, ct, k:k + CO]
                        if k == 0:
                            ins_ = dve.tensor_scalar(yc[:, ct, :], src, w, par[:, cvec(0, m, ct):cvec(0, m, ct) + 1],
                                                     ALU.mult, ALU.add)
                        else:
                            dve.wait_ge(conv_ready, m * len(DVE_STEPS) + DVE_STEPS.index((ct, k - 1)) + 1)
                            ins_ = dve.scalar_tensor_tensor(out=yc[:, ct, :], in0=src, scalar=w, in1=yc[:, ct, :],
                                                            op0=ALU.mult, op1=ALU.add)
                        ins_.then_inc(conv_ready, 1)

                conv(0, CONV_FIRST)
                ropes(m, 5, [proj[:, (Q + k) * T:(Q + k + 1) * T] for k in range(4)], (4, 5, 6, 7))
                conv(CONV_FIRST, CONV_EARLY)
                ropes(m, 9, [proj[:, (K + k) * T:(K + k + 1) * T] for k in range(4)], (4, 5, 6, 7))

                def softmax_max(n):
                    dve.wait_ge(s_done, 10 * m + n + 1)
                    if n >= 2:
                        dve.wait_ge(pT_done, 10 * m + n - 1)
                    spans = [(0, SKEYS)] if n < 2 else [(0, P), (P, 384)]
                    c = 8 * n
                    for j, (a, b) in enumerate(spans):
                        logits = ps[:, 1024 * (n % 2) + a:1024 * (n % 2) + b]
                        mask = maskS[:] if n < 2 else score[:, a:b]
                        link(dve.tensor_tensor_reduce(prob[:, n % 2, a:b], logits, mask, HD ** -0.5, -3.0e38,
                                                      ALU.add, ALU.max, stat[:, c + j:c + j + 1]))
                    k = len(spans)
                    dve.tensor_scalar(stat[:, c + 2:c + 2 + k], stat[:, c:c + k], -1.0, None,
                                      ALU.mult).then_inc(max_ready, 1)

                def softmax_norm(n):
                    dve.wait_ge(exp_ready, 10 * m + n + 1)
                    spans = [(0, SKEYS)] if n < 2 else [(0, P), (P, 384)]
                    k, c = len(spans), 8 * n
                    link(dve.reciprocal(stat[:, c + 6:c + 6 + k], stat[:, c + 4:c + 4 + k]))
                    for j, (a, b) in enumerate(spans):
                        last = dve.tensor_scalar(prob[:, n % 2, a:b], prob[:, n % 2, a:b],
                                                 stat[:, c + 6 + j:c + 7 + j], None, ALU.mult)
                    last.then_inc(p_ready, 1)

                def low_mix(k, c):
                    dve.wait_ge(hh_ready, 8 * (4 * m + 2) + k + 1)
                    dve.tensor_tensor(hl[:, c, :], y[:, c * T:(c + 1) * T], hh[:, c, :].bitcast(F32),
                                      ALU.subtract).then_inc(hl_ready, 1)

                conv(CONV_EARLY, CONV_LATE)
                softmax_max(0)
                for n in range(10):
                    if n < 9:
                        softmax_max(n + 1)
                    softmax_norm(n)
                    if n <= 6:
                        conv(CONV_LATE + n * CONV_ITEM, CONV_LATE + (n + 1) * CONV_ITEM if n < 6 else len(DVE_STEPS))
                    if n == 6:
                        dve.wait_ge(conv_ready, (m + 1) * len(DVE_STEPS))
                        dve.wait_ge(pconv_ready, (m + 1) * POOL_SUMS)
                        dve.tensor_tensor(yc[:, 2, :], yc[:, 2, :], yc2[:], ALU.add).then_inc(yc_ready, 1)
                    if n == 7:
                        dve.wait_ge(mu_done, m + 1)
                        for ct in range(CT):
                            dve.scalar_tensor_tensor(out=yc[:, ct, :], in0=bank(1, n=CO), scalar=-1.0 / CC,
                                                     in1=yc[:, ct, :], op0=ALU.mult, op1=ALU.add).then_inc(dev_ready, 1)
                    if n in (5, 7, 9):
                        low_mix((n - 5) // 2, 4 + (n - 5) // 2)
                dve.wait_ge(croot_ready, m + 1)
                link(dve.reciprocal(cinv[:], cinv[:]))
                for ct in range(CT):
                    dve.tensor_tensor(yc[:, ct, :], yc[:, ct, :], cinv[:], ALU.mult).then_inc(cn_ready, 1)
                low_mix(3, 7)
                for ct in range(CT):
                    low_mix(4 + ct, ct)
                clear_acc(s)
                for c in range(KD - 1):
                    add_sq(s, c, c % 2)
                residual(s, g, hq_next, g_next)

            dve.memset(ones[:], 1.0)
            dve.memset(epsc[:, 0:1], EPS)
            dve.memset(epsc[:, 1:2], 4.0 * EPS)
            dve.memset(ext[:, :, 0:HIST], 0.0).then_inc(ms_ready, 1)
            for c in range(KD):
                dve.wait_ge(x_T, c + 1)
                dve.tensor_copy(x[:, c, :], bank(c % 4)).then_inc(x_ready, 1)
            dve.wait_ge(par_ready, 1)
            dve.wait_ge(x_ready, KD)
            for c in range(KD):
                low_x(0, gain(0, 0, 0), c)
            for rel in range(4):
                split_quad(0, 0, rel)
            for l in range(DEPTH):
                ffn(2 * l, 3 * l, gain(1, l, 0), 4 * l + 1, gain(2, l, 0))
                mixer(l, 3 * l + 1, gain(3, l, 0), 4 * l + 3, gain(4, l, 0))
                dve.wait_ge(lo_ready, ffn_unit(2 * l + 1) + 4)
                following = (4 * l + 4, gain(0, l + 1, 0)) if l < DEPTH - 1 else (None, None)
                ffn(2 * l + 1, 3 * l + 2, gain(5, l, 0), *following)

        @block.gpsimd
        def _(pool):
            def split_lo(unit, raw_slot, split_slot, half):
                pool.wait_ge(hi_ready, unit + 1)
                cols = slice(half * P, (half + 1) * P)
                pool.tensor_tensor(wlo[:, split_slot, :, :], raw[:, raw_slot, :, cols],
                                   whi[:, split_slot, :, :].bitcast(F32), ALU.subtract).then_inc(lo_ready, 1)

            def step(u0, i):
                for rel in range(4):
                    split_lo(u0 + 4 * i + rel, rel // 2, rel, rel % 2)

            def sum_x(s):
                pool.wait_ge(sq_ready, 8 * s + 1)
                pool.memset(accx[:], 0.0).then_inc(accx_ready, 2)
                for c in range(KD):
                    pool.wait_ge(sq_ready, 8 * s + c + 1)
                    pool.wait_ge(accx_ready, 10 * s + c + 2)
                    pool.tensor_tensor(accx[:], accx[:], sq[:, c % 2, :], ALU.add).then_inc(accx_ready, 1)

            def split_last(u):
                pool.wait_ge(lo_ready, u + 3)
                split_lo(u + 3, 1, 3, 1)

            pool.dma_start(trow[:].rearrange("k (l c) -> k l c", l=DEPTH),
                           ins["conv_w"].rearrange("l k c -> k l c")).then_inc(taps_in, 16)
            for name, dst in (("swap", swap), ("cosT", cosT), ("sinT", sinT), ("stack", stack)):
                pool.dma_start(dst[:], consts[name]).then_inc(const_in, 16)
            sum_x(0)
            for m in range(DEPTH):
                u = mix_unit(m)
                pool.wait_ge(glo_ready, KF * (2 * m + 1))
                w_in = ins["w_in"][m].rearrange("(k p) n -> p k n", p=P)
                for d, (c0, n) in ((0, (KI_COL, HD)), (HD, (KI_COL, HD)), (2 * HD, (KI_COL + HD, HEADS))):
                    with nc.allow_non_contiguous_dma(reason="8 head-weight columns"):
                        pool.dma_start(wtail[:, :, d:d + n], w_in[:, :, c0:c0 + n]).then_inc(tail_in, 16)
                split_last(u)
                sum_x(3 * m + 1)
                pool.wait_ge(lo_ready, u + 4)
                step(u + 4, 0)
                with pool.Fori(1, 6) as i:
                    step(u + 4, i)
                for n in range(1, POOL_SUMS + 1):
                    j = n if n < TAPS else n + 1
                    dst = yc[:, 3, :] if n < TAPS else yc2[:]
                    pool.wait_ge(prod_ready, m * len(POOL_STEPS) + j + 1)
                    if n > 1:
                        pool.wait_ge(pconv_ready, m * POOL_SUMS + n - 1)
                    pool.tensor_tensor(dst, dst, prod[:, n % 3, :], ALU.add).then_inc(pconv_ready, 1)
                step(u + U_IN + 4, 0)
                step(u + U_IN + 4, 1)
                sum_x(3 * m + 2)
                if m < DEPTH - 1:
                    split_last(ffn_unit(2 * m + 2))
                    sum_x(3 * m + 3)

        @block.tensor
        def _(pe):
            def triple(out, slot, k, hi, lo, start, stop):
                pe.matmul(out, wlo[:, slot, k, :], hi, start=start, stop=False)
                pe.matmul(out, whi[:, slot, k, :], lo, start=False, stop=False)
                return pe.matmul(out, whi[:, slot, k, :], hi, start=False, stop=stop)

            def sum_squares(s):
                pe.wait_ge(accx_ready, 10 * s + 10)
                pe.matmul(bank(6), ones[:], accx[:], start=True, stop=True).then_inc(sx_done, 1)

            def sum_y(s):
                pe.wait_ge(acc_ready, 9 * s + 9)
                for j, t0 in enumerate(SPAN0):
                    pe.matmul(bank(5 + j, n=1), acc[:, t0:t0 + P], ones[:, 0:1], start=True, stop=False)
                pe.wait_ge(ysq_ready, 8 * s + 8)
                for j, t0 in enumerate(SPAN0):
                    last = pe.matmul(bank(5 + j, n=1), ysq[:, T + t0:T + t0 + P], ones[:, 0:1], start=False, stop=True)
                last.then_inc(ss_done, 1)
                pe.wait_ge(rcol_ready, s + 1)
                for j, (t0, n) in enumerate(TOK):
                    last = pe.matmul(bank(6, lo=8 + t0, n=n), rcol[:, j:j + 1].to_broadcast([P, P]),
                                     ident[:, t0 - SPAN0[j]:t0 - SPAN0[j] + n], start=True, stop=True)
                last.then_inc(rb_done, 1)
                for _ in range(KEEP_BUSY):
                    pe.matmul(bank(5, n=P), ones[:], ident[:], start=True, stop=True)

            def first_step(u0, hq, banks, order=range(KD), s=None, between=None):
                pe.wait_ge(lo_ready, u0 + 4)
                for n, k in enumerate(order[:MERGED]):
                    pe.wait_ge(hl_ready, 8 * hq + n + 1)
                    for rel in range(4):
                        triple(bank(banks[rel]), rel, k, hh[:, k, :], hl[:, k, :], n == 0, False)
                if between is not None:
                    between()
                for rel in range(4):
                    for n, k in enumerate(order[MERGED:], MERGED):
                        if rel == 0:
                            pe.wait_ge(hl_ready, 8 * hq + n + 1)
                        last = triple(bank(banks[rel]), rel, k, hh[:, k, :], hl[:, k, :], False, n == KD - 1)
                    last.then_inc(w_used, 1)
                    if rel == 1 and s is not None:
                        sum_squares(s)

            def up_step(f, i, second=False):
                u = ffn_unit(f)
                for rel in range(4):
                    pe.wait_ge(lo_ready, u + 4 * i + rel + 1)
                    if rel == 3 or not second:
                        pe.wait_ge(gr_ready if rel < 2 else up_ready, KF * f + 2 * i + rel % 2 - 1)
                    for k in range(KD):
                        last = triple(bank(rel), rel, k, hh[:, k, :], hl[:, k, :], k == 0, k == KD - 1)
                    last.then_inc(w_used, 1)

            def down_step(f, s, i, first):
                ud = ffn_unit(f) + U_UP
                for d in range(2):
                    for part in range(3):
                        for col in range(2):
                            j = 6 * d + 2 * part + col
                            pe.wait_ge(lo_ready, ud + 12 * i + j + 1)
                            if part == 0:
                                if first:
                                    pe.wait_ge(gr_ready if d == 0 else up_ready, KF * f + KF)
                                else:
                                    pe.wait_ge(y_saved, 8 * s + 4 * i + 2 * d + col - 3)
                            if first and d == 0 and col == 0:
                                pe.wait_ge(glo_ready, KF * f + 8 * part + PARTS[part])
                            for k in range(PARTS[part]):
                                kk = 8 * part + k
                                last = triple(bank(2 * d + col), j % 4, k, ghi[:, kk * T:(kk + 1) * T],
                                              glo[:, kk * T:(kk + 1) * T], kk == 0, kk == KF - 1)
                            last.then_inc(w_used, 1)

            def ffn(f, s, hq):
                first_step(ffn_unit(f), hq, (4, 5, 7, 3), s=s)
                up_step(f, 1, second=True)
                with pe.Fori(2, UP_STEPS) as i:
                    up_step(f, i)
                down_step(f, s, 0, True)
                down_step(f, s, 1, False)
                sum_y(s)

            def mixer(m, s, hq):
                u = mix_unit(m)
                first_step(u, hq, (0, 1, 2, 3), s=s)
                pe.wait_ge(tail_lo, m + 1)
                for b, c0, n in ((4, 0, P), (5, P, HEADS)):
                    for k in range(KD):
                        o = bank(b, slice(0, n))
                        pe.matmul(o, wtlo[:, k, c0:c0 + n], hh[:, k, :], start=(k == 0), stop=False)
                        pe.matmul(o, wthi[:, k, c0:c0 + n], hl[:, k, :], start=False, stop=False)
                        last = pe.matmul(o, wthi[:, k, c0:c0 + n], hh[:, k, :], start=False, stop=(k == KD - 1))
                    last.then_inc(tail_done, 1)
                def partner(k):
                    if k < 4:
                        pe.wait_ge(proj_saved, 24 * m + k + 1)
                        src = proj[:, (QI + k) * T:(QI + k + 1) * T]
                    else:
                        pe.wait_ge(tail_saved, 2 * m + 1)
                        src = kiT[:]
                    if k >= 2:
                        pe.wait_ge(rope_done, 13 * m + k - 1)
                    pe.matmul(bank(6 + k % 2), swap[:], src, start=True, stop=True).then_inc(rope_mm, 1)

                def in_unit(i, rel):
                    pe.wait_ge(lo_ready, u + 4 * i + rel + 1)
                    pe.wait_ge(proj_saved, 24 * m + 4 * i + rel - 3)
                    for k in range(KD):
                        last = triple(bank(rel), rel, k, hh[:, k, :], hl[:, k, :], k == 0, k == KD - 1)
                    last.then_inc(w_used, 1)

                pe.wait_ge(root_ready, 2 * s + 1)
                pe.wait_ge(const_in, 16 * 4)
                partner(0)
                partner(1)
                in_unit(1, 0)
                partner(2)
                partner(3)
                in_unit(1, 1)
                partner(4)
                in_unit(1, 2)
                in_unit(1, 3)
                pe.wait_ge(tail_saved, 2 * m + 2)
                pe.wait_ge(r_ready, s + 1)
                for tt, (t0, n) in enumerate(TOK):
                    pe.transpose(bank(4, slice(0, n), 8 * tt, 8), wiT[:, t0:t0 + n], ident[0:HEADS, 0:HEADS])
                    last = pe.matmul(bank(4, slice(0, n), 24 + tt, 1), rinv[0:1, t0:t0 + n], ones[0:1, 0:1],
                                     start=True, stop=True)
                last.then_inc(wi_T, 1)
                pe.wait_ge(kidx_in, 32 * (m + 1))
                for j in range(4):
                    last = pe.transpose(bank(5, n=P, lo=P * j), kidx[:, j, :], ident[:])
                last.then_inc(kidx_T, 1)
                pe.wait_ge(kc_in, 16 * (m + 1))
                pe.wait_ge(proj_saved, 24 * m + 8)
                for hp in range(4):
                    for j in range(4):
                        last = pe.transpose(bank(hp, lo=j * P, n=P), kc[:, j, hp * P:(hp + 1) * P], ident[:])
                    last.then_inc(kcT_done, 1)
                pe.wait_ge(rope_done, 13 * m + 5)

                def sample_logits():
                    pe.wait_ge(kiTs_ready, 2 * m + 2)
                    pe.wait_ge(kTs_ready, 8 * m + 4)
                    for g in range(2):
                        for j in range(4):
                            h = 4 * g + j
                            r = slice((h % 2) * HD, (h % 2 + 1) * HD)
                            o = slice(32 * j, 32 * j + 32)
                            q = proj[r, (QI + h // 2) * T + SEQ:(QI + h // 2 + 1) * T]
                            pe.matmul(bank(2 * g, o, n=PAST), q, kiTs[r, 0:PAST], start=True, stop=True)
                            last = pe.matmul(bank(2 * g + 1, o, n=DEC), q, kiTs[r, PAST:SKEYS], start=True, stop=True)
                        last.then_inc(lgS_done, 1)

                def sample_scores():
                    pe.wait_ge(wrow_ready, m + 1)
                    pe.wait_ge(relS_ready, 2 * m + 2)
                    for b, a0, n in ((4, 0, PAST), (5, PAST, DEC)):
                        for g in range(2):
                            last = pe.matmul(bank(b, slice(0, DEC), n=n), wdiag[:, g, :], relS[:, g, a0:a0 + n],
                                             start=(g == 0), stop=(g == 1))
                    last.then_inc(scoreS_done, 1)

                for h in range(HEADS):
                    r = slice((h % 2) * HD, (h % 2 + 1) * HD)
                    q0 = (QI + h // 2) * T
                    if h >= 2:
                        pe.wait_ge(rel_ready, 8 * m + h - 1)
                    b = 6 + h % 2
                    pe.matmul(bank(b, n=P), proj[r, q0:q0 + P], kiT[r, 0:P], start=True, stop=True)
                    pe.matmul(bank(b, lo=P, n=SEQ), proj[r, q0 + P:q0 + SEQ], kiT[r, 0:SEQ], start=True,
                              stop=True).then_inc(lg_done, 1)
                    if h == 3:
                        sample_logits()
                    if h == 6:
                        sample_scores()

                def in_step(i):
                    for rel in range(4):
                        in_unit(i, rel)

                def partners(k0):
                    for k in range(k0, k0 + 4):
                        pe.matmul(bank(4 + k - k0), swap[:], proj[:, (Q + k - 5) * T:(Q + k - 4) * T], start=True,
                                  stop=True).then_inc(rope_mm, 1)

                with pe.Fori(2, 4) as i:
                    in_step(i)
                pe.wait_ge(state_in, 16 * (m + 1))
                pe.wait_ge(scoreS_saved, m + 1)
                for ct in range(CT):
                    last = pe.transpose(bank(5, lo=HIST * ct, n=HIST), statein[:, ct * P:(ct + 1) * P],
                                        ident[0:HIST, 0:HIST])
                last.then_inc(st_T, 1)
                in_step(4)
                pe.wait_ge(proj_saved, 24 * m + 16)
                pe.wait_ge(st_ready, m + 1)
                pe.wait_ge(rel_ready, 8 * m + 8)
                partners(5)
                in_step(5)
                pe.wait_ge(proj_saved, 24 * m + 20)
                pe.wait_ge(rope_done, 13 * m + 9)
                partners(9)
                pe.wait_ge(proj_saved, 24 * m + 24)
                for tt, (t0, n) in enumerate(TOK):
                    for c in range(4):
                        o = (V + c) * T + t0
                        last = pe.transpose(bank(tt, slice(0, n), c * P, P), proj[:, o:o + n], ident[:])
                    last.then_inc(vrow_T, 1)

                def conv_mean():
                    pe.wait_ge(yc_ready, m + 1)
                    for ct in range(CT):
                        last = pe.matmul(bank(1, n=CO), ones[:], yc[:, ct, :], start=(ct == 0), stop=(ct == CT - 1))
                    last.then_inc(mu_done, 1)

                def conv_var():
                    for ct in range(CT):
                        pe.wait_ge(csq_ready, 4 * m + ct + 1)
                        pe.matmul(bank(3, n=CO), ones[:], y[:, (ct % 2) * CO:(ct % 2 + 1) * CO], start=(ct == 0),
                                  stop=(ct == CT - 1)).then_inc(csq_used, 1)

                def logits(n):
                    if n >= 2:
                        pe.wait_ge(max_ready, 10 * m + n - 1)
                    b = 2 * (n % 2)
                    if n < 2:
                        for j in range(4):
                            h = 4 * n + j
                            r = slice((h % 2) * HD, (h % 2 + 1) * HD)
                            o = slice(32 * j, 32 * j + 32)
                            q = proj[r, (Q + h // 2) * T + SEQ:(Q + h // 2 + 1) * T]
                            pe.matmul(bank(b, o, n=PAST), q, kTs[r, h // 2, 0:PAST], start=True, stop=True)
                            last = pe.matmul(bank(b + 1, o, n=DEC), q, kTs[r, h // 2, PAST:SKEYS], start=True, stop=True)
                    else:
                        h = n - 2
                        r = slice((h % 2) * HD, (h % 2 + 1) * HD)
                        q0, k0 = (Q + h // 2) * T, (K + h // 2) * T
                        pe.matmul(bank(b, n=P), proj[r, q0:q0 + P], proj[r, k0:k0 + P], start=True, stop=True)
                        last = pe.matmul(bank(b, lo=P, n=SEQ), proj[r, q0 + P:q0 + SEQ], proj[r, k0:k0 + SEQ],
                                         start=True, stop=True)
                    last.then_inc(s_done, 1)

                def turn(n):
                    pe.wait_ge(p_ready, 10 * m + n + 1)
                    if n >= 1:
                        pe.wait_ge(pT_ready, 10 * m + n)
                    if n < 2:
                        for j in range(4):
                            pe.transpose(bank(4, lo=j * P, n=P), prob[:, n % 2, j * P:(j + 1) * P], ident[:])
                        last = pe.transpose(bank(5, slice(0, DEC), n=P), prob[:, n % 2, PAST:SKEYS], ident[:])
                    else:
                        for j in range(3):
                            last = pe.transpose(bank(4 + n % 2, lo=j * P, n=P), prob[:, n % 2, j * P:(j + 1) * P], ident[:])
                    last.then_inc(pT_done, 1)

                def values(n):
                    pe.wait_ge(pT_ready, 10 * m + n + 1)
                    if n < 2:
                        pe.wait_ge(vc_in, 16 * (m + 1))
                        pe.wait_ge(vrow_ready, 3 * m + 3)
                        for j4 in range(4):
                            h = 4 * n + j4
                            r = slice((h % 2) * HD, (h % 2 + 1) * HD)
                            o = bank(7, r, 32 * (h // 2), DEC)
                            hc = slice(h * HD, (h + 1) * HD)
                            for j in range(4):
                                pe.matmul(o, vc[:, j, hc], probT[:, n % 2, j * P + 32 * j4:j * P + 32 * j4 + 32],
                                          start=(j == 0), stop=False)
                            last = pe.matmul(o, vrow[0:DEC, 2, hc], probT[0:DEC, n % 2, 512 + 32 * j4:544 + 32 * j4],
                                             start=False, stop=True)
                    else:
                        h = n - 2
                        hp = h // 2
                        if h % 2 == 0:
                            pe.wait_ge(att_saved, m + 1)
                            if hp >= 2:
                                pe.wait_ge(hh_ready, 8 * (4 * m + 2) + hp - 1)
                        r = slice((h % 2) * HD, (h % 2 + 1) * HD)
                        hc = slice(h * HD, (h + 1) * HD)
                        b = 6 + hp % 2
                        pe.matmul(bank(b, r, n=P), vrow[:, 0, hc], probT[:, n % 2, 0:P], start=True, stop=True)
                        pe.matmul(bank(b, r, P, P), vrow[:, 0, hc], probT[:, n % 2, P:2 * P], start=True, stop=False)
                        last = pe.matmul(bank(b, r, P, P), vrow[:, 1, hc], probT[:, n % 2, 2 * P:3 * P],
                                         start=False, stop=True)
                    last.then_inc(pv_done, 1)

                pe.wait_ge(rope_done, 13 * m + 13)
                pe.wait_ge(kTs_ready, 8 * m + 8)
                logits(0)
                logits(1)
                for n in range(10):
                    turn(n)
                    if n < 8:
                        logits(n + 2)
                    if n >= 1:
                        values(n - 1)
                    if n == 6:
                        conv_mean()
                    if n == 8:
                        conv_var()
                values(9)
                pe.wait_ge(croot_ready, m + 1)
                for g, c0 in enumerate((SEQ, EXT - HIST)):
                    for ct in range(CT):
                        last = pe.transpose(bank(2 * g + 1, slice(0, HIST), ct * P, P), ext[:, ct, c0:c0 + HIST], ident[:])
                    last.then_inc(crow_T, 1)

                def key_rows(tt, b):
                    t0, n = TOK[tt]
                    for c in range(4):
                        o = (K + c) * T + t0
                        last = pe.transpose(bank(b, slice(0, n), c * P, P), proj[:, o:o + n], ident[:])
                    last.then_inc(krow_T, 1)

                def last_rows():
                    pe.wait_ge(crow_ready, 2 * m + 2)
                    key_rows(2, 1)
                    for tt, (t0, n) in enumerate(TOK):
                        last = pe.transpose(bank(3, slice(0, n), HD * tt, HD), kiT[0:HD, t0:t0 + n], ident[0:HD, 0:HD])
                    last.then_inc(krow_T, 1)

                key_rows(0, 0)
                key_rows(1, 2)
                uo = u + U_IN
                pe.wait_ge(hh_ready, 8 * (4 * m + 2) + 4)
                first_step(uo, 4 * m + 2, (4, 5, 6, 7), (4, 5, 6, 7, 0, 1, 2, 3), between=last_rows)
                pe.wait_ge(krow_ready, 4 * m + 4)
                for rel in range(4):
                    pe.wait_ge(lo_ready, uo + 4 + rel + 1)
                    for k in range(KD):
                        last = triple(bank(rel), rel, k, hh[:, k, :], hl[:, k, :], k == 0, k == KD - 1)
                    last.then_inc(w_used, 1)
                sum_y(s)

            pe.wait_ge(ident_in, 16)
            pe.wait_ge(x_in, 32)
            for c in range(KD):
                if c >= 4:
                    pe.wait_ge(x_ready, c - 3)
                for tt, (t0, n) in enumerate(TOK):
                    last = pe.transpose(bank(c % 4, lo=t0, n=n), xrow[0:n, tt, c * P:(c + 1) * P], ident[0:n, 0:n])
                last.then_inc(x_T, 1)
            pe.wait_ge(par_in, 16 * 9)
            pe.transpose(bank(6, n=120), prow[:], ident[0:120, 0:120]).then_inc(par_T, 1)
            pe.wait_ge(taps_in, 16)
            pe.wait_ge(x_ready, 6)
            for j in range(DEPTH * CT):
                last = pe.transpose(bank(1, lo=TAPS * j, n=TAPS), trow[:, j * P:(j + 1) * P], ident[0:TAPS, 0:TAPS])
            last.then_inc(taps_T, 1)
            pe.wait_ge(ms_ready, 1)
            pe.wait_ge(par_ready, 1)
            pe.wait_ge(x_ready, KD)
            for l in range(DEPTH):
                ffn(2 * l, 3 * l, 4 * l)
                mixer(l, 3 * l + 1, 4 * l + 1)
                ffn(2 * l + 1, 3 * l + 2, 4 * l + 3)
            for n in range(6):
                half, tt = divmod(n, 3)
                pe.wait_ge(x_ready, 8 * 6 + 4 * (half + 1))
                t0, k = TOK[tt]
                for c in range(4):
                    last = pe.transpose(bank(n, slice(0, k), c * P, P), x[:, 4 * half + c, t0:t0 + k], ident[:])
                last.then_inc(yT_done, 1)


_INS = ["x_prompt", "x_sample", "cache_k", "cache_v", "cache_kidx", "state_conv", "ffn1_norm_pre",
        "ffn1_norm_post", "ffn1_w_up", "ffn1_w_down", "mix_norm_pre", "mix_norm_post", "w_in", "conv_w", "conv_b",
        "conv_ln_g", "conv_ln_b", "w_out", "ffn2_norm_pre", "ffn2_norm_post", "ffn2_w_up", "ffn2_w_down"]
_OUTS = [(1, SEQ, D), (1, DEC, D), (DEPTH, 1, SEQ, HEADS, HD), (DEPTH, 1, SEQ, HEADS, HD), (DEPTH, 1, SEQ, HD),
         (DEPTH, 1, HIST, CC), (DEPTH, 1, DEC, HEADS, HD), (DEPTH, 1, DEC, HEADS, HD), (DEPTH, 1, DEC, HD),
         (DEPTH, 1, HIST, CC)]


def shape_constants():
    f = np.float32
    pos = np.concatenate([np.arange(SEQ), PAST + np.arange(DEC)]).astype(f)
    inv = (f(1.0) / (f(THETA) ** (np.arange(0, HD, 2).astype(f) / f(HD)))).astype(f)
    angle = (pos[:, None] * inv[None, :]).astype(f)
    half = np.arange(P) % (HD // 2)
    swap = np.zeros((P, P), f)
    for j in range(P):
        if j % HD < HD // 2:
            swap[j + HD // 2, j] = -1.0
        else:
            swap[j - HD // 2, j] = 1.0
    return {"ident": np.eye(P, dtype=f), "swap": swap, "stack": np.tile(np.eye(DEC, dtype=f), (4, 1)),
            "cosT": np.ascontiguousarray(np.cos(angle).astype(f)[:, half].T),
            "sinT": np.ascontiguousarray(np.sin(angle).astype(f)[:, half].T)}


def kernel(**inputs):
    import concourse.bacc as _bacc
    from concourse.bass_utils import run_bass_kernel_spmd as _run

    nc = _bacc.Bacc("TRN2", target_bir_lowering=False, num_devices=1)
    arrays, ins, consts = {}, {}, {}
    for name in _INS:
        a = np.ascontiguousarray(inputs[name])
        arrays[f"in_{name}"] = a
        ins[name] = nc.dram_tensor(f"in_{name}", a.shape, mybir.dt.from_np(a.dtype), kind="ExternalInput").ap()
    for name, a in shape_constants().items():
        arrays[f"const_{name}"] = a
        consts[name] = nc.dram_tensor(f"const_{name}", a.shape, F32, kind="ExternalInput").ap()
    outs = [nc.dram_tensor(f"out_{i}", shape, F32, kind="ExternalOutput").ap() for i, shape in enumerate(_OUTS)]
    build(nc, ins, consts, outs)
    r = _run(nc, [arrays], core_ids=[0])
    return tuple(r.results[0][f"out_{i}"] for i in range(len(_OUTS)))
```
